# Optimizing a Trainium2 kernel written in Bass

```python
import math
import jax
import jax.numpy as jnp
from jax import lax
import numpy as np

D_MODEL = 1024
BATCH = 1
SEQ = 512
DEPTH = 2

GRID_W = 64
CTX_LEN = 256
N_EVEN = (DEPTH + 1) // 2
N_ODD = DEPTH // 2
EPS = 1e-6
ROPE_THETA = 10000.0
CONV_K = 5
Q_BLOCK = 128
DN_HEADS = 8
DN_DK = 128
DN_DV = 128
DN_CHUNK = 64
SSD_HEADS = 16
SSD_HEAD_DIM = 64
SSD_GROUPS = 2
SSD_STATE = 128
SSD_CHUNK = 128
SSD_INNER = SSD_HEADS * SSD_HEAD_DIM
DA_HEADS = 8
DA_DIM = 64
MLA_HEADS = 8
MLA_Q_RANK = 512
MLA_KV_RANK = 256
MLA_NOPE = 128
MLA_ROPE = 64
MLA_V = 128
FFN_HIDDEN = ((8 * D_MODEL + 3 * 256 - 1) // (3 * 256)) * 256

DN_QK = DN_HEADS * DN_DK
DN_VW = DN_HEADS * DN_DV
SSD_BC = SSD_GROUPS * SSD_STATE
EV_CONV = 2 * DN_QK + DN_VW + SSD_INNER + 2 * SSD_BC
EV_GATE = DN_VW + SSD_INNER
EV_SMALL = 4 * DN_HEADS + 2 * SSD_HEADS
EV_IN = EV_CONV + EV_GATE + EV_SMALL
EV_CONV_SPLITS = [DN_QK, 2 * DN_QK, 2 * DN_QK + DN_VW, 2 * DN_QK + DN_VW + SSD_INNER, 2 * DN_QK + DN_VW + SSD_INNER + SSD_BC]
EV_MIX = DN_VW + SSD_INNER
DA_QK = DA_HEADS * 2 * DA_DIM
DA_VW = DA_HEADS * 2 * DA_DIM
OD_IN = 2 * DA_QK + DA_VW + MLA_Q_RANK + MLA_KV_RANK + MLA_ROPE
OD_SPLITS = [DA_QK, 2 * DA_QK, 2 * DA_QK + DA_VW, 2 * DA_QK + DA_VW + MLA_Q_RANK, 2 * DA_QK + DA_VW + MLA_Q_RANK + MLA_KV_RANK]
OD_MIX = DA_VW + MLA_HEADS * MLA_V

kernel_name = "hybrid_dit_deltanet_ssd_diffattn_mla"

def rms_norm(x, g):
    xf = x.astype(jnp.float32)
    y = xf * lax.rsqrt(jnp.mean(xf * xf, axis=-1, keepdims=True) + EPS)
    return (y * g.astype(jnp.float32)).astype(x.dtype)

def l2_norm(x):
    xf = x.astype(jnp.float32)
    return xf * lax.rsqrt(jnp.sum(xf * xf, axis=-1, keepdims=True) + EPS)

def swiglu(h, w_in, w_out):
    gate, up = jnp.split(h @ w_in, 2, axis=-1)
    return (jax.nn.silu(gate) * up) @ w_out

def centred_depthwise_conv_silu(u, w, b):
    y = lax.conv_general_dilated(u, w[:, None, :].astype(u.dtype), window_strides=(1,), padding=[(CONV_K // 2, CONV_K // 2)], dimension_numbers=("NWC", "WIO", "NWC"), feature_group_count=u.shape[-1])
    return jax.nn.silu(y + b.astype(u.dtype))

def axial_rope_tables(n_tokens, rot_dim):
    rows = n_tokens // GRID_W
    row = jnp.broadcast_to(jnp.arange(rows, dtype=jnp.float32)[:, None], (rows, GRID_W)).reshape(-1)
    col = jnp.broadcast_to(jnp.arange(GRID_W, dtype=jnp.float32)[None, :], (rows, GRID_W)).reshape(-1)
    n_freq = rot_dim // 4
    inv_freq = ROPE_THETA ** (-jnp.arange(n_freq, dtype=jnp.float32) / n_freq)
    ang = jnp.concatenate([row[:, None] * inv_freq, col[:, None] * inv_freq], axis=-1)
    return jnp.cos(ang), jnp.sin(ang)

def apply_axial_rope(x, cos, sin):
    r4 = x.shape[-1] // 4
    xr1, xr2, xc1, xc2 = jnp.split(x.astype(jnp.float32), 4, axis=-1)
    x1 = jnp.concatenate([xr1, xc1], axis=-1)
    x2 = jnp.concatenate([xr2, xc2], axis=-1)
    shp = (cos.shape[0],) + (1,) * (x.ndim - 3) + (cos.shape[-1],)
    c = cos.reshape(shp)
    s = sin.reshape(shp)
    y1 = x1 * c - x2 * s
    y2 = x2 * c + x1 * s
    return jnp.concatenate([y1[..., :r4], y2[..., :r4], y1[..., r4:], y2[..., r4:]], axis=-1).astype(x.dtype)

def seq_to_chunks(a, size):
    b, n = a.shape[:2]
    return jnp.moveaxis(a.reshape(b, n // size, size, *a.shape[2:]), 1, 0)

def chunks_to_seq(a):
    nc, b, size = a.shape[:3]
    return jnp.moveaxis(a, 0, 1).reshape(b, nc * size, *a.shape[3:])

def heads_first_chunks(a, size):
    b, n, h = a.shape[:3]
    a = a.reshape(b, n // size, size, h, *a.shape[3:])
    return jnp.moveaxis(jnp.swapaxes(a, 2, 3), 1, 0)

def gated_delta_scan(q, k, v, g, beta, state0):
    f32 = jnp.float32
    bsz, seqlen, heads, _ = q.shape
    c = DN_CHUNK
    causal = jnp.tril(jnp.ones((c, c), dtype=bool))
    strict = jnp.tril(jnp.ones((c, c), dtype=bool), -1)
    eye = jnp.eye(c, dtype=f32)

    def body(s, xs):
        qc, kc, vc, gch, bc = xs
        gc = jnp.cumsum(gch, axis=-1)
        decay = jnp.exp(jnp.where(causal, gc[..., :, None] - gc[..., None, :], -jnp.inf))
        kb = kc * bc[..., None]
        a = jnp.where(strict, jnp.einsum("bhid,bhjd->bhij", kb, kc) * decay, 0.0)
        t = lax.linalg.triangular_solve(a + eye, jnp.broadcast_to(eye, a.shape), left_side=True, lower=True, unit_diagonal=True)
        u = t @ (vc * bc[..., None])
        w = t @ (kb * jnp.exp(gc)[..., None])
        v_new = u - w @ s
        attn = jnp.einsum("bhid,bhjd->bhij", qc, kc) * decay
        o = (qc * jnp.exp(gc)[..., None]) @ s + attn @ v_new
        s = s * jnp.exp(gc[..., -1])[..., None, None] + jnp.einsum("bhcd,bhce->bhde", kc * jnp.exp(gc[..., -1:] - gc)[..., None], v_new)
        return s, o

    xs = tuple(heads_first_chunks(t.astype(f32), c) for t in (q * DN_DK ** -0.5, k, v, g, beta))
    s, o = lax.scan(body, state0.astype(f32), xs)
    o = jnp.swapaxes(jnp.moveaxis(o, 0, 1), 2, 3).reshape(bsz, seqlen, heads, -1)
    return o, s

def ssd_scan(x, dt, a, bm, cm, state0):
    f32 = jnp.float32
    c = SSD_CHUNK
    causal = jnp.tril(jnp.ones((c, c), dtype=bool))[None, :, :, None, None]

    def body(h, xs):
        xc, dtc, ac, bc, cc = xs
        cum = jnp.cumsum(ac, axis=1)
        seg = jnp.exp(jnp.where(causal, cum[:, :, None] - cum[:, None, :], -jnp.inf))
        xdt = xc * dtc[..., None]
        mix = jnp.einsum("blgn,bsgn->blsg", cc, bc)[..., None] * seg
        y = jnp.einsum("blsgr,bsgrp->blgrp", mix, xdt) + jnp.einsum("blgn,bgrnp->blgrp", cc, h) * jnp.exp(cum)[..., None]
        h = h * jnp.exp(cum[:, -1])[..., None, None] + jnp.einsum("blgn,blgrp->bgrnp", bc, xdt * jnp.exp(cum[:, -1:] - cum)[..., None])
        return h, y

    xs = tuple(seq_to_chunks(t.astype(f32), c) for t in (x, dt, a, bm, cm))
    h, y = lax.scan(body, state0.astype(f32), xs)
    return chunks_to_seq(y), h

def bidirectional_prefix_scan(scan_fn, ctx_fwd, ctx_bwd, lat_fwd, lat_bwd, state0):
    rev = lambda args: tuple(jnp.flip(t, axis=1) for t in args)
    y_cf, s_f = scan_fn(*ctx_fwd, state0)
    y_cb, s_b = scan_fn(*rev(ctx_bwd), state0)
    y_lf, _ = scan_fn(*lat_fwd, s_f)
    y_lb, _ = scan_fn(*rev(lat_bwd), s_b)
    return y_cf + jnp.flip(y_cb, axis=1), y_lf + jnp.flip(y_lb, axis=1)

def sweep_query_blocks(fn, q):
    bsz, n = q.shape[:2]
    qb = jnp.moveaxis(q.reshape(bsz, n // Q_BLOCK, Q_BLOCK, *q.shape[2:]), 1, 0)
    out = lax.map(fn, qb)
    return jnp.moveaxis(out, 0, 1).reshape(bsz, n, *out.shape[3:])

def diff_attention(q, k, v, lam):
    kf = k.astype(jnp.float32)
    vf = v.astype(jnp.float32)
    scale = DA_DIM ** -0.5

    def block(qb):
        s = jnp.einsum("bqhcd,bkhcd->bchqk", qb.astype(jnp.float32) * scale, kf)
        p = jax.nn.softmax(s, axis=-1)
        return jnp.einsum("bhqk,bkhd->bqhd", p[:, 0] - lam * p[:, 1], vf)

    return sweep_query_blocks(block, q)

def softmax_attention(q, k, v):
    kf = k.astype(jnp.float32)
    vf = v.astype(jnp.float32)
    scale = q.shape[-1] ** -0.5

    def block(qb):
        s = jnp.einsum("bqhd,bkhd->bhqk", qb.astype(jnp.float32) * scale, kf)
        return jnp.einsum("bhqk,bkhd->bqhd", jax.nn.softmax(s, axis=-1), vf)

    return sweep_query_blocks(block, q)

def even_mixer(h_lat, h_ctx, w_in, conv_w, conv_b, dn_a_log, dn_dt_bias, dn_norm, ssd_a_log, ssd_dt_bias, ssd_d, ssd_norm, w_out, with_ctx_out):
    f32 = jnp.float32
    grp = SSD_HEADS // SSD_GROUPS

    def prepare(h):
        bsz, n = h.shape[:2]
        p = h @ w_in
        u = centred_depthwise_conv_silu(p[..., :EV_CONV], conv_w, conv_b)
        z = p[..., EV_CONV:EV_CONV + EV_GATE]
        small = p[..., EV_CONV + EV_GATE:].astype(f32)
        q, k, v, xs, bm, cm = jnp.split(u, EV_CONV_SPLITS, axis=-1)
        q = l2_norm(q.reshape(bsz, n, DN_HEADS, DN_DK))
        k = l2_norm(k.reshape(bsz, n, DN_HEADS, DN_DK))
        v = v.reshape(bsz, n, DN_HEADS, DN_DV)
        b_raw, a_raw, dt_raw = jnp.split(small, [2 * DN_HEADS, 4 * DN_HEADS], axis=-1)
        beta = jax.nn.sigmoid(b_raw).reshape(bsz, n, 2, DN_HEADS)
        g = -jnp.exp(dn_a_log.astype(f32)) * jax.nn.softplus(a_raw.reshape(bsz, n, 2, DN_HEADS) + dn_dt_bias.astype(f32))
        dt = jax.nn.softplus(dt_raw.reshape(bsz, n, 2, SSD_HEADS) + ssd_dt_bias.astype(f32))
        a = dt * -jnp.exp(ssd_a_log.astype(f32))
        dt = dt.reshape(bsz, n, 2, SSD_GROUPS, grp)
        a = a.reshape(bsz, n, 2, SSD_GROUPS, grp)
        x_ssd = xs.reshape(bsz, n, SSD_GROUPS, grp, SSD_HEAD_DIM)
        bm = bm.reshape(bsz, n, SSD_GROUPS, SSD_STATE)
        cm = cm.reshape(bsz, n, SSD_GROUPS, SSD_STATE)
        dn_dirs = [(q, k, v, g[:, :, d], beta[:, :, d]) for d in range(2)]
        ssd_dirs = [(x_ssd, dt[:, :, d], a[:, :, d], bm, cm) for d in range(2)]
        return dn_dirs, ssd_dirs, x_ssd, z

    def merge(o_dn, y_ssd, x_ssd, z):
        bsz, n = z.shape[:2]
        z_dn, z_ssd = jnp.split(z.astype(f32), [DN_VW], axis=-1)
        o_dn = rms_norm(o_dn, dn_norm).reshape(bsz, n, DN_VW) * jax.nn.silu(z_dn)
        y = (y_ssd + ssd_d.astype(f32).reshape(SSD_GROUPS, grp, 1) * x_ssd).reshape(bsz, n, SSD_INNER) * jax.nn.silu(z_ssd)
        y = rms_norm(y.reshape(bsz, n, SSD_GROUPS, SSD_INNER // SSD_GROUPS), ssd_norm.reshape(SSD_GROUPS, -1)).reshape(bsz, n, SSD_INNER)
        return jnp.concatenate([o_dn, y], axis=-1).astype(z.dtype) @ w_out

    dn_c, ssd_c, x_c, z_c = prepare(h_ctx)
    dn_l, ssd_l, x_l, z_l = prepare(h_lat)
    bsz = h_lat.shape[0]
    dn_s0 = jnp.zeros((bsz, DN_HEADS, DN_DK, DN_DV), f32)
    ssd_s0 = jnp.zeros((bsz, SSD_GROUPS, grp, SSD_STATE, SSD_HEAD_DIM), f32)
    o_dn_c, o_dn_l = bidirectional_prefix_scan(gated_delta_scan, dn_c[0], dn_c[1], dn_l[0], dn_l[1], dn_s0)
    y_ssd_c, y_ssd_l = bidirectional_prefix_scan(ssd_scan, ssd_c[0], ssd_c[1], ssd_l[0], ssd_l[1], ssd_s0)
    out_lat = merge(o_dn_l, y_ssd_l, x_l, z_l)
    out_ctx = merge(o_dn_c, y_ssd_c, x_c, z_c) if with_ctx_out else None
    return out_lat, out_ctx

def odd_mixer(h_lat, h_ctx, w_in, da_q_norm, da_k_norm, da_lambda, da_sub_norm, lambda_init, mla_q_a_norm, mla_w_uq, mla_kv_a_norm, mla_w_ukv, mla_q_norm, mla_k_norm, w_out, with_ctx_out):

    def prepare(h, rope, with_queries):
        bsz, n = h.shape[:2]
        dq, dk, dv, cq, ckv, kr = jnp.split(h @ w_in, OD_SPLITS, axis=-1)
        dk = rms_norm(dk.reshape(bsz, n, DA_HEADS, 2, DA_DIM), da_k_norm)
        dv = dv.reshape(bsz, n, DA_HEADS, 2 * DA_DIM)
        kv = (rms_norm(ckv, mla_kv_a_norm) @ mla_w_ukv).reshape(bsz, n, MLA_HEADS, MLA_NOPE + MLA_V)
        k_nope, v = jnp.split(kv, [MLA_NOPE], axis=-1)
        k_nope = rms_norm(k_nope, mla_k_norm[:MLA_NOPE])
        kr = rms_norm(kr, mla_k_norm[MLA_NOPE:])
        if rope is not None:
            dk = apply_axial_rope(dk, *rope[0])
            kr = apply_axial_rope(kr, *rope[1])
        k = jnp.concatenate([k_nope, jnp.broadcast_to(kr[:, :, None, :], (bsz, n, MLA_HEADS, MLA_ROPE))], axis=-1)
        keys = (dk, dv, k, v)
        if not with_queries:
            return None, keys
        dq = rms_norm(dq.reshape(bsz, n, DA_HEADS, 2, DA_DIM), da_q_norm)
        q = (rms_norm(cq, mla_q_a_norm) @ mla_w_uq).reshape(bsz, n, MLA_HEADS, MLA_NOPE + MLA_ROPE)
        q_nope = rms_norm(q[..., :MLA_NOPE], mla_q_norm[:MLA_NOPE])
        q_rope = rms_norm(q[..., MLA_NOPE:], mla_q_norm[MLA_NOPE:])
        if rope is not None:
            dq = apply_axial_rope(dq, *rope[0])
            q_rope = apply_axial_rope(q_rope, *rope[1])
        return (dq, jnp.concatenate([q_nope, q_rope], axis=-1)), keys

    lam_p = da_lambda.astype(jnp.float32)
    lam = jnp.exp(jnp.sum(lam_p[0] * lam_p[1])) - jnp.exp(jnp.sum(lam_p[2] * lam_p[3])) + lambda_init

    def attend(queries, keys):
        dq, q = queries
        dk, dv, k, v = keys
        bsz, n = q.shape[:2]
        da = rms_norm(diff_attention(dq, dk, dv, lam), da_sub_norm) * (1.0 - lambda_init)
        ml = softmax_attention(q, k, v)
        merged = jnp.concatenate([da.reshape(bsz, n, DA_VW), ml.reshape(bsz, n, MLA_HEADS * MLA_V)], axis=-1)
        return merged.astype(h_lat.dtype) @ w_out

    n_lat = h_lat.shape[1]
    rope = (axial_rope_tables(n_lat, DA_DIM), axial_rope_tables(n_lat, MLA_ROPE))
    q_lat, keys_lat = prepare(h_lat, rope, True)
    q_ctx, keys_ctx = prepare(h_ctx, None, with_ctx_out)
    keys_all = tuple(jnp.concatenate([kl, kc], axis=1) for kl, kc in zip(keys_lat, keys_ctx))
    out_lat = attend(q_lat, keys_all)
    out_ctx = attend(q_ctx, keys_ctx) if with_ctx_out else None
    return out_lat, out_ctx

def setup_inputs(seed: int = 0) -> dict:
    key = jax.random.key(seed)
    ks = iter(jax.random.split(key, 40))
    f32 = jnp.float32

    def nrm(shape, scale):
        return scale * jax.random.normal(next(ks), shape, f32)

    def gain(shape):
        return 1.0 + 0.02 * jax.random.normal(next(ks), shape, f32)

    def a_log(shape):
        return jnp.log(jax.random.uniform(next(ks), shape, f32, 1.0, 16.0))

    def dt_bias(shape):
        u = jax.random.uniform(next(ks), shape, f32)
        dt = jnp.exp(u * (math.log(0.1) - math.log(1e-3)) + math.log(1e-3))
        return dt + jnp.log(-jnp.expm1(-dt))

    d = D_MODEL
    return {
        "x": nrm((BATCH, SEQ, d), 1.0),
        "c": nrm((BATCH, d), 1.0),
        "ctx": nrm((BATCH, CTX_LEN, d), 1.0),
        "c_ctx": nrm((d,), 1.0),
        "ada_w": nrm((DEPTH, d, 6 * d), d ** -0.5),
        "ada_b": nrm((DEPTH, 6 * d), 0.02),
        "norm_mix": gain((DEPTH, d)),
        "norm_ffn": gain((DEPTH, d)),
        "ffn_w_in": nrm((DEPTH, d, 2 * FFN_HIDDEN), d ** -0.5),
        "ffn_w_out": nrm((DEPTH, FFN_HIDDEN, d), FFN_HIDDEN ** -0.5),
        "ev_w_in": nrm((N_EVEN, d, EV_IN), d ** -0.5),
        "ev_conv_w": nrm((N_EVEN, CONV_K, EV_CONV), CONV_K ** -0.5),
        "ev_conv_b": nrm((N_EVEN, EV_CONV), 0.02),
        "dn_a_log": a_log((N_EVEN, 2, DN_HEADS)),
        "dn_dt_bias": dt_bias((N_EVEN, 2, DN_HEADS)),
        "dn_norm": gain((N_EVEN, DN_DV)),
        "ssd_a_log": a_log((N_EVEN, 2, SSD_HEADS)),
        "ssd_dt_bias": dt_bias((N_EVEN, 2, SSD_HEADS)),
        "ssd_d": gain((N_EVEN, SSD_HEADS)),
        "ssd_norm": gain((N_EVEN, SSD_INNER)),
        "ev_w_out": nrm((N_EVEN, EV_MIX, d), EV_MIX ** -0.5),
        "od_w_in": nrm((N_ODD, d, OD_IN), d ** -0.5),
        "da_q_norm": gain((N_ODD, DA_DIM)),
        "da_k_norm": gain((N_ODD, DA_DIM)),
        "da_lambda": nrm((N_ODD, 4, DA_DIM), 0.1),
        "da_sub_norm": gain((N_ODD, 2 * DA_DIM)),
        "mla_q_a_norm": gain((N_ODD, MLA_Q_RANK)),
        "mla_w_uq": nrm((N_ODD, MLA_Q_RANK, MLA_HEADS * (MLA_NOPE + MLA_ROPE)), MLA_Q_RANK ** -0.5),
        "mla_kv_a_norm": gain((N_ODD, MLA_KV_RANK)),
        "mla_w_ukv": nrm((N_ODD, MLA_KV_RANK, MLA_HEADS * (MLA_NOPE + MLA_V)), MLA_KV_RANK ** -0.5),
        "mla_q_norm": gain((N_ODD, MLA_NOPE + MLA_ROPE)),
        "mla_k_norm": gain((N_ODD, MLA_NOPE + MLA_ROPE)),
        "od_w_out": nrm((N_ODD, OD_MIX, d), OD_MIX ** -0.5),
    }

def reference(x, c, ctx, c_ctx, ada_w, ada_b, norm_mix, norm_ffn, ffn_w_in, ffn_w_out,
              ev_w_in, ev_conv_w, ev_conv_b, dn_a_log, dn_dt_bias, dn_norm, ssd_a_log, ssd_dt_bias, ssd_d, ssd_norm, ev_w_out,
              od_w_in, da_q_norm, da_k_norm, da_lambda, da_sub_norm, mla_q_a_norm, mla_w_uq, mla_kv_a_norm, mla_w_ukv,
              mla_q_norm, mla_k_norm, od_w_out):
    for i in range(DEPTH):
        last = i == DEPTH - 1
        j = i // 2
        mod_l = (jax.nn.silu(c) @ ada_w[i] + ada_b[i])[:, None, :]
        mod_c = jax.nn.silu(c_ctx) @ ada_w[i] + ada_b[i]
        sh1, sc1, g1, sh2, sc2, g2 = jnp.split(mod_l, 6, axis=-1)
        csh1, csc1, cg1, csh2, csc2, cg2 = jnp.split(mod_c, 6, axis=-1)
        h_lat = rms_norm(x, norm_mix[i]) * (1.0 + sc1) + sh1
        h_ctx = rms_norm(ctx, norm_mix[i]) * (1.0 + csc1) + csh1
        if i % 2 == 0:
            m_lat, m_ctx = even_mixer(h_lat, h_ctx, ev_w_in[j], ev_conv_w[j], ev_conv_b[j], dn_a_log[j], dn_dt_bias[j], dn_norm[j],
                                      ssd_a_log[j], ssd_dt_bias[j], ssd_d[j], ssd_norm[j], ev_w_out[j], not last)
        else:
            lambda_init = 0.8 - 0.6 * math.exp(-0.3 * i)
            m_lat, m_ctx = odd_mixer(h_lat, h_ctx, od_w_in[j], da_q_norm[j], da_k_norm[j], da_lambda[j], da_sub_norm[j], lambda_init,
                                     mla_q_a_norm[j], mla_w_uq[j], mla_kv_a_norm[j], mla_w_ukv[j], mla_q_norm[j], mla_k_norm[j],
                                     od_w_out[j], not last)
        x = x + g1 * m_lat
        x = x + g2 * swiglu(rms_norm(x, norm_ffn[i]) * (1.0 + sc2) + sh2, ffn_w_in[i], ffn_w_out[i])
        if not last:
            ctx = ctx + cg1 * m_ctx
            ctx = ctx + cg2 * swiglu(rms_norm(ctx, norm_ffn[i]) * (1.0 + csc2) + csh2, ffn_w_in[i], ffn_w_out[i])
    return x


_drawn_inputs = setup_inputs


def setup_inputs(seed=0):
    import zlib

    import numpy as np

    out = dict(_drawn_inputs(seed))
    spreads = {}
    factors = {'norm_mix': 3.835,
     'norm_ffn': 3.133,
     'ev_conv_b': 4.682,
     'dn_norm': 7.999,
     'ssd_d': 200.0,
     'ssd_norm': 7.618,
     'da_q_norm': 8.0,
     'da_k_norm': 8.0,
     'da_sub_norm': 200.0,
     'mla_q_a_norm': 23.612,
     'mla_kv_a_norm': 26.78,
     'mla_q_norm': 23.873,
     'mla_k_norm': 22.983,
     'da_lambda': 2.847}
    for name, (base, spread) in spreads.items():
        noise = np.random.default_rng([zlib.crc32(name.encode()), seed]).standard_normal(out[name].shape)
        drawn = base * np.exp(spread * noise) if base else spread * noise
        out[name] = jnp.asarray(drawn.astype(out[name].dtype))
    for name, factor in factors.items():
        out[name] = (out[name] * factor).astype(out[name].dtype)
    return out
```

```python
import math
from contextlib import ExitStack

import numpy as np

import concourse.bass as bass
from concourse import mybir

P = 128
D = 1024
KD = D // P
LAT = 512
CTX = 256
T = LAT + CTX
NT = T // P
EPS = 1e-6
GRID_W = 64
ROPE_THETA = 10000.0
CONV_K = 5
DN_HEADS = 8
SSD_HEADS = 16
EV_CONV = 3 * 1024 + 1024 + 512
EV_GATE = 2048
EV_MAIN = EV_CONV + EV_GATE
EV_IN = EV_MAIN + 64
CONV_CHUNKS = EV_CONV // P
GATE_CHUNKS = EV_GATE // P
HIDDEN = 2816
HC = HIDDEN // P
HG = HC // 2
DA_HEADS = 8
MLA_HEADS = 8
LAMBDA_INIT = 0.8 - 0.6 * math.exp(-0.3)
NEG = -1.0e30

C_ID = 0
C_UF = 128
C_UB = 256
C_NEGF = 384
C_NEGB = 512
C_ONES = 640
C_BLK = 768
C_ROT = 896
C_LVL = 1024
C_COS = C_LVL + 14 * 128
C_SIN = C_COS + LAT
C_ALL = C_SIN + LAT
LEVELS = 7

V_ADAB = 0
V_NMIX = 96
V_NFFN = 112
V_C = 128
V_CCTX = 136
V_CONVB = 144
V_DNN = 180
V_SSDN = 181
V_DASUB = 189
V_QA = 190
V_KVA = 194
V_SSDD = 224
V_DAQ = 204
V_DAK = 205
V_MQN = 206
V_MQR = 207
V_MKN = 208
V_MKR = 209
V_TAP = 256


def constants():
    i = np.arange(P)
    lower, upper = i[:, None] <= i[None, :], i[:, None] >= i[None, :]
    out = np.zeros((P, C_ALL), np.float32)
    out[:, C_ID:C_ID + P] = np.eye(P)
    out[:, C_UF:C_UF + P] = lower
    out[:, C_UB:C_UB + P] = upper
    out[:, C_NEGF:C_NEGF + P] = np.where(lower, 0.0, NEG)
    out[:, C_NEGB:C_NEGB + P] = np.where(upper, 0.0, NEG)
    out[:, C_ONES:C_ONES + P] = 1.0
    out[:, C_BLK:C_BLK + P] = (i[:, None] // 64) == (i[None, :] // 64)
    rot = np.zeros((P, P), np.float32)
    for r in range(P):
        if r % 32 < 16:
            rot[r + 16, r] = -1.0
        else:
            rot[r - 16, r] = 1.0
    out[:, C_ROT:C_ROT + P] = rot
    for l in range(LEVELS):
        s = 1 << l
        pair = (i[:, None] // (2 * s)) == (i[None, :] // (2 * s))
        odd = (i // s) % 2 == 1
        out[:, C_LVL + l * P:C_LVL + (l + 1) * P] = pair & ~odd[:, None] & odd[None, :]
        out[:, C_LVL + (7 + l) * P:C_LVL + (8 + l) * P] = pair & odd[:, None] & ~odd[None, :]
    inv = np.float32(ROPE_THETA) ** (-np.arange(16, dtype=np.float32) / np.float32(16))
    t = np.arange(LAT)
    for r in range(P):
        axis = (r % 64) // 32
        pos = (t // GRID_W if axis == 0 else t % GRID_W).astype(np.float32)
        ang = pos * inv[r % 16]
        out[r, C_COS:C_COS + LAT] = np.cos(ang)
        out[r, C_SIN:C_SIN + LAT] = np.sin(ang)
    return out



def schedule():
    table, slab, use, chunk = {}, 1, 0, 1
    stages = [("in0", 26, 1), ("out0", 8, 0)]
    for layer in (0, 1):
        if layer:
            stages += [("qk1", 8, 1), ("dv1", 4, 1), ("lat1", 4, 1), ("uq1", 6, 1), ("uk1", 4, 1), ("uv1", 4, 1), ("out1", 8, 0)]
        for g, n in enumerate(GROUPS):
            stages += [(f"fi{layer}{g}", n, 1), (f"fo{layer}{g}", 4, 1)]
    for name, n, wide in stages:
        table[name] = (slab, n, use, chunk)
        slab += n
        chunk += (2 * n if wide else n) - (name == "lat1")
        use += n if wide else n // 2
    return table


GROUPS = (8, 8, 6)
ORDER = ((4, 5, 0, 1, 2, 3), (5, 4, 3, 2, 1, 0))
INTRA = (4, 5, 0, 3, 1, 2)

SHARED = {"sd_arg": ("dn_arg", 24), "sd_d": ("dn_d", 24), "sd_e": ("dn_e", 24), "sd_gg": ("dn_gg", 12),
          "sd_tr": ("dn_tr", 12), "sd_m0": ("dn_at", 24), "sd_m1": ("dn_eb", 24), "sd_tok": ("dn_kv", 24),
          "sd_xdt": ("dn_as", 168), "sd_y": ("dn_x", 168), "sd_yb": ("dn_kk", 12), "ss_acc": ("rec_acc", 12),
          "ss_ch": ("rec_ks", 20), "ss_s": ("rec_s", 20), "ss_sd": ("rec_sd", 16), "ss_su": ("rec_su", 20),
          "ss_t": ("rec_t", 20), "ss_x": ("rec_vs", 20), "ss_yt": ("dn_og", 12), "ss_tt": ("dn_ot", 12),
          "ss_rec": ("dn_orec", 4), "ss_root": ("dn_oroot", 2), "ss_sq": ("dn_sq", 4), "ss_ssum": ("dn_ss", 4),
          "at_r": ("un_rec", 74), "at_w": ("un_root", 37), "at_p": ("un_sq", 37), "an_hi": ("la_hi", 6),
          "an_lo": ("la_lo", 6), "an_n": ("la_n", 6), "an_rec": ("la_rec", 4), "an_root": ("la_root", 2),
          "an_sq": ("la_sq", 6), "an_ss": ("la_ss", 6)}


def build(nc, a, out, scr):
    f32, f32r = mybir.dt.float32, mybir.dt.float32r
    ALU, ACT, AX = mybir.AluOpType, mybir.ActivationFunctionType, mybir.AxisListType
    ds = bass.ds
    S = schedule()
    whole = ExitStack()
    table = {}

    def sig(name):
        name = SHARED[name][0] if name in SHARED else name
        if name not in table:
            table[name] = whole.enter_context(nc.semaphore(name))
        return table[name]

    def past(name):
        return SHARED[name][1]

    def tile(stack, name, shape, dt=f32):
        return stack.enter_context(nc.sbuf_tensor(name, [P] + shape, dt))

    with whole:
        cst = tile(whole, "cst", [C_ALL])
        vec = tile(whole, "vec", [512])
        xT = tile(whole, "xT", [KD, T])
        raw = [tile(whole, f"raw{j}", [2048]) for j in range(2)]
        modl = tile(whole, "modl", [96])
        modc = tile(whole, "modc", [96])
        amod = tile(whole, "amod", [2, KD])
        csil = tile(whole, "csil", [16])
        lam = tile(whole, "lam", [8])
        gts = tile(whole, "gts", [NT, 64])
        gcol = tile(whole, "gcol", [5, NT, 48])
        bet = tile(whole, "bet", [NT, 16])
        dts = tile(whole, "dts", [NT, 32])
        alog, gbias = tile(whole, "alog", [48]), tile(whole, "gbias", [48])
        ps = whole.enter_context(nc.psum_tensor("ps", [P, 8, 512], f32))

        ident = cst[:, C_ID:C_ID + P]
        ones = cst[:, C_ONES:C_ONES + P]
        blk = cst[:, C_BLK:C_BLK + P]
        rot = cst[:, C_ROT:C_ROT + P]
        cos, sin = cst[:, C_COS:C_COS + LAT], cst[:, C_SIN:C_SIN + LAT]
        tri = (cst[:, C_UF:C_UF + P], cst[:, C_UB:C_UB + P])
        neg = (cst[:, C_NEGF:C_NEGF + P], cst[:, C_NEGB:C_NEGB + P])

        def level(d, l):
            c = C_LVL + (7 * d + l) * P
            return cst[:, c:c + P]

        def banks(b, n, w):
            return ps[:, b:b + n, :].rearrange("p b n -> p (b n)")[:, 0:w]

        gemm = ExitStack()
        Wh = [tile(gemm, f"Wh{j}", [2048], f32r) for j in range(2)]
        Wl = [tile(gemm, f"Wl{j}", [2048], f32r) for j in range(2)]
        with ExitStack() as st:
            Hh, Hl = tile(st, "Hh", [KD, T], f32r), tile(st, "Hl", [KD, T], f32r)
            with ExitStack() as s2:
                ada = [tile(s2, f"ada{j}", [KD, 256]) for j in range(3)]
                with ExitStack() as s3:
                    ubuf = [tile(s3, f"ubuf{j}", [776]) for j in range(2)]
                    ybuf = [tile(s3, f"ybuf{j}", [776]) for j in range(2)]
                    obuf = [tile(s3, f"obuf{j}", [776]) for j in range(2)]
                    spw = [tile(s3, f"spw{j}", [NT, 48]) for j in range(6)]
                with ExitStack() as s3:
                    sqb = [tile(s3, f"sqb{j}", [T]) for j in range(2)]
                    rstd = tile(s3, "rstd", [T])
                    nrm = [tile(s3, f"nrm{j}", [T]) for j in range(2)]
                    mdl = [tile(s3, f"mdl{j}", [T]) for j in range(2)]
            with ExitStack() as s2:
                Gh, Gl = tile(s2, "Gh", [8, T], f32r), tile(s2, "Gl", [8, T], f32r)
                sgb = [tile(s2, f"sgb{j}", [T]) for j in range(2)]
                hdb = [tile(s2, f"hdb{j}", [T]) for j in range(2)]
            with ExitStack() as s2:
                latr = tile(s2, "latr", [7, T])
                latn = tile(s2, "latn", [2, T])
                lato = [tile(s2, f"lato{j}", [T]) for j in range(2)]
                qn = [tile(s2, f"qn{j}", [T]) for j in range(2)]
                qsq = [tile(s2, f"qsq{j}", [T]) for j in range(2)]
                qrs = [tile(s2, f"qrs{j}", [T]) for j in range(2)]
                qt = [tile(s2, f"qt{j}", [LAT]) for j in range(2)]
        with ExitStack() as st:
            Mh, Ml = tile(st, "Mh", [16, T], f32r), tile(st, "Ml", [16, T], f32r)
            mst = [tile(st, f"mst{j}", [T]) for j in range(4)]
        with ExitStack() as st:
            att = tile(st, "att", [16, LAT])
            Ah, Al = tile(st, "Ah", [16, LAT], f32r), tile(st, "Al", [16, LAT], f32r)
            asq = [tile(st, f"asq{j}", [LAT]) for j in range(2)]
            ars = [tile(st, f"ars{j}", [LAT]) for j in range(2)]
        gemm.close()
        with ExitStack() as st:
            X = tile(st, "X", [NT, D])
            rows = tile(st, "rows", [4, P])
            lrow = tile(st, "lrow", [4, 64])
            drow = tile(st, "drow", [2])
            Y = tile(st, "Y", [4, D])
        with ExitStack() as st:
            dq, dk, dv = (tile(st, f"d{n}", [4, T]) for n in "qkv")
            ktok, vtok = tile(st, "ktok", [NT, 512]), tile(st, "vtok", [NT, 512])
            TTs, ATs = tile(st, "TTs", [NT, 2, 4, P]), tile(st, "ATs", [NT, 2, 4, P])
            dgg = [tile(st, f"dgg{j}", [2, NT, 4]) for j in range(6)]
            Sst = [tile(st, f"Sst{d}", [4, P]) for d in range(2)]
            drs = tile(st, "drs", [NT, 4])
            with ExitStack() as s2:
                Ed = [tile(s2, f"Ed{d}", [4, P]) for d in range(2)]
                EB = [tile(s2, f"EB{d}", [4, P]) for d in range(2)]
                AT = [tile(s2, f"AT{d}", [4, P]) for d in range(2)]
                Am = [[tile(s2, f"Am{d}{j}", [4, P]) for j in range(2)] for d in range(2)]
                Tm = [tile(s2, f"Tm{d}", [4, P]) for d in range(2)]
                xs = [tile(s2, f"xs{d}", [4, P]) for d in range(2)]
            with ExitStack() as s2:
                rr = [tile(s2, f"rr{d}", [4, P]) for d in range(2)]
                vn = [tile(s2, f"vn{d}", [4, P]) for d in range(2)]
                vs = [tile(s2, f"vs{d}", [4, P]) for d in range(2)]
                to = [tile(s2, f"to{d}", [4, P]) for d in range(2)]
        with ExitStack() as st:
            sx, sz = tile(st, "sx", [4, T]), tile(st, "sz", [4, T])
            sB, sC = tile(st, "sB", [T]), tile(st, "sC", [T])
            xtok, yacc = tile(st, "xtok", [NT, 512]), tile(st, "yacc", [NT, 512])
            Btok = tile(st, "Btok", [NT, P])
            xdt = tile(st, "xdt", [2, NT, 512])
            sgg = [tile(st, f"sgg{j}", [2, NT, 8]) for j in range(6)]
            Es = [[tile(st, f"Es{d}{f}", [4, P]) for f in range(2)] for d in range(2)]
            bcs = tile(st, "bcs", [P])
            hst = [tile(st, f"hst{d}", [512]) for d in range(2)]
            sty = [tile(st, f"sty{d}", [512]) for d in range(2)]
            sxs = [tile(st, f"sxs{d}", [512]) for d in range(2)]
            ssq = [tile(st, f"ssq{j}", [T]) for j in range(2)]
            srs = tile(st, "srs", [T])
        with ExitStack() as st:
            tile(st, "hold", [8192 + 16 * LAT])
            aq, ak, av = ([tile(st, f"a{n}{j}", [w]) for j in range(2)] for n, w in (("q", LAT), ("k", T), ("v", T)))
            mq, mk, mv = ([tile(st, f"m{n}{j}", [w]) for j in range(2)] for n, w in (("q", LAT), ("k", T), ("v", T)))
            mr = [tile(st, f"mr{j}", [LAT]) for j in range(2)]
            mkr = tile(st, "mkr", [T])
            prb = [tile(st, f"prb{j}", [T]) for j in range(4)]
            pT = [tile(st, f"pT{j}", [NT, LAT]) for j in range(2)]
            stat = [tile(st, f"stat{j}", [8]) for j in range(2)]

        def phase_begin(eng, k):
            for e in ("pe", "act", "dve", "pool"):
                eng.wait_ge(sig(f"{e}_phase"), k)

        def phase_end(eng, name):
            eng.drain().then_inc(sig(f"{name}_phase"), 1)

        def loop(eng, n, body):
            if n > 1:
                with eng.Fori(0, n - 1) as i:
                    body(i, False)
            body(n - 1, True)

        class Link:

            def __init__(self, eng, name, start=0):
                self.eng, self.sem, self.n = eng, sig(name), start

            def __call__(self, ins):
                self.n = self.n + 1
                ins.then_inc(self.sem, 1)
                self.eng.wait_ge(self.sem, self.n)

        def wide(t, k=KD, w=256):
            return t[:, 0:k * w].rearrange("p (k n) -> p k n", k=k)

        def load_slab(sp, n, i, src, k=KD, w=256, view=None):
            dst = wide(raw[n % 2], k, w) if view is None else view(raw[n % 2])
            sp.wait_ge(sig("slab_lo"), 2 * i + n + 1)
            if view is None:
                cut = (0, k // 4, k // 2, k // 2 + k // 4, k) if k != 6 else (0, 2, 4, 5, 6)
                parts = [(slice(cut[j], cut[j + 1]),) for j in range(4)]
            elif k == 4:
                parts = [(slice(j, j + 1),) for j in range(4)]
            else:
                parts = [(slice(j * k // 2, (j + 1) * k // 2), u) for j in range(2) for u in range(2)]
            for part in parts:
                if len(part) == 1 and k == 4:
                    d, s_ = dst[:, part[0].start], src[:, part[0].start]
                elif len(part) == 1:
                    d, s_ = dst[:, part[0]], src[:, part[0]]
                else:
                    d, s_ = dst[:, part[0], part[1]], src[:, part[0], part[1]]
                sp.dma_start(d, s_).then_inc(sig(f"slab_in{n % 2}"), 16)

        def hi_slab(act, n, i, w=2048, before=None):
            act.wait_ge(sig(f"slab_in{n % 2}"), 64 * i + 64 * (n // 2 + 1))
            if before is not None:
                act.wait_ge(sig("gemm_done"), before)
            nc.scalar.activation(Wh[n % 2][:, 0:w], raw[n % 2][:, 0:w], ACT.Copy).then_inc(sig("slab_hi"), 1)

        def lo_slab(pool, n, i, w=2048):
            pool.wait_ge(sig("slab_hi"), 2 * i + n + 1)
            nc.gpsimd.tensor_tensor(Wl[n % 2][:, 0:w], raw[n % 2][:, 0:w], Wh[n % 2][:, 0:w].bitcast(f32),
                                    ALU.subtract).then_inc(sig("slab_lo"), 1)

        scr_p = scr["chunks"].rearrange("m p t -> p m t")
        vscr = scr["values"]
        mix_p = scr["mix"].rearrange("m p t -> p m t")

        def rows_from():
            def put(col, src, n):
                return rows[col % P:col % P + n, col // P, :], src
            r = [put(V_ADAB, a["ada_b"].rearrange("l (r n) -> (l r) n", n=P), 96),
                 put(V_NMIX, a["norm_mix"].rearrange("l (r n) -> (l r) n", n=P), 16),
                 put(V_NFFN, a["norm_ffn"].rearrange("l (r n) -> (l r) n", n=P), 16),
                 put(V_C, a["c"].rearrange("b (r n) -> (b r) n", n=P), 8),
                 put(V_CCTX, a["c_ctx"].rearrange("(r n) -> r n", n=P), 8),
                 put(V_CONVB, a["ev_conv_b"].rearrange("l (r n) -> (l r) n", n=P), 36),
                 put(V_DNN, a["dn_norm"], 1),
                 put(V_SSDN, a["ssd_norm"].rearrange("l (r n) -> (l r) n", n=P), 8),
                 put(V_DASUB, a["da_sub_norm"], 1),
                 put(V_QA, a["mla_q_a_norm"].rearrange("l (r n) -> (l r) n", n=P), 4),
                 put(V_KVA, a["mla_kv_a_norm"].rearrange("l (r n) -> (l r) n", n=P), 2),
                 put(V_MQN, a["mla_q_norm"][:, 0:P], 1),
                 put(V_MKN, a["mla_k_norm"][:, 0:P], 1)]
            for k in range(CONV_K):
                r.append((rows[36 * (k % 3):36 * (k % 3) + 36, 2 + k // 3, :],
                          a["ev_conv_w"][0, k, :].rearrange("(r n) -> r n", n=P)))
            for col, src in ((V_DAQ, a["da_q_norm"]), (V_DAK, a["da_k_norm"]),
                             (V_MQR, a["mla_q_norm"][:, P:P + 64]), (V_MKR, a["mla_k_norm"][:, P:P + 64])):
                for hf in range(2):
                    r.append((rows[col % P:col % P + 1, col // P, 64 * hf:64 * hf + 64], src))
            r.append((drow[V_SSDD % P:V_SSDD % P + 8, :], a["ssd_d"].rearrange("l (r two) -> (l r) two", two=2)))
            r.append((gbias[:, 0:16], a["dn_dt_bias"].rearrange("l d h -> l (d h)").broadcast_to([P, 16])))
            r.append((gbias[:, 16:48], a["ssd_dt_bias"].rearrange("l d h -> l (d h)").broadcast_to([P, 32])))
            r.append((alog[:, 0:16], a["dn_a_log"].rearrange("l d h -> l (d h)").broadcast_to([P, 16])))
            r.append((alog[:, 16:48], a["ssd_a_log"].rearrange("l d h -> l (d h)").broadcast_to([P, 32])))
            r.append((lrow[:, :, :].rearrange("p a n -> p (a n)"), a["da_lambda"].rearrange("l a n -> l (a n)").broadcast_to([P, 256])))
            return r

        def product(pe, pair, use, lhs, rhs, k, w, m=P):
            pe.wait_ge(sig(f"gemm_evac{pair}"), use + 1)
            for c in range(k):
                for b, (t0, t1) in enumerate(((0, min(w, 512)), (512, w))):
                    if t1 <= t0:
                        continue
                    o = ps[0:m, 2 * pair + b, 0:t1 - t0]
                    nc.tensor.matmul(o, lhs(c)[0], rhs(c, t0, t1)[0], start=(c == 0), stop=False)
                    nc.tensor.matmul(o, lhs(c)[0], rhs(c, t0, t1)[1], start=False, stop=False)
                    last = nc.tensor.matmul(o, lhs(c)[1], rhs(c, t0, t1)[0], start=False, stop=(c == k - 1))
            return last.then_inc(sig("gemm_done"), 1)

        def slab_ready(pe, n, i):
            pe.wait_ge(sig("slab_lo"), 2 * i + n + 3)

        def pe_wide(pe, name, k, hh, hl, w, between=None):
            n0, ns, u0, c0 = S[name]

            def body(i, last):
                for jj in range(2):
                    n = n0 + jj
                    slot = n % 2
                    slab_ready(pe, n, i)
                    for cc in range(2):
                        lw, ll = wide(Wh[slot], k), wide(Wl[slot], k)
                        ins = product(pe, cc, 2 * i + u0 + jj,
                                      lambda c: (lw[:, c, cc * P:(cc + 1) * P], ll[:, c, cc * P:(cc + 1) * P]),
                                      lambda c, t0, t1: (hh[:, c, t0:t1], hl[:, c, t0:t1]), k, w)
                    if between:
                        between(i, jj)
            loop(pe, ns // 2, body)

        def pe_narrow(pe, name, k, hh, hl, w):
            n0, ns, u0, c0 = S[name]

            def body(i, last):
                for jj in range(2):
                    n = n0 + jj
                    slot = n % 2
                    slab_ready(pe, n, i)
                    lw, ll = wide(Wh[slot], k, P), wide(Wl[slot], k, P)
                    product(pe, jj, i + u0, lambda c: (lw[:, c, :], ll[:, c, :]),
                            lambda c, t0, t1: (hh[:, c, t0:t1], hl[:, c, t0:t1]), k, w)
            loop(pe, ns // 2, body)

        def pe_rows(pe, name, k, hh, hl):
            n0, ns, u0, c0 = S[name]

            def body(i, last):
                for jj in range(2):
                    n = n0 + jj
                    slot = n % 2
                    slab_ready(pe, n, i)
                    lw, ll = wide(Wh[slot], k), wide(Wl[slot], k)
                    for cc in range(2):
                        pe.wait_ge(sig(f"gemm_evac{cc}"), 2 * i + u0 + jj + 1)
                        for r in range(3):
                            t = (3 * cc + r) * P
                            o = ps[:, 2 * cc + r // 2, (r % 2) * 256:(r % 2) * 256 + 256]
                            for c in range(k):
                                nc.tensor.matmul(o, hh[:, c, t:t + P], lw[:, c, :], start=(c == 0), stop=False)
                                nc.tensor.matmul(o, hh[:, c, t:t + P], ll[:, c, :], start=False, stop=False)
                                ins = nc.tensor.matmul(o, hl[:, c, t:t + P], lw[:, c, :], start=False, stop=(c == k - 1))
                        ins.then_inc(sig("gemm_done"), 1)
            loop(pe, ns // 2, body)

        def pe_ada(pe, q, it):
            pe.wait_ge(sig(f"ada_in{q}"), 16 * it + 16)
            for cc in range(2):
                for k in range(KD):
                    ins = nc.tensor.matmul(ps[:, 4, 4 * q + 2 * cc:4 * q + 2 * cc + 2], ada[q][:, k, cc * P:(cc + 1) * P],
                                           csil[:, k:16:8], start=(k == 0), stop=(k == KD - 1))
            ins.then_inc(sig("ada_used"), 1)

        def pe_norm(pe, r, w):
            for k in range(KD):
                pe.wait_ge(sig("sq_done"), 8 * r + k + 1)
                nc.tensor.matmul(ps[:, 6, 0:512], ones, sqb[k % 2][:, 0:512], start=(k == 0), stop=(k == KD - 1))\
                    .then_inc(sig("sq_used"), 1)
                if w > 512:
                    nc.tensor.matmul(ps[:, 7, 0:256], ones, sqb[k % 2][:, 512:768], start=(k == 0), stop=(k == KD - 1))\
                        .then_inc(sig("sq_used2"), 1)

        def pe_setup(pe):
            pe.wait_ge(sig("consts_in"), 16)
            pe.wait_ge(sig("rows_in"), 16 * len(rows_from()))
            pe.wait_ge(sig("rows_spread"), 1)
            for j in range(4):
                ins = nc.tensor.transpose(ps[:, 7, j * P:(j + 1) * P], rows[:, j, :], ident)
            ins.then_inc(sig("rows_turned"), 1)
            for t in range(NT):
                pe.wait_ge(sig("x_in"), 32)
                for hf in range(2):
                    u = 2 * t + hf
                    if u >= 6:
                        pe.wait_ge(sig("xt_evac"), u - 5)
                    for r in range(4):
                        k = 4 * hf + r
                        ins = nc.tensor.transpose(ps[:, u % 6, r * P:(r + 1) * P], X[:, t, k * P:(k + 1) * P], ident)
                    ins.then_inc(sig("xt_done"), 1)

        def pe_gate_products(pe):
            slab_ready(pe, 0, 0)
            lw, ll = wide(Wh[0], KD, 64), wide(Wl[0], KD, 64)
            for t in range(NT):
                o = ps[:, 5, t * 64:(t + 1) * 64]
                for c in range(KD):
                    tt = slice(t * P, (t + 1) * P)
                    nc.tensor.matmul(o, Hh[:, c, tt], lw[:, c, :], start=(c == 0), stop=False)
                    nc.tensor.matmul(o, Hh[:, c, tt], ll[:, c, :], start=False, stop=False)
                    ins = nc.tensor.matmul(o, Hl[:, c, tt], lw[:, c, :], start=False, stop=(c == KD - 1))
            ins.then_inc(sig("gemm_done"), 1)

        def sets(v, l, par):
            return v.rearrange("p (n two s) -> p n two s", two=2, s=1 << l)[:, :, par, :]

        def pe_deltanet(pe, g):
            for x in range(2):
                pe.wait_ge(sig("dn_sq"), 2 * g + x + 1)
                if x:
                    pe.wait_ge(sig("dn_rec"), 4 * g + 1)
                flat = TTs[:, :, :, :, :].rearrange("p c d h n -> p (c d h n)")
                for b in range(6):
                    ins = nc.tensor.matmul(ps[:, b, :], ones, flat[:, x * 3072 + b * 512:x * 3072 + (b + 1) * 512],
                                           start=True, stop=True)
                ins.then_inc(sig("dn_ss"), 1)
            pe.wait_ge(sig("dn_unit"), 2 * g + 2)
            pe.wait_ge(sig("dn_gg"), 6 * g + 6)
            pe.wait_ge(sig("ld_dv"), 16 * g + 16)
            for q, c in enumerate(INTRA):
                tc = slice(c * P, (c + 1) * P)
                if q:
                    pe.wait_ge(sig("dn_xs"), 72 * g + 12 * q)
                for b, src in ((4, dk), (5, dv)):
                    for h in range(4):
                        ins = nc.tensor.transpose(ps[:, b, h * P:(h + 1) * P], src[:, h, tc], ident)
                ins.then_inc(sig("dn_tr"), 1)
                if q:
                    pe.wait_ge(sig("dn_at"), 12 * g + 2 * q)
                for b, mv_ in ((0, dk), (1, dq)):
                    for h in range(4):
                        ins = nc.tensor.matmul(ps[:, b, h * P:(h + 1) * P], dk[:, h, tc], mv_[:, h, tc], start=True, stop=True)
                ins.then_inc(sig("dn_kk"), 1)
                for d in range(2):
                    if q:
                        pe.wait_ge(sig("dn_tt"), 72 * g + 12 * q - 1 + d)
                    nc.tensor.matmul(ps[:, 2 + d, :], tri[d], dgg[1][:, d, c, :].unsqueeze(2).broadcast_to([P, 4, P]),
                                     start=True, stop=False, skip_group_check=True)
                    for h in range(4):
                        ins = nc.tensor.matmul(ps[:, 2 + d, h * P:(h + 1) * P],
                                               dgg[0][:, d, c, h:h + 1].broadcast_to([P, P]), tri[d],
                                               start=False, stop=(h == 3), skip_group_check=True)
                    ins.then_inc(sig("dn_d"), 1)
                for d in range(2):
                    pe.wait_ge(sig("dn_as"), 84 * g + 14 * q + d + 1)
                    if d == 0:
                        pe.wait_ge(sig("dn_kv"), 12 * g + 2 * q + 2)
                    for h in range(4):
                        ins = nc.tensor.transpose(ps[:, 4 + d, h * P:(h + 1) * P], Am[d][0][:, h, :], ident)
                    ins.then_inc(sig("dn_x"), 1)
                for l in range(1, LEVELS):
                    for d in range(2):
                        pe.wait_ge(sig("dn_as"), 84 * g + 14 * q + 2 * l + d + 1)
                        pe.wait_ge(sig("dn_t"), 72 * g + 12 * q + 2 * (l - 1) + d + 1)
                        for h in range(4):
                            ins = nc.tensor.matmul(ps[:, 4 + d, h * P:(h + 1) * P], Am[d][l % 2][:, h, :], Tm[d][:, h, :],
                                                   start=True, stop=True)
                        ins.then_inc(sig("dn_x"), 1)
                    for d in range(2):
                        TT = TTs[:, c, d, :, :]
                        pe.wait_ge(sig("dn_xs"), 72 * g + 12 * q + 2 * (l - 1) + d + 1)
                        if l == 1:
                            pe.wait_ge(sig("dn_tt0"), 12 * g + 2 * q + d + 1)
                        else:
                            pe.wait_ge(sig("dn_tt"), 72 * g + 12 * q + 2 * (l - 2) + d + 1)
                        if l < LEVELS - 1:
                            for h in range(4):
                                ins = nc.tensor.matmul(ps[:, 6 + d, h * 64:(h + 1) * 64], TT[:, h, :],
                                                       sets(xs[d][:, h, :], l, d), start=True, stop=True)
                            ins.then_inc(sig("dn_tb"), 1)
                        for h in range(4):
                            ins = nc.tensor.matmul(ps[:, 2 + d, h * 64:(h + 1) * 64], xs[d][:, h, :],
                                                   sets(TT[:, h, :], l, 1 - d), start=True, stop=True)
                        ins.then_inc(sig("dn_ttb"), 1)
            pe.wait_ge(sig("dn_tt"), 72 * g + 72)
            pe.wait_ge(sig("dn_kv"), 12 * g + 12)
            pe.wait_ge(sig("dn_at"), 12 * g + 12)
            for k in range(NT):
                cs = [ORDER[d][k] for d in range(2)]
                if k:
                    for bank, src, name in ((0, dk, "rec_ks"), (2, dq, "rec_qs")):
                        for d in range(2):
                            tc = slice(cs[d] * P, (cs[d] + 1) * P)
                            pe.wait_ge(sig("rec_s"), 10 * g + 2 * (k - 1) + d + 1)
                            if k > 1 and bank == 2:
                                pe.wait_ge(sig("rec_t"), 10 * g + 2 * (k - 2) + d + 1)
                            for h in range(4):
                                ins = nc.tensor.matmul(ps[:, bank + d, h * P:(h + 1) * P], src[:, h, tc], Sst[d][:, h, :],
                                                       start=True, stop=True)
                            ins.then_inc(sig(name), 1)
                for d in range(2):
                    r = rr[d] if k else vtok[:, cs[d], :].rearrange("p (h n) -> p h n", h=4)
                    if k:
                        pe.wait_ge(sig("rec_r"), 10 * g + 2 * (k - 1) + d + 1)
                        pe.wait_ge(sig("rec_o"), 12 * g + 2 * (k - 1) + d + 1)
                    for h in range(4):
                        ins = nc.tensor.matmul(ps[:, 4 + d, h * P:(h + 1) * P], TTs[:, cs[d], d, h, :], r[:, h, :],
                                               start=True, stop=True)
                    ins.then_inc(sig("rec_v"), 1)
                for d in range(2):
                    if k < NT - 1:
                        pe.wait_ge(sig("rec_vs"), 10 * g + 2 * k + d + 1)
                        for h in range(4):
                            ins = nc.tensor.matmul(ps[:, 6 + d, h * P:(h + 1) * P], ktok[:, cs[d], h * P:(h + 1) * P],
                                                   vs[d][:, h, :], start=True, stop=True)
                        ins.then_inc(sig("rec_su"), 1)
                for d in range(2):
                    pe.wait_ge(sig("rec_vn"), 12 * g + 2 * k + d + 1)
                    for h in range(4):
                        ins = nc.tensor.matmul(ps[:, 4 + d, h * P:(h + 1) * P], ATs[:, cs[d], d, h, :], vn[d][:, h, :],
                                               start=True, stop=True)
                    ins.then_inc(sig("rec_ob"), 1)
            pe.wait_ge(sig("dn_on"), g + 1)
            oacc = dv[:, :, :].rearrange("p h t -> p (h t)").rearrange("p (c n) -> p c n", c=NT)
            for c in range(NT):
                if c >= 2:
                    pe.wait_ge(sig("dn_og"), 6 * g + c - 1)
                for h in range(4):
                    ins = nc.tensor.transpose(ps[:, 4 + c % 2, h * P:(h + 1) * P], oacc[:, c, h * P:(h + 1) * P], ident)
                ins.then_inc(sig("dn_ot"), 1)

        def pe_ssd(pe, g):
            pe.wait_ge(sig("sd_gg"), past("sd_gg") + 6 * g + 6)
            pe.wait_ge(sig("sd_in"), 64 * g + 64)
            for q, c in enumerate(INTRA):
                tc = slice(c * P, (c + 1) * P)
                if q:
                    pe.wait_ge(sig("sd_tok"), past("sd_tok") + 18 * g + 3 * q)
                for h in range(4):
                    nc.tensor.transpose(ps[:, 0, h * P:(h + 1) * P], sx[:, h, tc], ident)
                nc.tensor.transpose(ps[:, 1, 0:P], sB[:, tc], ident)
                nc.tensor.matmul(ps[:, 2, 0:P], sB[:, tc], sC[:, tc], start=True, stop=True).then_inc(sig("sd_tr"), 1)
                for d in range(2):
                    for f in range(2):
                        b = 3 + 2 * d + f
                        if q:
                            pe.wait_ge(sig("sd_arg"), past("sd_arg") + 24 * g + 4 * (q - 1) + 2 * d + f + 1)
                        nc.tensor.matmul(ps[:, b, :], tri[d], sgg[1][:, d, c, 4 * f:4 * f + 4].unsqueeze(2).broadcast_to([P, 4, P]),
                                         start=True, stop=False, skip_group_check=True)
                        for h in range(4):
                            ins = nc.tensor.matmul(ps[:, b, h * P:(h + 1) * P],
                                                   sgg[0][:, d, c, 4 * f + h:4 * f + h + 1].broadcast_to([P, P]), tri[d],
                                                   start=False, stop=(h == 3), skip_group_check=True)
                        ins.then_inc(sig("sd_d"), 1)
                if q:
                    pe.wait_ge(sig("sd_y"), past("sd_y") + 6 * g + q)
                pe.wait_ge(sig("sd_m0"), past("sd_m0") + 12 * g + 2 * q + 2)
                pe.wait_ge(sig("sd_m1"), past("sd_m1") + 12 * g + 2 * q + 2)
                pe.wait_ge(sig("sd_xdt"), past("sd_xdt") + 12 * g + 2 * q + 2)
                for h in range(8):
                    for d in range(2):
                        ins = nc.tensor.matmul(ps[:, 7, h * 64:(h + 1) * 64], Es[d][h // 4][:, h % 4, :],
                                               xdt[:, d, c, h * 64:(h + 1) * 64], start=(d == 0), stop=(d == 1))
                ins.then_inc(sig("sd_yb"), 1)
            for k in range(NT):
                for d in range(2):
                    c = ORDER[d][k]
                    tc = slice(c * P, (c + 1) * P)
                    if k:
                        pe.wait_ge(sig("ss_s"), past("ss_s") + 10 * g + 2 * (k - 1) + d + 1)
                        if k > 1:
                            pe.wait_ge(sig("ss_t"), past("ss_t") + 10 * g + 2 * (k - 2) + d + 1)
                        nc.tensor.matmul(ps[:, d, :], sC[:, tc], hst[d][:, :], start=True, stop=True).then_inc(sig("ss_ch"), 1)
                    if k < NT - 1:
                        pe.wait_ge(sig("ss_x"), past("ss_x") + 10 * g + 2 * k + d + 1)
                        nc.tensor.matmul(ps[:, 2 + d, :], Btok[:, c, :], sxs[d][:, :], start=True, stop=True)\
                            .then_inc(sig("ss_su"), 1)
            pe.wait_ge(sig("ss_acc"), past("ss_acc") + 10 * g + 10)
            for c in range(NT):
                if c >= 2:
                    pe.wait_ge(sig("ss_yt"), past("ss_yt") + 6 * g + c - 1)
                for h in range(4):
                    ins = nc.tensor.transpose(ps[:, 4 + c % 2, h * P:(h + 1) * P], yacc[:, c, h * P:(h + 1) * P], ident)
                ins.then_inc(sig("ss_tt"), 1)
            for h in range(4):
                pe.wait_ge(sig("ss_sq"), past("ss_sq") + 4 * g + h + 1)
                nc.tensor.matmul(ps[:, 6, 0:512], ones, ssq[h % 2][:, 0:512], start=(h == 0), stop=(h == 3))
                nc.tensor.matmul(ps[:, 7, 0:256], ones, ssq[h % 2][:, 512:768], start=(h == 0), stop=(h == 3))\
                    .then_inc(sig("ss_ssum"), 1)

        KINDS = (("dq", 0, 8, LAT, 64, V_DAQ, True), ("dk", 8, 8, T, 64, V_DAK, True),
                 ("qn", 16, 8, LAT, P, V_MQN, False), ("qr", 24, 4, LAT, 64, V_MQR, True),
                 ("kn", 28, 8, T, P, V_MKN, False), ("kr", 36, 1, T, 64, V_MKR, True))

        def units(eng, unit):
            rotated = 0
            for kind in KINDS:
                _, u0, n, _, _, _, rope = kind
                if n == 1:
                    unit(kind, u0, 0, 0, rotated)
                else:
                    with eng.Fori(0, n // 2) as i:
                        for j in range(2):
                            unit(kind, u0 + j, i, j, rotated + j)
                rotated += n if rope else 0

        def pe_units(pe):
            def unit(kind, u, i, j, r):
                _, _, _, w, span, _, rope = kind
                mat = ones if span == P else blk
                pe.wait_ge(sig("un_sq"), 2 * i + u + 1)
                nc_last = None
                for b, (t0, t1) in enumerate(((0, 512), (512, w))):
                    if t1 > t0:
                        nc_last = nc.tensor.matmul(ps[:, 2 * j + b, 0:t1 - t0], mat, qsq[j][:, t0:t1], start=True, stop=True)
                nc_last.then_inc(sig("un_ss"), 1)
                if rope:
                    pe.wait_ge(sig("un_n"), 2 * i + u + 1)
                    nc.tensor.matmul(ps[:, 4 + j, :], rot, qn[j][:, 0:LAT], start=True, stop=True).then_inc(sig("un_rot"), 1)
            units(pe, unit)

        def attention_units():
            used, out = [0, 0], []
            for hu in range(4):
                da, hh = hu % 2 == 0, hu // 2
                for qt in range(4):
                    pairs = []
                    for p in ((0, 1) if da else (qt % 2,)):
                        pairs.append((p, used[p]))
                        used[p] += 1
                    out.append((4 * hu + qt, da, hh, qt, pairs))
            assert used == [12, 12]
            return out

        def pe_attention(pe):
            U = attention_units()
            with pe.Fori(0, 4) as i:
                def scores(u, da, hh, qt, pairs):
                    if qt == 0:
                        pe.wait_ge(sig(f"at_in{hh}{0 if da else 1}"), (48 if da else 64) * i + (48 if da else 64))
                    tq = slice(qt * P, (qt + 1) * P)
                    for p, use in pairs:
                        pe.wait_ge(sig(f"at_e{p}"), 12 * i + use + 1)
                        rows_ = slice(64 * p, 64 * p + 64) if da else slice(0, P)
                        q_, k_ = (aq[hh], ak[hh]) if da else (mq[hh], mk[hh])
                        for b, (t0, t1) in enumerate(((0, 512), (512, T))):
                            o = ps[:, 2 * p + b, 0:t1 - t0]
                            ins = nc.tensor.matmul(o, q_[rows_, tq], k_[rows_, t0:t1], start=True, stop=da)
                            if not da:
                                ins = nc.tensor.matmul(o, mr[hh][0:64, tq], mkr[0:64, t0:t1], start=False, stop=True)
                        ins.then_inc(sig(f"at_s{p}"), 1)
                scores(*U[0])
                for u, da, hh, qt, _ in U:
                    if u < 15:
                        scores(*U[u + 1])
                    pe.wait_ge(sig("at_p"), past("at_p") + 16 * i + u + 1)
                    pe.wait_ge(sig("at_pt"), 16 * i + u + 1)
                    for kt in range(NT):
                        ins = nc.tensor.transpose(ps[:, 4 + kt // 4, (kt % 4) * P:(kt % 4 + 1) * P],
                                                  prb[2 * (u % 2)][:, kt * P:(kt + 1) * P], ident)
                    ins.then_inc(sig("at_tr"), 1)
                    if qt == 3:
                        hu = u // 4
                        pe.wait_ge(sig("at_pt"), 16 * i + u + 2)
                        pe.wait_ge(sig("at_o"), 4 * i + hu + 1)
                        v_ = (av if da else mv)[hh]
                        for kt in range(NT):
                            ins = nc.tensor.matmul(ps[:, 6 + hu % 2, :], v_[:, kt * P:(kt + 1) * P], pT[hu % 2][:, kt, :],
                                                   start=(kt == 0), stop=(kt == NT - 1))
                        ins.then_inc(sig("at_pv"), 1)

        def pe_latents(pe):
            for k in range(6):
                pe.wait_ge(sig("la_sq"), k + 1)
                if k < 4:
                    ins = nc.tensor.matmul(ps[:, 6, :], ones, lato[k % 2][:, 0:512], start=(k == 0), stop=(k == 3))
                else:
                    nc.tensor.matmul(ps[:, 4, :], ones, lato[k % 2][:, 0:512], start=(k == 4), stop=(k == 5))
                    ins = nc.tensor.matmul(ps[:, 5, 0:256], ones, lato[k % 2][:, 512:T], start=(k == 4), stop=(k == 5))
                ins.then_inc(sig("la_ss"), 1)

        def pe_ffn(pe, layer, w):
            for grp, n in enumerate(GROUPS):
                pe_wide(pe, f"fi{layer}{grp}", KD, Hh, Hl, w)
                pe.wait_ge(sig("hid_lo"), 22 * layer + sum(GROUPS[:grp + 1]))
                pe.wait_ge(sig("hid_hi"), 22 * layer + sum(GROUPS[:grp + 1]))
                pe_wide(pe, f"fo{layer}{grp}", n, Gh, Gl, w)

        def pe_att_norm(pe):
            for k in range(8):
                pe.wait_ge(sig("an_sq"), past("an_sq") + k + 1)
                nc.tensor.matmul(ps[:, 4 + k % 2, :], ones, asq[k % 2][:, :], start=True, stop=True).then_inc(sig("an_ss"), 1)

        def tensor_program(pe):
            pe_setup(pe)
            for it in range(3):
                if it == 0:
                    pe.wait_ge(sig("silu_c"), 1)
                    pe.wait_ge(sig("xt_evac"), 12)
                else:
                    pe.wait_ge(sig("mod_evac"), it)
                for q in range(3):
                    pe_ada(pe, q, it)
            phase_end(pe, "pe")
            phase_begin(pe, 1)
            pe_norm(pe, 0, T)
            phase_end(pe, "pe")
            phase_begin(pe, 2)
            pe_gate_products(pe)

            def ada_between(i, jj):
                if jj == 0:
                    pe.wait_ge(sig("mod_evac"), i + 3)
                for q in ((0, 1), (2,))[jj]:
                    pe_ada(pe, q, i + 3)
            pe_wide(pe, "in0", KD, Hh, Hl, T, ada_between)
            phase_end(pe, "pe")
            phase_begin(pe, 3)
            flat = gcol[:, 0, :, :].rearrange("p c n -> p (c n)")
            for b, mat in enumerate((tri[0], tri[1], ones)):
                ins = nc.tensor.matmul(ps[:, b, 0:NT * 48], mat, flat, start=True, stop=True)
            ins.then_inc(sig("cum_sums"), 1)
            pe.wait_ge(sig("cum_ready"), 6)
            for base, part in ((3, pe_deltanet), (5, pe_ssd)):
                with pe.Fori(0, 2) as g:
                    phase_begin(pe, base + g)
                    part(pe, g)
                    phase_end(pe, "pe")
            phase_begin(pe, 7)
            pe.wait_ge(sig("mix_lo"), 16)
            pe.wait_ge(sig("mix_hi"), 16)
            pe_narrow(pe, "out0", 16, Mh, Ml, T)
            phase_end(pe, "pe")
            phase_begin(pe, 8)
            pe_norm(pe, 1, T)
            phase_end(pe, "pe")
            phase_begin(pe, 9)
            pe_ffn(pe, 0, T)
            phase_end(pe, "pe")
            phase_begin(pe, 10)
            pe_norm(pe, 2, T)
            phase_end(pe, "pe")
            phase_begin(pe, 11)
            pe_qkv1(pe)
            phase_end(pe, "pe")
            phase_begin(pe, 12)
            pe_latents(pe)
            pe.wait_ge(sig("la_lo"), 6)
            pe.wait_ge(sig("la_hi"), 6)
            pe_wide(pe, "uq1", 4, Hh, Hl, LAT)
            pe_wide(pe, "uk1", 2, Hh[:, 4:6, :], Hl[:, 4:6, :], T)
            pe_rows(pe, "uv1", 2, Hh[:, 4:6, :], Hl[:, 4:6, :])
            phase_end(pe, "pe")
            phase_begin(pe, 13)
            pe_units(pe)
            phase_end(pe, "pe")
            phase_begin(pe, 14)
            pe_attention(pe)
            phase_end(pe, "pe")
            phase_begin(pe, 15)
            pe_att_norm(pe)
            pe.wait_ge(sig("an_lo"), past("an_lo") + 16)
            pe.wait_ge(sig("an_hi"), past("an_hi") + 16)
            pe_narrow(pe, "out1", 16, Ah, Al, LAT)
            phase_end(pe, "pe")
            phase_begin(pe, 16)
            pe_norm(pe, 3, LAT)
            phase_end(pe, "pe")
            phase_begin(pe, 17)
            pe_ffn(pe, 1, LAT)
            phase_end(pe, "pe")
            phase_begin(pe, 18)
            for t in range(4):
                for hf in range(2):
                    u = 2 * t + hf
                    for r in range(4):
                        ins = nc.tensor.transpose(ps[:, u, r * P:(r + 1) * P], xT[:, 4 * hf + r, t * P:(t + 1) * P], ident)
                    ins.then_inc(sig("yt_done"), 1)

        def pe_qkv1(pe):
            n0, ns, u0, c0 = S["qk1"]
            for part, w in ((0, LAT), (1, T)):
                def body(i, last):
                    for jj in range(2):
                        n = n0 + 4 * part + jj
                        slot = n % 2
                        slab_ready(pe, n, i)
                        for cc in range(2):
                            lw, ll = wide(Wh[slot]), wide(Wl[slot])
                            ins = product(pe, cc, 2 * i + u0 + 4 * part + jj,
                                          lambda c: (lw[:, c, cc * P:(cc + 1) * P], ll[:, c, cc * P:(cc + 1) * P]),
                                          lambda c, t0, t1: (Hh[:, c, t0:t1], Hl[:, c, t0:t1]), KD, w)
                loop(pe, 2, body)
            pe_rows(pe, "dv1", KD, Hh, Hl)
            n0, ns, u0, c0 = S["lat1"]
            for jj in range(4):
                n = n0 + jj
                slot = n % 2
                slab_ready(pe, n, 0)
                w = LAT if jj < 2 else T
                lw, ll = (wide(Wh[slot]), wide(Wl[slot])) if jj < 3 else (wide(Wh[slot], KD, P), wide(Wl[slot], KD, P))
                for cc in range(2 if jj < 3 else 1):
                    ins = product(pe, cc, u0 + jj,
                                  lambda c: (lw[:, c, cc * P:(cc + 1) * P], ll[:, c, cc * P:(cc + 1) * P]),
                                  lambda c, t0, t1: (Hh[:, c, t0:t1], Hl[:, c, t0:t1]), KD, w)
                ins

        def pairbank(pair, w):
            return banks(2 * pair, 2, w)

        def act_norm(act, r, w, wides):
            for k in range(KD):
                if 8 * r + k >= 2:
                    act.wait_ge(sig("sq_used"), 8 * r + k - 1)
                if k >= 2 and w > 512:
                    act.wait_ge(sig("sq_used2"), 8 * wides + k - 1)
                nc.scalar.activation(sqb[k % 2][:, 0:w], xT[:, k, 0:w], ACT.Square).then_inc(sig("sq_done"), 1)
            act.wait_ge(sig("rec_done"), r + 1)
            nc.scalar.activation(rstd[:, 0:w], rstd[:, 0:w], ACT.Sqrt).then_inc(sig("rstd_done"), 1)
            for k in range(KD):
                act.wait_ge(sig("mod_done"), 8 * r + k + 1)
                nc.scalar.activation(Hh[:, k, 0:w], mdl[k % 2][:, 0:w], ACT.Copy).then_inc(sig("hi_done"), 1)

        def act_stage(act, name, evac, prefetch=True):
            n0, ns, _, c0 = S[name]
            per = 1 if name.startswith("out") else 2

            def body(i, last):
                for jj in range(2):
                    if not (last and jj == 1 and not prefetch):
                        hi_slab(act, n0 + jj + 1, i, before=2 * per * i + c0 + per * jj)
                    if evac:
                        evac(i, jj, S[name][2])
            loop(act, ns // 2, body)

        def act_in0(act):
            n0, ns, u0, c0 = S["in0"]

            def copy_out(i, jj, cc):
                act.wait_ge(sig("gemm_done"), 4 * i + c0 + 2 * jj + cc + 1)
                act.wait_ge(sig("conv_step"), 20 * i + 5 * (2 * jj + cc) + 5)
                nc.scalar.activation(ubuf[cc][:, 2:514], ps[:, 2 * cc, :], ACT.Copy)
                nc.scalar.activation(ubuf[cc][:, 516:772], ps[:, 2 * cc + 1, 0:256], ACT.Copy)\
                    .then_inc(sig(f"gemm_evac{cc}"), 1)

            def silu_out(i, jj, cc):
                m = 4 * i + 2 * jj + cc
                act.wait_ge(sig("conv_step"), 20 * i + 5 * (2 * jj + cc) + 15)
                act.wait_ge(sig(f"store{cc}"), 64 * i + 32 * jj + 32)
                nc.scalar.activation(obuf[cc][:, 0:770], ybuf[cc][:, 0:770], ACT.Silu,
                                     bias=vec[:, ds(V_CONVB + m, 1)]).then_inc(sig("silu_done"), 1)
                act.wait_ge(sig("silu_done"), 4 * i + 2 * jj + cc + 3)
                act.dma_start(scr_p[:, ds(m, 1), 0:512], obuf[cc][:, 0:512].unsqueeze(1)).then_inc(sig(f"store{cc}"), 16)
                act.dma_start(scr_p[:, ds(m, 1), 512:T], obuf[cc][:, 514:770].unsqueeze(1)).then_inc(sig(f"store{cc}"), 16)

            def conv_body(i):
                hi_slab(act, n0 + 1, i, before=4 * i + c0)
                copy_out(i, 0, 0)
                copy_out(i, 0, 1)
                silu_out(i, 0, 0)
                hi_slab(act, n0 + 2, i, before=4 * i + c0 + 2)
                copy_out(i, 1, 0)
                silu_out(i, 0, 1)
                copy_out(i, 1, 1)
                silu_out(i, 1, 0)
                silu_out(i, 1, 1)
            with act.Fori(0, 9) as i:
                conv_body(i)

            def gate_body(i, last):
                for jj in range(2):
                    if not (last and jj == 1):
                        hi_slab(act, n0 + 18 + jj + 1, i, before=4 * i + c0 + 36 + 2 * jj)
                    for cc in range(2):
                        act.wait_ge(sig("gemm_done"), 4 * i + c0 + 36 + 2 * jj + cc + 1)
                        act.wait_ge(sig(f"store{cc}"), 64 * i + 32 * jj + 64 * 9 + 32)
                        nc.scalar.activation(obuf[cc][:, 0:T], pairbank(cc, T), ACT.Silu)\
                            .then_inc(sig(f"gemm_evac{cc}"), 1)
                        act.wait_ge(sig(f"gemm_evac{cc}"), 2 * i + 18 + jj + 2)
                        m = 4 * i + 2 * jj + cc + 36
                        act.dma_start(scr_p[:, ds(m, 1), 0:512], obuf[cc][:, 0:512].unsqueeze(1)).then_inc(sig(f"store{cc}"), 16)
                        act.dma_start(scr_p[:, ds(m, 1), 512:T], obuf[cc][:, 512:T].unsqueeze(1)).then_inc(sig(f"store{cc}"), 16)
            loop(act, 4, gate_body)

        def act_deltanet(act, g):
            for x in range(2):
                act.wait_ge(sig("dn_rec"), 4 * g + 2 * x + 2)
                flat = ATs[:, :, :, :, :].rearrange("p c d h n -> p (c d h n)")
                nc.scalar.activation(flat[:, x * 3072:(x + 1) * 3072], flat[:, x * 3072:(x + 1) * 3072], ACT.Sqrt,
                                     scale=(1.0 / P if x == 0 else 1.0)).then_inc(sig("dn_root"), 1)
            for q, c in enumerate(INTRA):
                act.wait_ge(sig("dn_tr"), 6 * g + q + 1)
                nc.scalar.activation(ktok[:, c, :], ps[:, 4, :], ACT.Copy).then_inc(sig("dn_kv"), 1)
                nc.scalar.activation(vtok[:, c, :], ps[:, 5, :], ACT.Copy).then_inc(sig("dn_kv"), 1)
                for d in range(2):
                    act.wait_ge(sig("dn_arg"), 12 * g + 2 * q + d + 1)
                    nc.scalar.activation(Ed[d][:, :, :], Ed[d][:, :, :], ACT.Exp).then_inc(sig("dn_e"), 1)
                for l in range(1, LEVELS):
                    for d in range(2):
                        act.wait_ge(sig("dn_x"), 84 * g + 14 * q + 2 * l + d + 1)
                        if l > 1 or q:
                            act.wait_ge(sig("dn_ttb"), 72 * g + 12 * q + 2 * (l - 2) + d + 1)
                        nc.scalar.activation(xs[d][:, :, :].rearrange("p h n -> p (h n)"), ps[:, 4 + d, :], ACT.Copy)\
                            .then_inc(sig("dn_xs"), 1)
            act.wait_ge(sig("dn_orec"), 2 * g + 2)
            nc.scalar.activation(drs[:, :, :], drs[:, :, :], ACT.Sqrt).then_inc(sig("dn_oroot"), 1)

        def act_ssd(act, g):
            for q, c in enumerate(INTRA):
                act.wait_ge(sig("sd_tr"), past("sd_tr") + 6 * g + q + 1)
                nc.scalar.activation(xtok[:, c, :], ps[:, 0, :], ACT.Copy).then_inc(sig("sd_tok"), 1)
                nc.scalar.activation(Btok[:, c, :], ps[:, 1, 0:P], ACT.Copy).then_inc(sig("sd_tok"), 1)
                if q:
                    act.wait_ge(sig("sd_m0"), past("sd_m0") + 12 * g + 2 * q)
                    act.wait_ge(sig("sd_m1"), past("sd_m1") + 12 * g + 2 * q)
                nc.scalar.activation(bcs[:, :], ps[:, 2, 0:P], ACT.Copy).then_inc(sig("sd_tok"), 1)
                for d in range(2):
                    for f in range(2):
                        act.wait_ge(sig("sd_arg"), past("sd_arg") + 24 * g + 4 * q + 2 * d + f + 1)
                        nc.scalar.activation(Es[d][f][:, :, :], Es[d][f][:, :, :], ACT.Exp).then_inc(sig("sd_e"), 1)
                act.wait_ge(sig("sd_yb"), past("sd_yb") + 6 * g + q + 1)
                nc.scalar.activation(yacc[:, c, :], ps[:, 7, :], ACT.Copy).then_inc(sig("sd_y"), 1)
            for h in range(4):
                act.wait_ge(sig("ss_gated"), 4 * g + h + 1)
                if h >= 2:
                    act.wait_ge(sig("ss_ssum"), past("ss_ssum") + 4 * g + h - 1)
                nc.scalar.activation(ssq[h % 2][:, :], sx[:, h, :], ACT.Square).then_inc(sig("ss_sq"), 1)
            act.wait_ge(sig("ss_rec"), past("ss_rec") + 2 * g + 2)
            nc.scalar.activation(srs[:, :], srs[:, :], ACT.Sqrt).then_inc(sig("ss_root"), 1)

        def act_ffn(act, layer, w):
            for grp, n in enumerate(GROUPS):
                name = f"fi{layer}{grp}"

                def hidden(i, jj, u0):
                    act.wait_ge(sig("gemm_done"), 4 * i + S[name][3] + 2 * jj + 1)
                    act.wait_ge(sig("gemm_evac1"), 2 * i + u0 + jj)
                    nc.scalar.activation(sgb[jj][:, 0:w], pairbank(0, w), ACT.Silu).then_inc(sig("gemm_evac0"), 1)
                    act.wait_ge(sig("gemm_evac1"), 2 * i + u0 + jj + 2)
                    nc.scalar.activation(Gh[:, ds(2 * i + jj, 1), 0:w], hdb[jj][:, 0:w].unsqueeze(1), ACT.Copy)\
                        .then_inc(sig("hid_hi"), 1)
                act_stage(act, name, hidden)
                act_stage(act, f"fo{layer}{grp}", None, prefetch=not (layer and grp == 2))

        def act_units(act):
            def unit(kind, u, i, j, r):
                w = kind[3]
                act.wait_ge(sig("un_rec"), 4 * i + 2 * u + 2)
                nc.scalar.activation(qrs[j][:, 0:w], qrs[j][:, 0:w], ACT.Sqrt).then_inc(sig("un_root"), 1)
            units(act, unit)

        def act_attention(act):
            U = attention_units()
            with act.Fori(0, 4) as i:
                def exps(u, da, hh, qt, pairs):
                    for x, (p, use) in enumerate(pairs):
                        act.wait_ge(sig(f"at_m{p}"), 12 * i + use + 1)
                        act.wait_ge(sig("at_tr"), 16 * i + u + 1)
                        st = stat[u % 2]
                        nc.scalar.activation(prb[2 * (u % 2) + x][:, :], pairbank(p, T), ACT.Exp,
                                             bias=st[:, x:x + 1], scale=(64 if da else 192) ** -0.5,
                                             accum_out=st[:, 2 + x:3 + x]).then_inc(sig(f"at_e{p}"), 1)

                def turned(u, da, hh, qt, pairs):
                    hu = u // 4
                    act.wait_ge(sig("at_tr"), 16 * i + u + 3)
                    if qt == 0:
                        act.wait_ge(sig("at_pv"), 4 * i + hu + 2)
                    nc.scalar.activation(pT[hu % 2][:, :, qt * P:(qt + 1) * P],
                                         banks(4, 2, T).rearrange("p (k n) -> p k n", k=NT), ACT.Copy)\
                        .then_inc(sig("at_pt"), 1)

                def take(hu):
                    act.wait_ge(sig("at_pv"), 4 * i + hu + 4)
                    nc.scalar.activation(att[:, ds(2 * i + (8 if hu % 2 else 0) + hu // 2, 1), :], ps[:, 6 + hu % 2:7 + hu % 2, :], ACT.Copy)\
                        .then_inc(sig("at_o"), 1)
                exps(*U[0])
                for x in U:
                    u = x[0]
                    if u < 15:
                        exps(*U[u + 1])
                    turned(*x)
                    if u % 4 == 0 and u:
                        take(u // 4 - 1)
                take(3)

        def scalar_program(act):
            act.sem_inc(sig("at_pt"), 1)
            act.sem_inc(sig("at_o"), 2)
            for e in (0, 1):
                act.sem_inc(sig(f"at_e{e}"), 1)
            act.wait_ge(sig("rows_clear"), 1)
            for dst, src in rows_from():
                act.dma_start(dst, src).then_inc(sig("rows_in"), 16)
            act.wait_ge(sig("vec_ready"), 1)
            nc.scalar.activation(csil[:, :], vec[:, V_C:V_C + 16], ACT.Silu).then_inc(sig("silu_c"), 1)
            for u in range(1, 12, 2):
                act.wait_ge(sig("xt_done"), u + 1)
                act.wait_ge(sig("xt_evac"), u)
                t, hf = u // 2, u % 2
                nc.scalar.activation(xT[:, 4 * hf:4 * hf + 4, t * P:(t + 1) * P],
                                     ps[:, u % 6, :].rearrange("p (k n) -> p k n", k=4), ACT.Copy).then_inc(sig("xt_evac"), 1)
            phase_end(act, "act")
            phase_begin(act, 1)
            act_norm(act, 0, T, 0)
            hi_slab(act, 0, 0, 512)
            phase_end(act, "act")
            phase_begin(act, 2)
            hi_slab(act, 1, 0)
            act.wait_ge(sig("gate_step"), 3)
            nc.scalar.activation(bet[:, :, :], gts[:, :, 0:16], ACT.Exp, scale=-1.0).then_inc(sig("gate_exp"), 1)
            nc.scalar.activation(spw[1][:, :, :], spw[1][:, :, :], ACT.Exp).then_inc(sig("gate_exp"), 1)
            nc.scalar.activation(alog[:, :], alog[:, :], ACT.Exp).then_inc(sig("gate_exp"), 1)
            nc.scalar.activation(lam[:, 2:4], lam[:, 0:2], ACT.Exp).then_inc(sig("gate_exp"), 1)
            act_in0(act)
            phase_end(act, "act")
            phase_begin(act, 3)
            act.wait_ge(sig("cum_ready"), 6)
            for j in (2, 3, 4):
                nc.scalar.activation(gcol[:, j, :, :], gcol[:, j, :, :], ACT.Exp).then_inc(sig("cum_exp"), 1)
            for base, part in ((3, act_deltanet), (5, act_ssd)):
                with act.Fori(0, 2) as g:
                    phase_begin(act, base + g)
                    part(act, g)
                    phase_end(act, "act")
            phase_begin(act, 7)
            act.wait_ge(sig("mix_out"), 80)
            hi_slab(act, S["out0"][0], 0)
            with act.Fori(0, 4) as i:
                for j in range(4):
                    act.wait_ge(sig(f"mix_in{j}"), 16 * i + 16)
                    nc.scalar.activation(Mh[:, ds(4 * i + j, 1), :], mst[j][:, :].unsqueeze(1), ACT.Copy).then_inc(sig("mix_hi"), 1)
            act_stage(act, "out0", None)
            phase_end(act, "act")
            phase_begin(act, 8)
            act_norm(act, 1, T, 1)
            phase_end(act, "act")
            phase_begin(act, 9)
            act_ffn(act, 0, T)
            phase_end(act, "act")
            phase_begin(act, 10)
            act_norm(act, 2, T, 2)
            phase_end(act, "act")
            phase_begin(act, 11)
            act_qkv1(act)
            phase_end(act, "act")
            phase_begin(act, 12)
            for e in (0, 1):
                act.wait_ge(sig(f"lstore{e}"), 16 * 13)
            for k in range(6):
                w = LAT if k < 4 else T
                if k >= 2:
                    act.wait_ge(sig("la_ss"), k - 1)
                nc.scalar.activation(lato[k % 2][:, 0:w], latr[:, k, 0:w], ACT.Square).then_inc(sig("la_sq"), 1)
            act.wait_ge(sig("la_rec"), 4)
            nc.scalar.activation(latn[:, 0, 0:LAT], latn[:, 0, 0:LAT], ACT.Sqrt).then_inc(sig("la_root"), 1)
            nc.scalar.activation(latn[:, 1, :], latn[:, 1, :], ACT.Sqrt).then_inc(sig("la_root"), 1)
            for k in range(6):
                w = LAT if k < 4 else T
                act.wait_ge(sig("la_n"), k + 1)
                nc.scalar.activation(Hh[:, k, 0:w], latr[:, k, 0:w], ACT.Copy).then_inc(sig("la_hi"), 1)
            act_copy_stage(act, "uq1", LAT, 24, lambda i, jj, cc: scr_chunk(4 * i + 16 + 2 * jj + cc, LAT))
            act_copy_stage(act, "uk1", T, 36, lambda i, jj, cc: scr_chunk(4 * i + 28 + 2 * jj + cc, T))
            act_copy_stage(act, "uv1", T, 44, lambda i, jj, cc: v_block(1, i, jj, cc), prefetch=False)
            phase_end(act, "act")
            phase_begin(act, 13)
            act_units(act)
            phase_end(act, "act")
            phase_begin(act, 14)
            act_attention(act)
            phase_end(act, "act")
            phase_begin(act, 15)
            hi_slab(act, S["out1"][0], 0)
            for k in range(8):
                if k >= 2:
                    act.wait_ge(sig("an_ss"), past("an_ss") + k - 1)
                nc.scalar.activation(asq[k % 2][:, :], att[:, k, :], ACT.Square).then_inc(sig("an_sq"), 1)
                act.wait_ge(sig("an_rec"), past("an_rec") + 2 * k + 2)
                nc.scalar.activation(ars[k % 2][:, :], ars[k % 2][:, :], ACT.Sqrt).then_inc(sig("an_root"), 1)
            for k in range(16):
                if k < 8:
                    act.wait_ge(sig("an_n"), past("an_n") + k + 1)
                nc.scalar.activation(Ah[:, k, :], att[:, k, :], ACT.Copy).then_inc(sig("an_hi"), 1)
            act_stage(act, "out1", None)
            phase_end(act, "act")
            phase_begin(act, 16)
            act_norm(act, 3, LAT, 3)
            phase_end(act, "act")
            phase_begin(act, 17)
            act_ffn(act, 1, LAT)
            phase_end(act, "act")
            phase_begin(act, 18)
            for u in range(1, 8, 2):
                act.wait_ge(sig("yt_done"), u + 1)
                nc.scalar.activation(Y[:, u // 2, 512:1024], ps[:, u, :], ACT.Copy).then_inc(sig("y_odd"), 1)

        def copy_and_store(act, i, use, chunk, count, cc, w, dst):
            act.wait_ge(sig("gemm_done"), 4 * i + chunk + cc + 1)
            act.wait_ge(sig(f"lstore{cc}"), 32 * i + 16 * count + 16)
            nc.scalar.activation(lato[cc][:, 0:w], pairbank(cc, w), ACT.Copy)\
                .then_inc(sig(f"gemm_evac{cc}"), 1)
            act.wait_ge(sig(f"gemm_evac{cc}"), 2 * i + use + 2)
            src = lato[cc][:, 0:T].rearrange("p (t n) -> p t n", t=3) if dst.shape[1] == 3 else lato[cc][:, 0:w].unsqueeze(1)
            act.dma_start(dst, src).then_inc(sig(f"lstore{cc}"), 16)

        def act_copy_stage(act, name, w, count0, dst, prefetch=True):
            def evac(i, jj, u0):
                for cc in range(2):
                    copy_and_store(act, i, u0 + jj, S[name][3] + 2 * jj, count0 // 2 + jj, cc, w, dst(i, jj, cc))
            act_stage(act, name, evac, prefetch)

        def scr_chunk(chunk, w):
            return scr_p[:, ds(chunk, 1), 0:w]

        def v_block(x, i, jj, cc):
            return vscr[x].rearrange("(t p) n -> p t n", p=P)[:, 3 * cc:3 * cc + 3, ds(512 * i + 256 * jj, 256)]

        def act_qkv1(act):
            n0, ns, u0, c0 = S["qk1"]
            for part, w in ((0, LAT), (1, T)):
                def body(i, last):
                    for jj in range(2):
                        hi_slab(act, n0 + 4 * part + jj + 1, i, before=4 * i + c0 + 8 * part + 2 * jj)
                        for cc in range(2):
                            copy_and_store(act, i, u0 + 4 * part + jj, c0 + 8 * part + 2 * jj, 4 * part + jj, cc, w,
                                           scr_chunk(4 * i + 8 * part + 2 * jj + cc, w))
                loop(act, 2, body)
            act_copy_stage(act, "dv1", T, 16, lambda i, jj, cc: v_block(0, i, jj, cc))
            n0, ns, u0, c0 = S["lat1"]
            for jj in range(4):
                hi_slab(act, n0 + jj + 1, 0, before=c0 + 2 * jj)
                w = LAT if jj < 2 else T
                for cc in range(2 if jj < 3 else 1):
                    act.wait_ge(sig("gemm_done"), c0 + 2 * jj + cc + 1)
                    ins = nc.scalar.activation(latr[:, 2 * jj + cc, 0:w], pairbank(cc, w), ACT.Copy)
                    ins.then_inc(sig(f"gemm_evac{cc}"), 1)
            act.sem_inc(sig("gemm_evac1"), 1)
            act.wait_ge(sig("gemm_evac0"), u0 + 5)
            act.dma_start(scr_chunk(36, T), latr[:, 6:7, :]).then_inc(sig("kr_stored"), 16)

        def pool_stage(pool, name, prefetch=True):
            n0, ns, _, c0 = S[name]

            def body(i, last):
                for jj in range(2):
                    if not (last and jj == 1 and not prefetch):
                        lo_slab(pool, n0 + jj + 1, i)
            loop(pool, ns // 2, body)

        def pool_norm(pool, r, w):
            pool.wait_ge(sig("rstd_done"), r + 1)
            for k in range(KD):
                if 8 * r + k >= 2:
                    pool.wait_ge(sig("mod_done"), 8 * r + k - 1)
                nc.gpsimd.tensor_tensor(nrm[k % 2][:, 0:w], xT[:, k, 0:w], rstd[:, 0:w], ALU.mult).then_inc(sig("nrm_done"), 1)

        def pool_deltanet(pool, g):
            for x, src in ((0, dq), (1, dk)):
                pool.wait_ge(sig(f"ld_{'dq' if x == 0 else 'dk'}"), 16 * g + 16)
                flat = TTs[:, :, :, :, :].rearrange("p c d h n -> p (c d h n)")
                sf = src[:, :, :].rearrange("p h t -> p (h t)")
                nc.gpsimd.tensor_tensor(flat[:, x * 3072:(x + 1) * 3072], sf, sf, ALU.mult).then_inc(sig("dn_sq"), 1)
            if True:
                pool.wait_ge(sig("cum_exp"), 3)
                for j in range(6):
                    src = bet[:, :, :] if j == 5 else gcol[:, j, :, 0:16]
                    nc.gpsimd.tensor_copy(dgg[j][:, :, :, :],
                                          src.rearrange("p c (d x) -> p d c x", d=2)[:, :, :, ds(4 * g, 4)]).then_inc(sig("dn_gg"), 1)
            pool.wait_ge(sig("dn_gg"), 6 * g + 6)
            for q, c in enumerate(INTRA):
                for d in range(2):
                    pool.wait_ge(sig("dn_e"), 12 * g + 2 * q + d + 1)
                    nc.gpsimd.tensor_tensor(EB[d][:, :, :], Ed[d][:, :, :],
                                            dgg[5][:, d, c, :].unsqueeze(2).broadcast_to([P, 4, P]), ALU.mult)\
                        .then_inc(sig("dn_eb"), 1)
                for l in range(LEVELS):
                    for d in range(2):
                        if l == 0:
                            pool.wait_ge(sig("dn_at"), 12 * g + 2 * q + d + 1)
                        if l >= 2 or q:
                            back = 84 * g + 14 * q + 2 * (l - 2) + d + 1
                            pool.wait_ge(sig("dn_x"), back)
                        if l == 2:
                            pool.wait_ge(sig("dn_tt0"), 12 * g + 2 * q + d + 1)
                        nc.gpsimd.tensor_tensor(Am[d][l % 2][:, :, :], AT[d][:, :, :],
                                                level(d, l).unsqueeze(1).broadcast_to([P, 4, P]), ALU.mult)\
                            .then_inc(sig("dn_as"), 1)
                    if l == 0:
                        for d in range(2):
                            pool.wait_ge(sig("dn_as"), 84 * g + 14 * q + d + 1)
                            nc.gpsimd.tensor_tensor(TTs[:, c, d, :, :], ident.unsqueeze(1).broadcast_to([P, 4, P]),
                                                    Am[d][0][:, :, :], ALU.subtract).then_inc(sig("dn_tt0"), 1)
            for k in range(NT):
                for d in range(2):
                    c = ORDER[d][k]
                    if 0 < k < NT - 1:
                        pool.wait_ge(sig("rec_ks"), 10 * g + 2 * (k - 1) + d + 1)
                        pool.wait_ge(sig("rec_qs"), 10 * g + 2 * (k - 1) + d + 1)
                        pool.wait_ge(sig("rec_s"), 10 * g + 2 * (k - 1) + d + 1)
                        nc.gpsimd.tensor_tensor(Sst[d][:, :, :], Sst[d][:, :, :],
                                                dgg[4][:, d, c, :].unsqueeze(2).broadcast_to([P, 4, P]), ALU.mult)\
                            .then_inc(sig("rec_sd"), 1)
                for d in range(2):
                    c = ORDER[d][k]
                    if k < NT - 1:
                        pool.wait_ge(sig("rec_vn"), 12 * g + 2 * k + d + 1)
                        if k:
                            pool.wait_ge(sig("rec_su"), 10 * g + 2 * (k - 1) + d + 1)
                        nc.gpsimd.tensor_tensor(vs[d][:, :, :], vn[d][:, :, :],
                                                dgg[3][:, d, c, :].unsqueeze(2).broadcast_to([P, 4, P]), ALU.mult)\
                            .then_inc(sig("rec_vs"), 1)
            pool.wait_ge(sig("rec_o"), 12 * g + 12)
            pool.wait_ge(sig("rec_acc"), 6 * g + 6)
            flat = dk[:, :, :].rearrange("p h t -> p (h t)")
            of = dv[:, :, :].rearrange("p h t -> p (h t)")
            nc.gpsimd.tensor_tensor(flat, of, of, ALU.mult).then_inc(sig("dn_osq"), 1)

        def pool_ssd(pool, g):
            pool.wait_ge(sig("cum_exp"), 3)
            for j in range(6):
                src = dts[:, :, :] if j == 5 else gcol[:, j, :, 16:48]
                nc.gpsimd.tensor_copy(sgg[j][:, :, :, :],
                                      src.rearrange("p c (d x) -> p d c x", d=2)[:, :, :, ds(8 * g, 8)]).then_inc(sig("sd_gg"), 1)
            pool.wait_ge(sig("sd_gg"), past("sd_gg") + 6 * g + 6)
            for q, c in enumerate(INTRA):
                pool.wait_ge(sig("sd_tok"), past("sd_tok") + 18 * g + 3 * q + 3)
                for d in range(2):
                    nc.gpsimd.tensor_tensor(xdt[:, d, c, :].rearrange("p (h n) -> p h n", h=8),
                                            xtok[:, c, :].rearrange("p (h n) -> p h n", h=8),
                                            sgg[5][:, d, c, :].unsqueeze(2).broadcast_to([P, 8, 64]), ALU.mult)\
                        .then_inc(sig("sd_xdt"), 1)
                for f in range(2):
                    pool.wait_ge(sig("sd_e"), past("sd_e") + 24 * g + 4 * q + 2 + f + 1)
                    nc.gpsimd.tensor_tensor(Es[1][f][:, :, :], Es[1][f][:, :, :],
                                            bcs[:, :].unsqueeze(1).broadcast_to([P, 4, P]), ALU.mult).then_inc(sig("sd_m1"), 1)
            for k in range(NT - 1):
                for d in range(2):
                    c = ORDER[d][k]
                    if k:
                        pool.wait_ge(sig("ss_su"), past("ss_su") + 10 * g + 2 * (k - 1) + d + 1)
                    nc.gpsimd.tensor_tensor(sxs[d][:, :].rearrange("p (h n) -> p h n", h=8),
                                            xdt[:, d, c, :].rearrange("p (h n) -> p h n", h=8),
                                            sgg[3][:, d, c, :].unsqueeze(2).broadcast_to([P, 8, 64]), ALU.mult)\
                        .then_inc(sig("ss_x"), 1)

        def pool_units(pool):
            def unit(kind, u, i, j, r):
                _, _, _, w, _, _, rope = kind
                pool.wait_ge(sig(f"un_in{j}"), 16 * i + 16 * (u // 2) + 16)
                nc.gpsimd.tensor_tensor(qsq[j][:, 0:w], qn[j][:, 0:w], qn[j][:, 0:w], ALU.mult).then_inc(sig("un_sq"), 1)
                if rope:
                    pool.wait_ge(sig("un_n"), 2 * i + u + 1)
                    nc.gpsimd.tensor_tensor(qt[j][:, :], qn[j][:, 0:LAT], cos, ALU.mult).then_inc(sig("un_cos"), 1)
            units(pool, unit)

        def gpsimd_program(pool):
            pool.sem_inc(sig("slab_lo"), 2)
            nc.gpsimd.memset(rows[:, :, :], 0.0).then_inc(sig("rows_clear"), 1)
            pool.wait_ge(sig("rows_in"), 16 * len(rows_from()))
            r0 = V_SSDD % P
            nc.gpsimd.tensor_copy(rows[r0:r0 + 8, V_SSDD // P, :].rearrange("r (two n) -> r two n", two=2),
                                  drow[r0:r0 + 8, :].unsqueeze(2).broadcast_to([8, 2, 64])).then_inc(sig("rows_spread"), 1)
            phase_end(pool, "pool")
            phase_begin(pool, 1)
            pool_norm(pool, 0, T)
            lo_slab(pool, 0, 0, 512)
            phase_end(pool, "pool")
            phase_begin(pool, 2)
            for j in range(2):
                for e in (0, 514, 772):
                    nc.gpsimd.memset(ubuf[j][:, e:e + 2], 0.0).then_inc(sig("edges"), 1)
            lo_slab(pool, 1, 0)
            pool_stage(pool, "in0", prefetch=False)
            phase_end(pool, "pool")
            for base, part in ((3, pool_deltanet), (5, pool_ssd)):
                with pool.Fori(0, 2) as g:
                    phase_begin(pool, base + g)
                    part(pool, g)
                    phase_end(pool, "pool")
            phase_begin(pool, 7)
            lo_slab(pool, S["out0"][0], 0)
            with pool.Fori(0, 4) as i:
                for j in range(4):
                    pool.wait_ge(sig("mix_hi"), 4 * i + j + 1)
                    nc.gpsimd.tensor_tensor(Ml[:, ds(4 * i + j, 1), :], mst[j][:, :].unsqueeze(1),
                                            Mh[:, ds(4 * i + j, 1), :].bitcast(f32), ALU.subtract).then_inc(sig("mix_lo"), 1)
            pool_stage(pool, "out0")
            phase_end(pool, "pool")
            phase_begin(pool, 8)
            pool_norm(pool, 1, T)
            phase_end(pool, "pool")
            phase_begin(pool, 9)
            for grp in range(3):
                pool_stage(pool, f"fi0{grp}")
                pool_stage(pool, f"fo0{grp}")
            phase_end(pool, "pool")
            phase_begin(pool, 10)
            pool_norm(pool, 2, T)
            phase_end(pool, "pool")
            phase_begin(pool, 11)
            for name in ("qk1", "dv1", "lat1"):
                pool_stage(pool, name)
            phase_end(pool, "pool")
            phase_begin(pool, 12)
            pool_stage(pool, "uq1")
            pool_stage(pool, "uk1")
            pool_stage(pool, "uv1", prefetch=False)
            phase_end(pool, "pool")
            phase_begin(pool, 13)
            pool_units(pool)
            phase_end(pool, "pool")
            phase_begin(pool, 14)
            phase_end(pool, "pool")
            phase_begin(pool, 15)
            lo_slab(pool, S["out1"][0], 0)
            for k in range(16):
                pool.wait_ge(sig("an_hi"), past("an_hi") + k + 1)
                nc.gpsimd.tensor_tensor(Al[:, k, :], att[:, k, :], Ah[:, k, :].bitcast(f32), ALU.subtract).then_inc(sig("an_lo"), 1)
            pool_stage(pool, "out1")
            phase_end(pool, "pool")
            phase_begin(pool, 16)
            pool_norm(pool, 3, LAT)
            phase_end(pool, "pool")
            phase_begin(pool, 17)
            for grp in range(3):
                pool_stage(pool, f"fi1{grp}")
                pool_stage(pool, f"fo1{grp}", prefetch=(grp < 2))
            phase_end(pool, "pool")

        def dve_norm(dve, r, w, layer, part, gain):
            for x, mod in enumerate((modl, modc)):
                nc.vector.scalar_tensor_tensor(amod[:, x, :], mod[:, 48 * layer + 8 * (part + 1):48 * layer + 8 * (part + 2)],
                                               1.0, vec[:, gain:gain + 8], ALU.add, ALU.mult).then_inc(sig("amod_done"), 1)
            dve.wait_ge(sig("sq_used"), 8 * r + 8)
            if w > 512:
                dve.wait_ge(sig("sq_used2"), 8 * r + 8)
            nc.vector.tensor_scalar(rstd[:, 0:w], banks(6, 2, w), 1.0 / D, EPS, ALU.mult, ALU.add).then_inc(sig("ms_done"), 1)
            dve.wait_ge(sig("ms_done"), r + 1)
            nc.vector.reciprocal(rstd[:, 0:w], rstd[:, 0:w]).then_inc(sig("rec_done"), 1)
            dve.wait_ge(sig("amod_done"), 2 * r + 2)

            def low(k):
                dve.wait_ge(sig("hi_done"), 8 * r + k + 1)
                nc.vector.tensor_tensor(Hl[:, k, 0:w], mdl[k % 2][:, 0:w], Hh[:, k, 0:w].bitcast(f32), ALU.subtract)\
                    .then_inc(sig("lo_done"), 1)
            for k in range(KD):
                if k >= 2:
                    low(k - 2)
                    dve.wait_ge(sig("lo_done"), 8 * r + k - 1)
                dve.wait_ge(sig("nrm_done"), 8 * r + k + 1)
                for x, (t0, t1, mod) in enumerate(((0, LAT, modl), (LAT, w, modc))):
                    if t1 > t0:
                        c = 48 * layer + 8 * part + k
                        ins = nc.vector.tensor_scalar(mdl[k % 2][:, t0:t1], nrm[k % 2][:, t0:t1], amod[:, x, k:k + 1],
                                                      mod[:, c:c + 1], ALU.mult, ALU.add)
                ins.then_inc(sig("mod_done"), 1)
            low(6)
            low(7)

        def dve_mod(dve, it):
            dve.wait_ge(sig("ada_used"), 3 * it + 3)
            src = ps[:, 4, 0:12].rearrange("p (c s) -> p c s", s=2)
            nc.vector.tensor_tensor(modl[:, ds(6 * it, 6)], src[:, :, 0], vec[:, ds(6 * it, 6)], ALU.add)
            nc.vector.tensor_tensor(modc[:, ds(6 * it, 6)], src[:, :, 1], vec[:, ds(6 * it, 6)], ALU.add)\
                .then_inc(sig("mod_evac"), 1)

        def dve_gates(dve):
            link = Link(dve, "gate_step")
            dve.wait_ge(sig("gemm_done"), 1)
            link(nc.vector.tensor_copy(gts[:, :, :], ps[:, 5, 0:NT * 64].rearrange("p (c n) -> p c n", n=64)))
            x, ax = spw[0], spw[1]
            link(nc.vector.tensor_tensor(x[:, :, :], gts[:, :, 16:64], gbias[:, :].unsqueeze(1).broadcast_to([P, NT, 48]), ALU.add))
            link(nc.vector.scalar_tensor_tensor(ax[:, :, :].rearrange("p c n -> p (c n)"), x[:, :, :].rearrange("p c n -> p (c n)"),
                                                -1.0, x[:, :, :].rearrange("p c n -> p (c n)"), ALU.mult, ALU.min))
            dve.wait_ge(sig("gate_exp"), 4)
            f = [t[:, :, :].rearrange("p c n -> p (c n)") for t in spw]
            link(nc.vector.tensor_scalar(f[2], f[1], 2.0, None, ALU.add))
            link(nc.vector.reciprocal(f[3], f[2]))
            link(nc.vector.tensor_tensor(f[2], f[1], f[3], ALU.mult))
            link(nc.vector.tensor_tensor(f[3], f[2], f[2], ALU.mult))
            link(nc.vector.tensor_scalar(f[4], f[3], 1.0 / 17, None, ALU.mult))
            for m in (15, 13, 11, 9, 7, 5, 3):
                link(nc.vector.scalar_tensor_tensor(f[4], f[4], 1.0 / m, f[3], ALU.add, ALU.mult))
            link(nc.vector.scalar_tensor_tensor(f[4], f[4], 1.0, f[2], ALU.add, ALU.mult))
            link(nc.vector.tensor_scalar(f[5], f[0], 0.0, None, ALU.max))
            link(nc.vector.scalar_tensor_tensor(f[5], f[4], 2.0, f[5], ALU.mult, ALU.add))
            link(nc.vector.tensor_copy(dts[:, :, :], spw[5][:, :, 16:48]))
            link(nc.vector.tensor_tensor(gcol[:, 1, :, :], spw[5][:, :, :], alog[:, :].unsqueeze(1).broadcast_to([P, NT, 48]), ALU.mult))
            link(nc.vector.tensor_scalar(gcol[:, 0, :, :], gcol[:, 1, :, :], -1.0, None, ALU.mult))
            link(nc.vector.tensor_scalar(bet[:, :, :], bet[:, :, :], 1.0, None, ALU.add))
            link(nc.vector.reciprocal(bet[:, :, :], bet[:, :, :]))
            link(nc.vector.tensor_tensor(lam[:, 4:5], lam[:, 2:3], lam[:, 3:4], ALU.subtract))
            link(nc.vector.tensor_scalar(lam[:, 5:6], lam[:, 4:5], LAMBDA_INIT, -1.0, ALU.add, ALU.mult))
            link(nc.vector.tensor_scalar(lam[:, 6:7], vec[:, V_DASUB:V_DASUB + 1], 1.0 - LAMBDA_INIT, None, ALU.mult))

        def dve_conv(dve, i):
            for r in range(4):
                m, cc = 4 * i + r, r % 2
                dve.wait_ge(sig(f"gemm_evac{cc}"), 2 * i + r // 2 + 2)
                dve.wait_ge(sig("silu_done"), 4 * i + r + 1)
                for k in range(CONV_K):
                    col = 256 + P * (k // 3) + 36 * (k % 3)
                    w = vec[:, ds(col + m, 1)]
                    if k == 0:
                        ins = nc.vector.tensor_scalar(ybuf[cc][:, 0:770], ubuf[cc][:, 0:770], w, None, ALU.mult)
                    else:
                        dve.wait_ge(sig("conv_step"), 20 * i + 5 * r + k + 10)
                        ins = nc.vector.scalar_tensor_tensor(ybuf[cc][:, 0:770], ubuf[cc][:, k:k + 770], w, ybuf[cc][:, 0:770],
                                                             ALU.mult, ALU.add)
                    ins.then_inc(sig("conv_step"), 1)

        def dve_deltanet(dve, g):
            for x, src in ((0, dq), (1, dk)):
                flat = ATs[:, :, :, :, :].rearrange("p c d h n -> p (c d h n)")[:, x * 3072:(x + 1) * 3072]
                dve.wait_ge(sig("dn_ss"), 2 * g + x + 1)
                nc.vector.tensor_scalar(flat, banks(0, 6, 3072), EPS, None, ALU.add).then_inc(sig("dn_rec"), 1)
                dve.wait_ge(sig("dn_rec"), 4 * g + 2 * x + 1)
                nc.vector.reciprocal(flat, flat).then_inc(sig("dn_rec"), 1)
                dve.wait_ge(sig("dn_root"), 2 * g + x + 1)
                sf = src[:, :, :].rearrange("p h t -> p (h t)")
                nc.vector.tensor_tensor(sf, sf, flat, ALU.mult).then_inc(sig("dn_unit"), 1)
            dve.wait_ge(sig("dn_gg"), 6 * g + 6)
            dve.wait_ge(sig("dn_unit"), 2 * g + 2)
            for q, c in enumerate(INTRA):
                dve.wait_ge(sig("dn_kk"), 6 * g + q + 1)
                for d in range(2):
                    dve.wait_ge(sig("dn_d"), 12 * g + 2 * q + d + 1)
                    nc.vector.scalar_tensor_tensor(Ed[d][:, :, :], ps[:, 2 + d, :].rearrange("p (h n) -> p h n", h=4), 0.0,
                                                   neg[d].unsqueeze(1).broadcast_to([P, 4, P]), ALU.min, ALU.add)\
                        .then_inc(sig("dn_arg"), 1)
                for d in range(2):
                    dve.wait_ge(sig("dn_e"), 12 * g + 2 * q + d + 1)
                    nc.vector.tensor_tensor(ATs[:, c, d, :, :], ps[:, 1, :].rearrange("p (h n) -> p h n", h=4), Ed[d][:, :, :], ALU.mult)
                    dve.wait_ge(sig("dn_eb"), 12 * g + 2 * q + d + 1)
                    if q:
                        dve.wait_ge(sig("dn_as"), 84 * g + 14 * q - 1 + d)
                    nc.vector.tensor_tensor(AT[d][:, :, :], ps[:, 0, :].rearrange("p (h n) -> p h n", h=4), EB[d][:, :, :], ALU.mult)\
                        .then_inc(sig("dn_at"), 1)
                for d in range(2):
                    dve.wait_ge(sig("dn_x"), 84 * g + 14 * q + d + 1)
                    nc.vector.tensor_tensor(Tm[d][:, :, :], ident.unsqueeze(1).broadcast_to([P, 4, P]),
                                            ps[:, 4 + d, :].rearrange("p (h n) -> p h n", h=4), ALU.subtract).then_inc(sig("dn_t"), 1)
                for l in range(1, LEVELS):
                    s = 1 << l
                    for d in range(2):
                        if l < LEVELS - 1:
                            dve.wait_ge(sig("dn_tb"), 60 * g + 10 * q + 2 * (l - 1) + d + 1)
                            dve.wait_ge(sig("dn_t"), 72 * g + 12 * q + 2 * (l - 1) + d + 1)
                            v = sets(Tm[d][:, :, :].rearrange("p h n -> p (h n)"), l, d)
                            nc.vector.tensor_tensor(v, v, ps[:, 6 + d, 0:256].rearrange("p (n s) -> p n s", s=s), ALU.subtract)\
                                .then_inc(sig("dn_t"), 1)
                        dve.wait_ge(sig("dn_ttb"), 72 * g + 12 * q + 2 * (l - 1) + d + 1)
                        if l > 1:
                            dve.wait_ge(sig("dn_tt"), 72 * g + 12 * q + 2 * (l - 2) + d + 1)
                        v = sets(TTs[:, c, d, :, :].rearrange("p h n -> p (h n)"), l, 1 - d)
                        nc.vector.tensor_tensor(v, v, ps[:, 2 + d, 0:256].rearrange("p (n s) -> p n s", s=s), ALU.subtract)\
                            .then_inc(sig("dn_tt"), 1)
            oacc = dv[:, :, :].rearrange("p h t -> p (h t)").rearrange("p (c h n) -> p c h n", c=NT, h=4)

            def bc(j, d, c):
                return dgg[j][:, d, c, :].unsqueeze(2).broadcast_to([P, 4, P])

            def bank(b):
                return ps[:, b, :].rearrange("p (h n) -> p h n", h=4)
            seen = set()
            dve.wait_ge(sig("dn_kv"), 12 * g + 12)
            for k in range(NT):
                cs = [ORDER[d][k] for d in range(2)]
                for d in range(2):
                    c = cs[d]
                    if k:
                        dve.wait_ge(sig("rec_ks"), 10 * g + 2 * (k - 1) + d + 1)
                        nc.vector.tensor_tensor(rr[d][:, :, :], bank(d), bc(2, d, c), ALU.mult).then_inc(sig("rec_m"), 1)
                        dve.wait_ge(sig("rec_m"), 10 * g + 2 * (k - 1) + d + 1)
                        nc.vector.tensor_tensor(rr[d][:, :, :], vtok[:, c, :].rearrange("p (h n) -> p h n", h=4), rr[d][:, :, :],
                                                ALU.subtract).then_inc(sig("rec_r"), 1)
                for d in range(2):
                    dve.wait_ge(sig("rec_v"), 12 * g + 2 * k + d + 1)
                    nc.vector.tensor_tensor(vn[d][:, :, :], bank(4 + d), bc(5, d, cs[d]), ALU.mult).then_inc(sig("rec_vn"), 1)
                for d in range(2):
                    if k:
                        dve.wait_ge(sig("rec_qs"), 10 * g + 2 * (k - 1) + d + 1)
                        nc.vector.tensor_tensor(to[d][:, :, :], bank(2 + d), bc(2, d, cs[d]), ALU.mult).then_inc(sig("rec_t"), 1)
                for d in range(2):
                    if k < NT - 1:
                        dve.wait_ge(sig("rec_su"), 10 * g + 2 * k + d + 1)
                        if k:
                            dve.wait_ge(sig("rec_sd"), 8 * g + 2 * (k - 1) + d + 1)
                            nc.vector.tensor_tensor(Sst[d][:, :, :], Sst[d][:, :, :], bank(6 + d), ALU.add).then_inc(sig("rec_s"), 1)
                        else:
                            nc.vector.tensor_copy(Sst[d][:, :, :], bank(6 + d)).then_inc(sig("rec_s"), 1)
                for d in range(2):
                    c = cs[d]
                    dve.wait_ge(sig("rec_ob"), 12 * g + 2 * k + d + 1)
                    if k:
                        dve.wait_ge(sig("rec_t"), 10 * g + 2 * (k - 1) + d + 1)
                        if c in seen:
                            nc.vector.tensor_tensor(to[d][:, :, :], to[d][:, :, :], bank(4 + d), ALU.add).then_inc(sig("rec_o"), 1)
                            dve.wait_ge(sig("rec_o"), 12 * g + 2 * k + d + 1)
                            nc.vector.tensor_tensor(oacc[:, c, :, :], oacc[:, c, :, :], to[d][:, :, :], ALU.add).then_inc(sig("rec_acc"), 1)
                        else:
                            nc.vector.tensor_tensor(oacc[:, c, :, :], to[d][:, :, :], bank(4 + d), ALU.add).then_inc(sig("rec_o"), 1)
                    else:
                        nc.vector.tensor_copy(oacc[:, c, :, :], bank(4 + d)).then_inc(sig("rec_o"), 1)
                    seen.add(c)
            dve.wait_ge(sig("dn_osq"), g + 1)
            nc.vector.tensor_reduce(drs[:, :, :], dk[:, :, :].rearrange("p h t -> p (h t)").rearrange("p (c h n) -> p c h n", c=NT, h=4),
                                    AX.X, ALU.add).then_inc(sig("dn_ored"), 1)
            dve.wait_ge(sig("dn_ored"), g + 1)
            nc.vector.tensor_scalar(drs[:, :, :], drs[:, :, :], 1.0 / P, EPS, ALU.mult, ALU.add).then_inc(sig("dn_orec"), 1)
            dve.wait_ge(sig("dn_orec"), 2 * g + 1)
            nc.vector.reciprocal(drs[:, :, :], drs[:, :, :]).then_inc(sig("dn_orec"), 1)
            dve.wait_ge(sig("dn_oroot"), g + 1)
            nc.vector.tensor_tensor(oacc, oacc, drs[:, :, :].unsqueeze(3).broadcast_to([P, NT, 4, P]), ALU.mult).then_inc(sig("dn_on"), 1)
            dve.wait_ge(sig("ld_dz"), 16 * g + 16)
            for c in range(NT):
                dve.wait_ge(sig("dn_ot"), 6 * g + c + 1)
                nc.vector.scalar_tensor_tensor(dq[:, :, c * P:(c + 1) * P], bank(4 + c % 2), vec[:, V_DNN:V_DNN + 1],
                                               dq[:, :, c * P:(c + 1) * P], ALU.mult, ALU.mult).then_inc(sig("dn_og"), 1)

        def dve_ssd(dve, g):
            dve.wait_ge(sig("sd_gg"), past("sd_gg") + 6 * g + 6)
            dve.wait_ge(sig("sd_in"), 64 * g + 64)
            for q, c in enumerate(INTRA):
                for d in range(2):
                    for f in range(2):
                        dve.wait_ge(sig("sd_d"), past("sd_d") + 24 * g + 4 * q + 2 * d + f + 1)
                        if q:
                            dve.wait_ge(sig("sd_yb"), past("sd_yb") + 6 * g + q)
                        nc.vector.scalar_tensor_tensor(Es[d][f][:, :, :], ps[:, 3 + 2 * d + f, :].rearrange("p (h n) -> p h n", h=4), 0.0,
                                                       neg[d].unsqueeze(1).broadcast_to([P, 4, P]), ALU.min, ALU.add)\
                            .then_inc(sig("sd_arg"), 1)
                dve.wait_ge(sig("sd_tok"), past("sd_tok") + 18 * g + 3 * q + 3)
                for f in range(2):
                    dve.wait_ge(sig("sd_e"), past("sd_e") + 24 * g + 4 * q + f + 1)
                    nc.vector.tensor_tensor(Es[0][f][:, :, :], Es[0][f][:, :, :], bcs[:, :].unsqueeze(1).broadcast_to([P, 4, P]),
                                            ALU.mult).then_inc(sig("sd_m0"), 1)
            dve.wait_ge(sig("sd_y"), past("sd_y") + 6 * g + 6)
            acc = 0
            for k in range(NT):
                for d in range(2):
                    c = ORDER[d][k]

                    def e(v):
                        return v.rearrange("p (h n) -> p h n", h=8)

                    def bc(j):
                        return sgg[j][:, d, c, :].unsqueeze(2).broadcast_to([P, 8, 64])
                    if k:
                        dve.wait_ge(sig("ss_ch"), past("ss_ch") + 10 * g + 2 * (k - 1) + d + 1)
                        nc.vector.tensor_tensor(e(sty[d][:, :]), e(ps[:, d, :]), bc(2), ALU.mult).then_inc(sig("ss_t"), 1)
                    if k < NT - 1:
                        if k:
                            nc.vector.tensor_tensor(e(hst[d][:, :]), e(hst[d][:, :]), bc(4), ALU.mult).then_inc(sig("ss_sd"), 1)
                            dve.wait_ge(sig("ss_sd"), past("ss_sd") + 8 * g + 2 * (k - 1) + d + 1)
                        dve.wait_ge(sig("ss_su"), past("ss_su") + 10 * g + 2 * k + d + 1)
                        if k:
                            nc.vector.tensor_tensor(hst[d][:, :], hst[d][:, :], ps[:, 2 + d, :], ALU.add).then_inc(sig("ss_s"), 1)
                        else:
                            nc.vector.tensor_copy(hst[d][:, :], ps[:, 2 + d, :]).then_inc(sig("ss_s"), 1)
                    if k:
                        dve.wait_ge(sig("ss_t"), past("ss_t") + 10 * g + 2 * (k - 1) + d + 1)
                        if acc:
                            dve.wait_ge(sig("ss_acc"), past("ss_acc") + 10 * g + acc)
                        nc.vector.tensor_tensor(yacc[:, c, :], yacc[:, c, :], sty[d][:, :], ALU.add).then_inc(sig("ss_acc"), 1)
                        acc += 1
            for h in range(4):
                nc.vector.tensor_scalar(sx[:, h, :], sx[:, h, :], vec[:, ds(V_SSDD + 4 * g + h, 1)], None, ALU.mult).then_inc(sig("ss_dx"), 1)
            dve.wait_ge(sig("ss_dx"), 4 * g + 4)
            for c in range(NT):
                dve.wait_ge(sig("ss_tt"), past("ss_tt") + 6 * g + c + 1)
                v = sx[:, :, c * P:(c + 1) * P]
                nc.vector.tensor_tensor(v, v, ps[:, 4 + c % 2, :].rearrange("p (h n) -> p h n", h=4), ALU.add).then_inc(sig("ss_yt"), 1)
            dve.wait_ge(sig("ss_yt"), past("ss_yt") + 6 * g + 6)
            for h in range(4):
                nc.vector.tensor_tensor(sx[:, h, :], sx[:, h, :], sz[:, h, :], ALU.mult).then_inc(sig("ss_gated"), 1)
            dve.wait_ge(sig("ss_ssum"), past("ss_ssum") + 4 * g + 4)
            nc.vector.tensor_scalar(srs[:, :], banks(6, 2, T), 1.0 / 512, EPS, ALU.mult, ALU.add).then_inc(sig("ss_rec"), 1)
            dve.wait_ge(sig("ss_rec"), past("ss_rec") + 2 * g + 1)
            nc.vector.reciprocal(srs[:, :], srs[:, :]).then_inc(sig("ss_rec"), 1)
            dve.wait_ge(sig("ss_root"), past("ss_root") + g + 1)
            dve.wait_ge(sig("ss_gated"), 4 * g + 4)
            for h in range(4):
                nc.vector.scalar_tensor_tensor(sx[:, h, :], sx[:, h, :], vec[:, ds(V_SSDN + 4 * g + h, 1)], srs[:, :],
                                               ALU.mult, ALU.mult).then_inc(sig("ss_out"), 1)

        def residual(dve, use, pair, layer, part, k, w):
            dve.wait_ge(sig("gemm_done"), use)
            c = 48 * layer + 8 * part
            for t0, t1, mod in ((0, LAT, modl), (LAT, w, modc)):
                if t1 > t0:
                    x = xT[:, ds(k, 1), t0:t1].rearrange("p a t -> p (a t)")
                    ins = nc.vector.scalar_tensor_tensor(x, pairbank(pair, w)[:, t0:t1], mod[:, ds(k + c, 1)], x, ALU.mult, ALU.add)
            ins.then_inc(sig(f"gemm_evac{pair}"), 1)

        def dve_out(dve, name, layer, w):
            n0, ns, u0, c0 = S[name]
            with dve.Fori(0, 4) as i:
                for jj in range(2):
                    residual(dve, 2 * i + c0 + jj + 1, jj, layer, 2, 2 * i + jj, w)

        def dve_ffn(dve, layer, w):
            for grp, n in enumerate(GROUPS):
                first = 22 * layer + sum(GROUPS[:grp])
                n0, ns, u0, c0 = S[f"fi{layer}{grp}"]
                with dve.Fori(0, n // 2) as i:
                    for jj in range(2):
                        dve.wait_ge(sig("gemm_done"), 4 * i + c0 + 2 * jj + 2)
                        dve.wait_ge(sig("gemm_evac0"), 2 * i + u0 + jj + 2)
                        nc.vector.tensor_tensor(hdb[jj][:, 0:w], sgb[jj][:, 0:w], pairbank(1, w), ALU.mult)\
                            .then_inc(sig("gemm_evac1"), 1)
                        dve.wait_ge(sig("hid_hi"), 2 * i + first + jj + 1)
                        nc.vector.tensor_tensor(Gl[:, ds(2 * i + jj, 1), 0:w], hdb[jj][:, 0:w].unsqueeze(1),
                                                Gh[:, ds(2 * i + jj, 1), 0:w].bitcast(f32), ALU.subtract).then_inc(sig("hid_lo"), 1)
                n0, ns, u0, c0 = S[f"fo{layer}{grp}"]
                with dve.Fori(0, 2) as i:
                    for jj in range(2):
                        for cc in range(2):
                            residual(dve, 4 * i + c0 + 2 * jj + cc + 1, cc, layer, 5, 4 * i + 2 * jj + cc, w)

        def dve_units(dve):
            def unit(kind, u, i, j, r):
                _, u0, _, w, span, gain, rope = kind
                dve.wait_ge(sig("un_ss"), 2 * i + u + 1)
                nc.vector.tensor_scalar(qrs[j][:, 0:w], banks(2 * j, 2, w), 1.0 / span, EPS, ALU.mult, ALU.add).then_inc(sig("un_rec"), 1)
                dve.wait_ge(sig("un_rec"), 4 * i + 2 * u + 1)
                nc.vector.reciprocal(qrs[j][:, 0:w], qrs[j][:, 0:w]).then_inc(sig("un_rec"), 1)
                dve.wait_ge(sig("un_root"), 2 * i + u + 1)
                ins = nc.vector.scalar_tensor_tensor(qn[j][:, 0:w], qn[j][:, 0:w], vec[:, gain:gain + 1], qrs[j][:, 0:w],
                                                     ALU.mult, ALU.mult)
                ins.then_inc(sig("un_n"), 1)
                if rope:
                    step = 2 * i + r
                    dve.wait_ge(sig("un_rot"), step + 1)
                    nc.vector.tensor_tensor(qsq[j][:, 0:LAT], ps[:, 4 + j, :], sin, ALU.mult).then_inc(sig("un_sin"), 1)
                    dve.wait_ge(sig("un_sin"), step + 1)
                    dve.wait_ge(sig("un_cos"), step + 1)
                    nc.vector.tensor_tensor(qn[j][:, 0:LAT], qt[j][:, :], qsq[j][:, 0:LAT], ALU.add).then_inc(sig("un_done"), 1)
            units(dve, unit)

        def dve_attention(dve):
            U = attention_units()
            with dve.Fori(0, 4) as i:
                def maxima(u, da, hh, qt, pairs):
                    st = stat[u % 2]
                    for x, (p, use) in enumerate(pairs):
                        dve.wait_ge(sig(f"at_s{p}"), 12 * i + use + 1)
                        nc.vector.tensor_reduce(st[:, x:x + 1], pairbank(p, T), AX.X, ALU.max).then_inc(sig(f"at_x{p}"), 1)
                    for x, (p, use) in enumerate(pairs):
                        dve.wait_ge(sig(f"at_x{p}"), 12 * i + use + 1)
                        nc.vector.tensor_scalar(st[:, x:x + 1], st[:, x:x + 1], -(64 if da else 192) ** -0.5, None, ALU.mult)\
                            .then_inc(sig(f"at_m{p}"), 1)

                def weights(u, da, hh, qt, pairs):
                    st, n = stat[u % 2], len(pairs)
                    for p, use in pairs:
                        dve.wait_ge(sig(f"at_e{p}"), 12 * i + use + 2)
                    nc.vector.reciprocal(st[:, 4:4 + n], st[:, 2:2 + n]).then_inc(sig("at_r"), 1)
                    dve.wait_ge(sig("at_r"), past("at_r") + 16 * i + u + 1)
                    p0, p1 = prb[2 * (u % 2)], prb[2 * (u % 2) + 1]
                    ins = nc.vector.tensor_scalar(p0[:, :], p0[:, :], st[:, 4:5], None, ALU.mult)
                    if not da:
                        ins.then_inc(sig("at_p"), 1)
                        return
                    ins.then_inc(sig("at_w"), 1)
                    nc.vector.tensor_scalar(st[:, 5:6], st[:, 5:6], lam[:, 5:6], None, ALU.mult).then_inc(sig("at_w"), 1)
                    dve.wait_ge(sig("at_w"), past("at_w") + 16 * i + 2 * (4 * hh + qt) + 2)
                    nc.vector.scalar_tensor_tensor(p0[:, :], p1[:, :], st[:, 5:6], p0[:, :], ALU.mult, ALU.add).then_inc(sig("at_p"), 1)
                maxima(*U[0])
                for x in U:
                    if x[0] < 15:
                        maxima(*U[x[0] + 1])
                    weights(*x)

        def vector_program(dve):
            dve.sem_inc(sig("gemm_evac0"), 1)
            dve.sem_inc(sig("gemm_evac1"), 1)
            dve.sem_inc(sig("conv_step"), 10)
            dve.wait_ge(sig("rows_turned"), 1)
            nc.vector.tensor_copy(vec[:, :], ps[:, 7, :]).then_inc(sig("vec_ready"), 1)
            for u in range(0, 12, 2):
                dve.wait_ge(sig("xt_done"), u + 1)
                if u:
                    dve.wait_ge(sig("xt_evac"), u)
                t, hf = u // 2, u % 2
                nc.vector.tensor_copy(xT[:, 0:4, t * P:(t + 1) * P], ps[:, u % 6, :].rearrange("p (k n) -> p k n", k=4))\
                    .then_inc(sig("xt_evac"), 1)
            dve.wait_ge(sig("rows_in"), 16 * len(rows_from()))
            pair = lrow[:, :, :].rearrange("p (x two) n -> p x two n", two=2)
            nc.vector.tensor_tensor(pair[:, :, 0, :], pair[:, :, 0, :], pair[:, :, 1, :], ALU.mult).then_inc(sig("lam_step"), 1)
            dve.wait_ge(sig("lam_step"), 1)
            nc.vector.tensor_reduce(lam[:, 0:2], pair[:, :, 0, :], AX.X, ALU.add).then_inc(sig("lam_step"), 1)
            for it in range(3):
                dve_mod(dve, it)
            phase_end(dve, "dve")
            phase_begin(dve, 1)
            dve_norm(dve, 0, T, 0, 0, V_NMIX)
            phase_end(dve, "dve")
            phase_begin(dve, 2)
            dve_gates(dve)
            dve.wait_ge(sig("edges"), 6)
            with dve.Fori(0, 9) as i:
                dve_conv(dve, i)
                dve_mod(dve, i + 3)
            with dve.Fori(9, 13) as i:
                dve_mod(dve, i + 3)
            phase_end(dve, "dve")
            phase_begin(dve, 3)
            dve.wait_ge(sig("cum_sums"), 1)
            link = Link(dve, "cum_ready")

            def sums(b):
                return ps[:, b, 0:NT * 48].rearrange("p (c n) -> p c n", n=48)
            for b, c0, c1 in ((0, 0, 8), (0, 16, 32), (1, 8, 16), (1, 32, 48)):
                link(nc.vector.tensor_copy(gcol[:, 2, :, c0:c1], sums(b)[:, :, c0:c1]))
            link(nc.vector.tensor_tensor(gcol[:, 3, :, :], sums(2), gcol[:, 2, :, :], ALU.subtract))
            link(nc.vector.tensor_copy(gcol[:, 4, :, :], sums(2)))
            for base, part in ((3, dve_deltanet), (5, dve_ssd)):
                with dve.Fori(0, 2) as g:
                    phase_begin(dve, base + g)
                    part(dve, g)
                    phase_end(dve, "dve")
            phase_begin(dve, 7)
            dve_out(dve, "out0", 0, T)
            phase_end(dve, "dve")
            phase_begin(dve, 8)
            dve_norm(dve, 1, T, 0, 3, V_NFFN)
            phase_end(dve, "dve")
            phase_begin(dve, 9)
            dve_ffn(dve, 0, T)
            phase_end(dve, "dve")
            phase_begin(dve, 10)
            dve_norm(dve, 2, T, 1, 0, V_NMIX + 8)
            phase_end(dve, "dve")
            phase_begin(dve, 11)
            phase_end(dve, "dve")
            phase_begin(dve, 12)
            dve.wait_ge(sig("la_ss"), 6)
            nc.vector.tensor_scalar(latn[:, 0, 0:LAT], ps[:, 6, :], 1.0 / 512, EPS, ALU.mult, ALU.add).then_inc(sig("la_rec"), 1)
            nc.vector.tensor_scalar(latn[:, 1, :], banks(4, 2, T), 1.0 / 256, EPS, ALU.mult, ALU.add).then_inc(sig("la_rec"), 1)
            dve.wait_ge(sig("la_rec"), 2)
            nc.vector.reciprocal(latn[:, 0, 0:LAT], latn[:, 0, 0:LAT]).then_inc(sig("la_rec"), 1)
            nc.vector.reciprocal(latn[:, 1, :], latn[:, 1, :]).then_inc(sig("la_rec"), 1)
            dve.wait_ge(sig("la_root"), 2)
            for k in range(6):
                w, x = (LAT, 0) if k < 4 else (T, 1)
                nc.vector.scalar_tensor_tensor(latr[:, k, 0:w], latr[:, k, 0:w], vec[:, V_QA + k:V_QA + k + 1], latn[:, x, 0:w],
                                               ALU.mult, ALU.mult).then_inc(sig("la_n"), 1)
            for k in range(6):
                w = LAT if k < 4 else T
                dve.wait_ge(sig("la_hi"), k + 1)
                nc.vector.tensor_tensor(Hl[:, k, 0:w], latr[:, k, 0:w], Hh[:, k, 0:w].bitcast(f32), ALU.subtract).then_inc(sig("la_lo"), 1)
            phase_end(dve, "dve")
            phase_begin(dve, 13)
            dve_units(dve)
            phase_end(dve, "dve")
            phase_begin(dve, 14)
            dve_attention(dve)
            phase_end(dve, "dve")
            phase_begin(dve, 15)
            for k in range(8):
                dve.wait_ge(sig("an_ss"), past("an_ss") + k + 1)
                nc.vector.tensor_scalar(ars[k % 2][:, :], ps[:, 4 + k % 2, :], 1.0 / P, EPS, ALU.mult, ALU.add).then_inc(sig("an_rec"), 1)
                dve.wait_ge(sig("an_rec"), past("an_rec") + 2 * k + 1)
                nc.vector.reciprocal(ars[k % 2][:, :], ars[k % 2][:, :]).then_inc(sig("an_rec"), 1)
                dve.wait_ge(sig("an_root"), past("an_root") + k + 1)
                nc.vector.scalar_tensor_tensor(att[:, k, :], att[:, k, :], lam[:, 6:7], ars[k % 2][:, :], ALU.mult, ALU.mult)\
                    .then_inc(sig("an_n"), 1)
            dve_out(dve, "out1", 1, LAT)
            phase_end(dve, "dve")
            phase_begin(dve, 16)
            dve_norm(dve, 3, LAT, 1, 3, V_NFFN + 8)
            phase_end(dve, "dve")
            phase_begin(dve, 17)
            dve_ffn(dve, 1, LAT)
            phase_end(dve, "dve")
            phase_begin(dve, 18)
            for u in range(0, 8, 2):
                dve.wait_ge(sig("yt_done"), u + 1)
                nc.vector.tensor_copy(Y[:, u // 2, 0:512], ps[:, u, :]).then_inc(sig("y_even"), 1)

        def sp_stage(sp, name, src, k=KD, w=256, view=None):
            n0, ns, _, c0 = S[name]
            with sp.Fori(0, ns // 2) as i:
                for jj in range(2):
                    load_slab(sp, n0 + jj, i, src(i, jj), k, w, view)

        def rows_of(w, k):
            return w.rearrange("(k p) n -> p k n", p=P)

        def sp_ffn(sp, layer):
            w1 = a["ffn_w_in"][layer].rearrange("(k p) (u n) -> p k u n", p=P, u=2)
            w2 = a["ffn_w_out"][layer].rearrange("(k p) n -> p k n", p=P)
            for grp, n in enumerate(GROUPS):
                c0 = sum(GROUPS[:grp])
                sp_stage(sp, f"fi{layer}{grp}", lambda i, jj: w1[:, :, :, ds(256 * i + P * (c0 + jj), P)],
                         view=lambda t: t[:, 0:2048].rearrange("p (k u n) -> p k u n", k=KD, u=2))
                sp_stage(sp, f"fo{layer}{grp}", lambda i, jj: w2[:, c0:c0 + n, ds(512 * i + 256 * jj, 256)], k=n)

        def sync_program(sp):
            for e in (0, 1):
                sp.sem_inc(sig(f"store{e}"), 32)
                sp.sem_inc(sig(f"lstore{e}"), 16)
                sp.sem_inc(sig(f"ustore{e}"), 16)
            sp.sem_inc(sig("silu_done"), 2)
            sp.sem_inc(sig("at_tr"), 2)
            sp.sem_inc(sig("at_pv"), 3)
            sp.sem_inc(sig("mix_out"), 16)
            sp.dma_start(cst[:, :], a["consts"]).then_inc(sig("consts_in"), 16)
            sp.dma_start(X[:, 0:4, :], a["x"][0].rearrange("(t p) n -> p t n", p=P)).then_inc(sig("x_in"), 16)
            sp.dma_start(X[:, 4:6, :], a["ctx"][0].rearrange("(t p) n -> p t n", p=P)).then_inc(sig("x_in"), 16)
            adaw = [rows_of(a["ada_w"][layer], KD) for layer in range(2)]
            w0 = rows_of(a["ev_w_in"][0], KD)
            for it in range(3):
                for q in range(3):
                    if it:
                        sp.wait_ge(sig("ada_used"), 3 * it + q - 2)
                    n = 3 * it + q
                    sp.dma_start(ada[q][:, :, :], adaw[0][:, :, n * 256:(n + 1) * 256]).then_inc(sig(f"ada_in{q}"), 16)
            load_slab(sp, 0, 0, w0[:, :, EV_MAIN:EV_IN], KD, 64)
            n0 = S["in0"][0]
            for lo, n_it, layer in ((0, 5, 0), (5, 13, 1)):
                with sp.Fori(lo, n_it) as i:
                    for jj in range(2):
                        load_slab(sp, n0 + jj, i, w0[:, :, ds(512 * i + 256 * jj, 256)])
                        for q in ((0, 1), (2,))[jj]:
                            sp.wait_ge(sig("ada_used"), 3 * i + 9 + q - 2)
                            sp.dma_start(ada[q][:, :, :], adaw[layer][:, :, ds(768 * i + (2304 if layer == 0 else 2304 - 6144) + 256 * q, 256)])\
                                .then_inc(sig(f"ada_in{q}"), 16)
            wo0 = rows_of(a["ev_w_out"][0], 16)
            for jj in range(2):
                load_slab(sp, S["out0"][0] + jj, 0, wo0[:, :, jj * P:(jj + 1) * P], 16, P)
            with sp.Fori(0, 2) as g:
                phase_begin(sp, 3 + g)
                for e in (0, 1):
                    sp.wait_ge(sig(f"store{e}"), 32 * 27)
                sp.wait_ge(sig("mix_out"), 16 * g + 16)
                for t, off, name in ((dq, 0, "ld_dq"), (dk, 8, "ld_dk"), (dv, 16, "ld_dv")):
                    sp.dma_start(t[:, :, :], scr_p[:, ds(4 * g + off, 4), :]).then_inc(sig(name), 16)
                sp.wait_ge(sig("rec_qs"), 10 * g + 10)
                sp.dma_start(dq[:, :, :], scr_p[:, ds(4 * g + 36, 4), :]).then_inc(sig("ld_dz"), 16)
                sp.wait_ge(sig("dn_og"), 6 * g + 6)
                sp.dma_start(mix_p[:, ds(4 * g, 4), :], dq[:, :, :]).then_inc(sig("mix_out"), 16)
            with sp.Fori(0, 2) as g:
                phase_begin(sp, 5 + g)
                sp.wait_ge(sig("mix_out"), 16 * g + 48)
                sp.dma_start(sx[:, :, :], scr_p[:, ds(4 * g + 24, 4), :]).then_inc(sig("sd_in"), 16)
                sp.dma_start(sB[:, :], scr_p[:, ds(g + 32, 1), :].rearrange("p a t -> p (a t)")).then_inc(sig("sd_in"), 16)
                sp.dma_start(sC[:, :], scr_p[:, ds(g + 34, 1), :].rearrange("p a t -> p (a t)")).then_inc(sig("sd_in"), 16)
                sp.dma_start(sz[:, :, :], scr_p[:, ds(4 * g + 44, 4), :]).then_inc(sig("sd_in"), 16)
                sp.wait_ge(sig("ss_out"), 4 * g + 4)
                sp.dma_start(mix_p[:, ds(4 * g + 8, 4), :], sx[:, :, :]).then_inc(sig("mix_out"), 16)
            phase_begin(sp, 7)
            sp.wait_ge(sig("mix_out"), 80)
            for i in range(4):
                for j in range(4):
                    if i:
                        sp.wait_ge(sig("mix_lo"), 4 * (i - 1) + j + 1)
                    sp.dma_start(mst[j][:, :], mix_p[:, 4 * i + j, :]).then_inc(sig(f"mix_in{j}"), 16)
            with sp.Fori(1, 4) as i:
                for jj in range(2):
                    load_slab(sp, S["out0"][0] + jj, i, wo0[:, :, ds(256 * i + P * jj, P)], 16, P)
            sp_ffn(sp, 0)
            w1 = rows_of(a["od_w_in"][0], KD)
            sp_stage(sp, "qk1", lambda i, jj: w1[:, :, ds(512 * i + 256 * jj, 256)])
            sp_stage(sp, "dv1", lambda i, jj: w1[:, :, ds(512 * i + 256 * jj + 2048, 256)])
            n0 = S["lat1"][0]
            for jj in range(3):
                load_slab(sp, n0 + jj, 0, w1[:, :, 3072 + 256 * jj:3328 + 256 * jj])
            load_slab(sp, n0 + 3, 0, w1[:, :, 3840:3904].unsqueeze(2).broadcast_to([P, KD, 2, 64]),
                      view=lambda t: t[:, 0:1024].rearrange("p (k two n) -> p k two n", k=KD, two=2))
            wq = a["mla_w_uq"][0].rearrange("(k p) (h n) -> p k h n", p=P, h=8)
            n0 = S["uq1"][0]
            for s_ in range(4):
                load_slab(sp, n0 + s_, 0, wq[:, :, 2 * s_:2 * s_ + 2, 0:P],
                          view=lambda t: t[:, 0:1024].rearrange("p (k h n) -> p k h n", k=4, h=2), k=4)
            for s_ in range(2):
                load_slab(sp, n0 + 4 + s_, 0, wq[:, :, 4 * s_:4 * s_ + 4, P:192],
                          view=lambda t: t[:, 0:1024].rearrange("p (k h n) -> p k h n", k=4, h=4), k=4)
            wkv = a["mla_w_ukv"][0].rearrange("(k p) (h n) -> p k h n", p=P, h=8)
            for name, c0 in (("uk1", 0), ("uv1", P)):
                for s_ in range(4):
                    load_slab(sp, S[name][0] + s_, 0, wkv[:, :, 2 * s_:2 * s_ + 2, c0:c0 + P],
                              view=lambda t: t[:, 0:512].rearrange("p (k h n) -> p k h n", k=2, h=2), k=2)
            wo1 = rows_of(a["od_w_out"][0], 16)
            for jj in range(2):
                load_slab(sp, S["out1"][0] + jj, 0, wo1[:, :, jj * P:(jj + 1) * P], 16, P)
            phase_begin(sp, 13)
            for e in (0, 1):
                sp.wait_ge(sig(f"lstore{e}"), 16 * 27)
            sp.wait_ge(sig("kr_stored"), 16)
            sp_units(sp)
            phase_begin(sp, 14)
            sp.wait_ge(sig("ustore0"), 16 * 20)
            sp.wait_ge(sig("ustore1"), 16 * 19)
            sp.dma_start(mkr[0:64, :], scr["chunks"][36, 0:64, :]).then_inc(sig("mkr_in"), 16)
            rows64 = scr["chunks"].rearrange("m p t -> (m p) t")
            with sp.Fori(0, 4) as i:
                for hh in range(2):
                    for da in (True, False):
                        hu = 2 * hh + (0 if da else 1)
                        sp.wait_ge(sig("at_pv"), 4 * i + max(hu - 1, 0) + 1)
                        name = f"at_in{hh}{0 if da else 1}"
                        if da:
                            parts = ((aq, 0, LAT), (ak, 8, T))
                            vx, vt = 0, av
                        else:
                            parts = ((mq, 16, LAT), (mk, 28, T))
                            vx, vt = 1, mv
                        for t_, off, w in parts:
                            sp.dma_start(t_[hh][:, 0:w], scr_p[:, ds(2 * i + hh + off, 1), 0:w].rearrange("p a t -> p (a t)"))\
                                .then_inc(sig(name), 16)
                        if not da:
                            sp.dma_start(mr[hh][0:64, :], rows64[ds(24 * P + 128 * i + 64 * hh, 64), 0:LAT]).then_inc(sig(name), 16)
                        sp.dma_start(vt[hh][:, :].rearrange("p (t n) -> p t n", n=P),
                                     vscr[vx].rearrange("(t p) n -> p t n", p=P)[:, :, ds(256 * i + P * hh, P)]).then_inc(sig(name), 16)
            with sp.Fori(1, 4) as i:
                for jj in range(2):
                    load_slab(sp, S["out1"][0] + jj, i, wo1[:, :, ds(256 * i + P * jj, P)], 16, P)
            sp_ffn(sp, 1)
            sp.wait_ge(sig("y_even"), 4)
            sp.wait_ge(sig("y_odd"), 4)
            sp.dma_start(out[0].rearrange("(t p) n -> p t n", p=P), Y[:, :, :]).then_inc(sig("out_done"), 16)
            sp.wait_ge(sig("out_done"), 16)

        def sp_units(sp):
            def unit(kind, u, i, j, r):
                w = kind[3]
                sp.wait_ge(sig(f"ustore{j}"), 16 * i + 16 * (u // 2) + 16)
                sp.dma_start(qn[j][:, 0:w].unsqueeze(1), scr_p[:, ds(2 * i + u, 1), 0:w]).then_inc(sig(f"un_in{j}"), 16)

            def stored(kind, u, i, j, r):
                w = kind[3]
                if kind[6]:
                    sp.wait_ge(sig("un_done"), 2 * i + r + 1)
                else:
                    sp.wait_ge(sig("un_n"), 2 * i + u + 1)
                sp.dma_start(scr_p[:, ds(2 * i + u, 1), 0:w], qn[j][:, 0:w].unsqueeze(1)).then_inc(sig(f"ustore{j}"), 16)
            r = 0
            for kind in KINDS:
                _, u0, n = kind[0:3]
                if n == 1:
                    unit(kind, u0, 0, 0, 0)
                    stored(kind, u0, 0, 0, r)
                else:
                    with sp.Fori(0, n // 2) as i:
                        for j in range(2):
                            unit(kind, u0 + j, i, j, 0)
                        for j in range(2):
                            stored(kind, u0 + j, i, j, r + j)
                r += n if kind[6] else 0

        block = whole.enter_context(nc.Block())

        @block.sync
        def _(sp):
            sync_program(sp)

        @block.scalar
        def _(act):
            scalar_program(act)

        @block.gpsimd
        def _(pool):
            gpsimd_program(pool)

        @block.vector
        def _(dve):
            vector_program(dve)

        @block.tensor
        def _(pe):
            tensor_program(pe)


INPUTS = ["x", "c", "ctx", "c_ctx", "ada_w", "ada_b", "norm_mix", "norm_ffn", "ffn_w_in", "ffn_w_out",
          "ev_w_in", "ev_conv_w", "ev_conv_b", "dn_a_log", "dn_dt_bias", "dn_norm", "ssd_a_log", "ssd_dt_bias",
          "ssd_d", "ssd_norm", "ev_w_out", "od_w_in", "da_q_norm", "da_k_norm", "da_lambda", "da_sub_norm",
          "mla_q_a_norm", "mla_w_uq", "mla_kv_a_norm", "mla_w_ukv", "mla_q_norm", "mla_k_norm", "od_w_out"]


def kernel(**inputs):
    import concourse.bacc as bacc
    from concourse.bass_utils import run_bass_kernel_spmd

    f32 = mybir.dt.float32
    nc = bacc.Bacc("TRN2", target_bir_lowering=False, num_devices=1)
    arrays, a = {}, {}
    for name in INPUTS:
        arr = np.ascontiguousarray(inputs[name])
        arrays["in_" + name] = arr
        a[name] = nc.dram_tensor("in_" + name, arr.shape, f32, kind="ExternalInput").ap()
    arrays["consts"] = constants()
    a["consts"] = nc.dram_tensor("consts", (P, C_ALL), f32, kind="ExternalInput").ap()
    out = nc.dram_tensor("out", (1, LAT, D), f32, kind="ExternalOutput").ap()
    kw = {}
    scr = {"chunks": nc.dram_tensor("chunks", (52, P, T), f32, **kw).ap(),
           "values": nc.dram_tensor("values", (2, T, D), f32, **kw).ap(),
           "mix": nc.dram_tensor("mix", (16, P, T), f32, **kw).ap()}
    build(nc, a, out, scr)
    r = run_bass_kernel_spmd(nc, [arrays], core_ids=[0])
    return r.results[0]["out"]
```

```python
import math
from contextlib import ExitStack

import numpy as np

import concourse.bass as bass
from concourse import mybir

P = 128
D = 1024
KD = D // P
LAT = 512
CTX = 256
T = LAT + CTX
NT = T // P
EPS = 1e-6
GRID_W = 64
ROPE_THETA = 10000.0
CONV_K = 5
DN_HEADS = 8
SSD_HEADS = 16
EV_CONV = 3 * 1024 + 1024 + 512
EV_GATE = 2048
EV_MAIN = EV_CONV + EV_GATE
EV_IN = EV_MAIN + 64
CONV_CHUNKS = EV_CONV // P
GATE_CHUNKS = EV_GATE // P
HIDDEN = 2816
HC = HIDDEN // P
HG = HC // 2
DA_HEADS = 8
MLA_HEADS = 8
LAMBDA_INIT = 0.8 - 0.6 * math.exp(-0.3)
NEG = -1.0e30

C_ID = 0
C_UF = 128
C_UB = 256
C_NEGF = 384
C_NEGB = 512
C_ONES = 640
C_BLK = 768
C_ROT = 896
C_LVL = 1024
C_COS = C_LVL + 14 * 128
C_SIN = C_COS + LAT
C_ALL = C_SIN + LAT
LEVELS = 7

V_ADAB = 0
V_NMIX = 96
V_NFFN = 112
V_C = 128
V_CCTX = 136
V_CONVB = 144
V_DNN = 180
V_SSDN = 181
V_DASUB = 189
V_QA = 190
V_KVA = 194
V_SSDD = 224
V_DAQ = 204
V_DAK = 205
V_MQN = 206
V_MQR = 207
V_MKN = 208
V_MKR = 209
V_TAP = 256


def constants():
    i = np.arange(P)
    lower, upper = i[:, None] <= i[None, :], i[:, None] >= i[None, :]
    out = np.zeros((P, C_ALL), np.float32)
    out[:, C_ID:C_ID + P] = np.eye(P)
    out[:, C_UF:C_UF + P] = lower
    out[:, C_UB:C_UB + P] = upper
    out[:, C_NEGF:C_NEGF + P] = np.where(lower, 0.0, NEG)
    out[:, C_NEGB:C_NEGB + P] = np.where(upper, 0.0, NEG)
    out[:, C_ONES:C_ONES + P] = 1.0
    out[:, C_BLK:C_BLK + P] = (i[:, None] // 64) == (i[None, :] // 64)
    rot = np.zeros((P, P), np.float32)
    for r in range(P):
        if r % 32 < 16:
            rot[r + 16, r] = -1.0
        else:
            rot[r - 16, r] = 1.0
    out[:, C_ROT:C_ROT + P] = rot
    for l in range(LEVELS):
        s = 1 << l
        pair = (i[:, None] // (2 * s)) == (i[None, :] // (2 * s))
        odd = (i // s) % 2 == 1
        out[:, C_LVL + l * P:C_LVL + (l + 1) * P] = pair & ~odd[:, None] & odd[None, :]
        out[:, C_LVL + (7 + l) * P:C_LVL + (8 + l) * P] = pair & odd[:, None] & ~odd[None, :]
    inv = np.float32(ROPE_THETA) ** (-np.arange(16, dtype=np.float32) / np.float32(16))
    t = np.arange(LAT)
    for r in range(P):
        axis = (r % 64) // 32
        pos = (t // GRID_W if axis == 0 else t % GRID_W).astype(np.float32)
        ang = pos * inv[r % 16]
        out[r, C_COS:C_COS + LAT] = np.cos(ang)
        out[r, C_SIN:C_SIN + LAT] = np.sin(ang)
    return out



def schedule():
    table, slab, use, chunk = {}, 1, 0, 1
    stages = [("in0", 26, 1), ("out0", 8, 0)]
    for layer in (0, 1):
        if layer:
            stages += [("qk1", 8, 1), ("dv1", 4, 1), ("lat1", 4, 1), ("uq1", 6, 1), ("uk1", 4, 1), ("uv1", 4, 1), ("out1", 8, 0)]
        for g, n in enumerate(GROUPS):
            stages += [(f"fi{layer}{g}", n, 1), (f"fo{layer}{g}", 4, 1)]
    for name, n, wide in stages:
        table[name] = (slab, n, use, chunk)
        slab += n
        chunk += (2 * n if wide else n) - (name == "lat1")
        use += n if wide else n // 2
    return table


ADA_IN0 = 8
GROUPS = (8, 8, 6)
ATT_ORDER = (8, 9, 10, 0, 11, 1, 12, 2, 13, 3, 14, 4, 15, 5, 6, 7)
ORDER = ((4, 5, 0, 1, 2, 3), (5, 4, 3, 2, 1, 0))
INTRA = (4, 5, 0, 3, 1, 2)

SHARED = {"sd_arg": ("dn_arg", 24), "sd_d": ("dn_d", 24), "sd_e": ("dn_e", 24), "sd_gg": ("dn_gg", 12),
          "sd_tr": ("dn_tr", 12), "sd_m0": ("dn_at", 24), "sd_m1": ("dn_eb", 24), "sd_tok": ("dn_kv", 24),
          "sd_xdt": ("dn_as", 168), "sd_y": ("dn_x", 168), "sd_yb": ("dn_kk", 12), "ss_acc": ("rec_acc", 12),
          "ss_ch": ("rec_ks", 20), "ss_s": ("rec_s", 20), "ss_sd": ("rec_sd", 16), "ss_su": ("rec_su", 20),
          "ss_t": ("rec_t", 20), "ss_x": ("rec_vs", 20), "ss_yt": ("dn_og", 12), "ss_tt": ("dn_ot", 12),
          "ss_rec": ("dn_orec", 4), "ss_root": ("dn_oroot", 2), "ss_sq": ("dn_sq", 8), "ss_ssum": ("dn_ss", 8),
          "at_x0": ("un_rot", 21), "at_x1": ("un_sin", 21), "at_m0": ("un_add", 21),
          "at_m1": ("un_cos", 21), "at_s0": ("un_ss", 37), "at_s1": ("un_done", 37), "at_r": ("un_rec", 37), "at_w": ("un_root", 37), "at_p": ("un_sq", 37), "an_hi": ("la_hi", 6),
          "an_lo": ("la_lo", 6), "an_n": ("la_n", 6), "an_rec": ("la_rec", 2), "an_root": ("la_root", 2),
          "an_sq": ("la_sq", 6), "an_ss": ("la_ss", 6)}


def build(nc, a, out, scr):
    f32, f32r = mybir.dt.float32, mybir.dt.float32r
    ALU, ACT, AX = mybir.AluOpType, mybir.ActivationFunctionType, mybir.AxisListType
    ds = bass.ds
    S = schedule()
    whole = ExitStack()
    table = {}

    def sig(name):
        name = SHARED[name][0] if name in SHARED else name
        if name not in table:
            table[name] = whole.enter_context(nc.semaphore(name))
        return table[name]

    def past(name):
        return SHARED[name][1]

    def tile(stack, name, shape, dt=f32):
        return stack.enter_context(nc.sbuf_tensor(name, [P] + shape, dt))

    with whole:
        cst = tile(whole, "cst", [C_ALL])
        vec = tile(whole, "vec", [512])
        xT = tile(whole, "xT", [KD, T])
        raw = [tile(whole, f"raw{j}", [2048]) for j in range(2)]
        modl = tile(whole, "modl", [96])
        modc = tile(whole, "modc", [96])
        amod = tile(whole, "amod", [2, KD])
        csil = tile(whole, "csil", [16])
        epsc = tile(whole, "epsc", [2])
        lam = tile(whole, "lam", [8])
        gts = tile(whole, "gts", [NT, 64])
        gcol = tile(whole, "gcol", [5, NT, 48])
        bet = tile(whole, "bet", [NT, 16])
        dts = tile(whole, "dts", [NT, 32])
        alog, gbias = tile(whole, "alog", [48]), tile(whole, "gbias", [48])
        ps = whole.enter_context(nc.psum_tensor("ps", [P, 8, 512], f32))

        ident = cst[:, C_ID:C_ID + P]
        ones = cst[:, C_ONES:C_ONES + P]
        blk = cst[:, C_BLK:C_BLK + P]
        rot = cst[:, C_ROT:C_ROT + P]
        cos, sin = cst[:, C_COS:C_COS + LAT], cst[:, C_SIN:C_SIN + LAT]
        tri = (cst[:, C_UF:C_UF + P], cst[:, C_UB:C_UB + P])
        neg = (cst[:, C_NEGF:C_NEGF + P], cst[:, C_NEGB:C_NEGB + P])

        def level(d, l):
            c = C_LVL + (7 * d + l) * P
            return cst[:, c:c + P]

        def banks(b, n, w):
            return ps[:, b:b + n, :].rearrange("p b n -> p (b n)")[:, 0:w]

        gemm = ExitStack()
        Wh = [tile(gemm, f"Wh{j}", [2048], f32r) for j in range(2)]
        Wl = [tile(gemm, f"Wl{j}", [2048], f32r) for j in range(2)]
        with ExitStack() as st:
            Hh, Hl = tile(st, "Hh", [KD, T], f32r), tile(st, "Hl", [KD, T], f32r)
            with ExitStack() as s2:
                ada = [tile(s2, f"ada{j}", [KD, 256]) for j in range(3)]
                aacc = [tile(s2, f"aacc{j}", [2, 256]) for j in range(3)]
                with ExitStack() as s3:
                    ubuf = [tile(s3, f"ubuf{j}", [776]) for j in range(2)]
                    ybuf = [tile(s3, f"ybuf{j}", [776]) for j in range(2)]
                    obuf = [tile(s3, f"obuf{j}", [776]) for j in range(2)]
                    spw = [tile(s3, f"spw{j}", [NT, 48]) for j in range(6)]
                with ExitStack() as s3:
                    sqb = [tile(s3, f"sqb{j}", [T]) for j in range(2)]
                    rstd = tile(s3, "rstd", [T])
                    nrm = [tile(s3, f"nrm{j}", [T]) for j in range(2)]
                    mdl = [tile(s3, f"mdl{j}", [T]) for j in range(2)]
            with ExitStack() as s2:
                Gh, Gl = tile(s2, "Gh", [8, T], f32r), tile(s2, "Gl", [8, T], f32r)
                sgb = [tile(s2, f"sgb{j}", [T]) for j in range(2)]
                hdb = [tile(s2, f"hdb{j}", [T]) for j in range(2)]
            with ExitStack() as s2:
                latr = tile(s2, "latr", [7, T])
                lato = [tile(s2, f"lato{j}", [T]) for j in range(2)]
                with ExitStack() as s3:
                    latn = tile(s3, "latn", [2, T])
                with ExitStack() as s3:
                    ada1 = [tile(s3, f"adb{j}", [KD, 256]) for j in range(3)]
                    aacc1 = [tile(s3, f"abcc{j}", [2, 256]) for j in range(3)]
        with ExitStack() as st:
            qn = [tile(st, f"qn{j}", [T]) for j in range(4)]
            qsq = [tile(st, f"qsq{j}", [T]) for j in range(2)]
            qrs = [tile(st, f"qrs{j}", [T]) for j in range(2)]
            qsin = [tile(st, f"qsin{j}", [LAT]) for j in range(2)]
            qcos = [tile(st, f"qcos{j}", [LAT]) for j in range(2)]
            gcos = tile(st, "gcos", [4, LAT])
            rotg = tile(st, "rotg", [4, P])
        with ExitStack() as st:
            Mh, Ml = tile(st, "Mh", [16, T], f32r), tile(st, "Ml", [16, T], f32r)
            mst = [tile(st, f"mst{j}", [T]) for j in range(4)]
        with ExitStack() as st:
            att = tile(st, "att", [16, LAT])
            Ah, Al = tile(st, "Ah", [16, LAT], f32r), tile(st, "Al", [16, LAT], f32r)
            asq = [tile(st, f"asq{j}", [LAT]) for j in range(2)]
            ars = [tile(st, f"ars{j}", [LAT]) for j in range(2)]
        gemm.close()
        with ExitStack() as st:
            X = tile(st, "X", [NT, D])
            rows = tile(st, "rows", [4, P])
            lrow = tile(st, "lrow", [4, 64])
            drow = tile(st, "drow", [2])
            Y = tile(st, "Y", [4, D])
        with ExitStack() as st:
            dq, dk, dv = (tile(st, f"d{n}", [4, T]) for n in "qkv")
            ktok, vtok = tile(st, "ktok", [NT, 512]), tile(st, "vtok", [NT, 512])
            TTs, ATs = tile(st, "TTs", [NT, 2, 4, P]), tile(st, "ATs", [NT, 2, 4, P])
            dgg = [tile(st, f"dgg{j}", [2, NT, 4]) for j in range(6)]
            Sst = [tile(st, f"Sst{d}", [4, P]) for d in range(2)]
            drs = tile(st, "drs", [NT, 4])
            with ExitStack() as s2:
                Ed = [tile(s2, f"Ed{d}", [4, P]) for d in range(2)]
                EB = [tile(s2, f"EB{d}", [4, P]) for d in range(2)]
                AT = [tile(s2, f"AT{d}", [4, P]) for d in range(2)]
                Am = [[tile(s2, f"Am{d}{j}", [4, P]) for j in range(2)] for d in range(2)]
                Tm = [tile(s2, f"Tm{d}", [4, P]) for d in range(2)]
                xs = [tile(s2, f"xs{d}", [4, P]) for d in range(2)]
            with ExitStack() as s2:
                rr = [tile(s2, f"rr{d}", [4, P]) for d in range(2)]
                vn = [tile(s2, f"vn{d}", [4, P]) for d in range(2)]
                vs = [tile(s2, f"vs{d}", [4, P]) for d in range(2)]
                to = [tile(s2, f"to{d}", [4, P]) for d in range(2)]
        with ExitStack() as st:
            sx, sz = tile(st, "sx", [4, T]), tile(st, "sz", [4, T])
            sB, sC = tile(st, "sB", [T]), tile(st, "sC", [T])
            xtok, yacc = tile(st, "xtok", [NT, 512]), tile(st, "yacc", [NT, 512])
            Btok = tile(st, "Btok", [NT, P])
            xdt = tile(st, "xdt", [2, NT, 512])
            sgg = [tile(st, f"sgg{j}", [2, NT, 8]) for j in range(6)]
            Es = [[tile(st, f"Es{d}{f}", [4, P]) for f in range(2)] for d in range(2)]
            bcs = tile(st, "bcs", [P])
            hst = [tile(st, f"hst{d}", [512]) for d in range(2)]
            sty = [tile(st, f"sty{d}", [512]) for d in range(2)]
            sxs = [tile(st, f"sxs{d}", [512]) for d in range(2)]
            ssq = [tile(st, f"ssq{j}", [T]) for j in range(2)]
            srs = tile(st, "srs", [T])
        with ExitStack() as st:
            tile(st, "hold", [8192 + 16 * LAT])
            aq, ak, av = ([tile(st, f"a{n}{j}", [w]) for j in range(2)] for n, w in (("q", LAT), ("k", T), ("v", T)))
            mq, mk, mv = ([tile(st, f"m{n}{j}", [w]) for j in range(2)] for n, w in (("q", LAT), ("k", T), ("v", T)))
            mr = [tile(st, f"mr{j}", [LAT]) for j in range(2)]
            mkr = tile(st, "mkr", [T])
            prb = [tile(st, f"prb{j}", [T]) for j in range(4)]
            pT = [tile(st, f"pT{j}", [NT, LAT]) for j in range(2)]
            stat = [tile(st, f"stat{j}", [8]) for j in range(2)]

        def phase_begin(eng, k):
            for e in ("pe", "act", "dve", "pool"):
                eng.wait_ge(sig(f"{e}_phase"), k)

        def phase_end(eng, name):
            eng.drain().then_inc(sig(f"{name}_phase"), 1)

        def loop(eng, n, body):
            if n > 1:
                with eng.Fori(0, n - 1) as i:
                    body(i, False)
            body(n - 1, True)

        class Link:

            def __init__(self, eng, name, start=0):
                self.eng, self.sem, self.n = eng, sig(name), start

            def __call__(self, ins):
                self.n = self.n + 1
                ins.then_inc(self.sem, 1)
                self.eng.wait_ge(self.sem, self.n)

        def wide(t, k=KD, w=256):
            return t[:, 0:k * w].rearrange("p (k n) -> p k n", k=k)

        def load_slab(sp, n, i, src, k=KD, w=256, view=None):
            dst = wide(raw[n % 2], k, w) if view is None else view(raw[n % 2])
            sp.wait_ge(sig("slab_lo"), 2 * i + n + 1)
            if view is None:
                cut = (0, k // 4, k // 2, k // 2 + k // 4, k) if k != 6 else (0, 2, 4, 5, 6)
                parts = [(slice(cut[j], cut[j + 1]),) for j in range(4)]
            elif k == 4:
                parts = [(slice(j, j + 1),) for j in range(4)]
            else:
                parts = [(slice(j * k // 2, (j + 1) * k // 2), u) for j in range(2) for u in range(2)]
            for part in parts:
                if len(part) == 1 and k == 4:
                    d, s_ = dst[:, part[0].start], src[:, part[0].start]
                elif len(part) == 1:
                    d, s_ = dst[:, part[0]], src[:, part[0]]
                else:
                    d, s_ = dst[:, part[0], part[1]], src[:, part[0], part[1]]
                sp.dma_start(d, s_).then_inc(sig(f"slab_in{n % 2}"), 16)

        def width(n, i):
            n = n + 2 * i if type(i) is int else n
            if n == 0:
                return 512
            if n == S["lat1"][0] + 3 or S["uq1"][0] <= n < S["uk1"][0]:
                return 1024
            if S["uk1"][0] <= n < S["out1"][0]:
                return 512
            return 256 * GROUPS[2] if any(S[f"fo{l}2"][0] <= n < S[f"fo{l}2"][0] + 4 for l in (0, 1)) else 2048

        def hi_slab(act, n, i, before=None):
            w = width(n, i)
            act.wait_ge(sig(f"slab_in{n % 2}"), 64 * i + 64 * (n // 2 + 1))
            if before is not None:
                act.wait_ge(sig("gemm_done"), before)
            nc.scalar.activation(Wh[n % 2][:, 0:w], raw[n % 2][:, 0:w], ACT.Copy).then_inc(sig("slab_hi"), 1)

        def lo_slab(pool, n, i):
            w = width(n, i)
            pool.wait_ge(sig("slab_hi"), 2 * i + n + 1)
            nc.gpsimd.tensor_tensor(Wl[n % 2][:, 0:w], raw[n % 2][:, 0:w], Wh[n % 2][:, 0:w].bitcast(f32),
                                    ALU.subtract).then_inc(sig("slab_lo"), 1)

        scr_p = scr["chunks"].rearrange("m p t -> p m t")
        vscr = scr["values"]
        mix_p = scr["mix"].rearrange("m p t -> p m t")

        def rows_from():
            def put(col, src, n):
                return rows[col % P:col % P + n, col // P, :], src
            r = [put(V_ADAB, a["ada_b"].rearrange("l (r n) -> (l r) n", n=P), 96),
                 put(V_NMIX, a["norm_mix"].rearrange("l (r n) -> (l r) n", n=P), 16),
                 put(V_NFFN, a["norm_ffn"].rearrange("l (r n) -> (l r) n", n=P), 16),
                 put(V_C, a["c"].rearrange("b (r n) -> (b r) n", n=P), 8),
                 put(V_CCTX, a["c_ctx"].rearrange("(r n) -> r n", n=P), 8),
                 put(V_CONVB, a["ev_conv_b"].rearrange("l (r n) -> (l r) n", n=P), 36),
                 put(V_DNN, a["dn_norm"], 1),
                 put(V_SSDN, a["ssd_norm"].rearrange("l (r n) -> (l r) n", n=P), 8),
                 put(V_DASUB, a["da_sub_norm"], 1),
                 put(V_QA, a["mla_q_a_norm"].rearrange("l (r n) -> (l r) n", n=P), 4),
                 put(V_KVA, a["mla_kv_a_norm"].rearrange("l (r n) -> (l r) n", n=P), 2),
                 put(V_MQN, a["mla_q_norm"][:, 0:P], 1),
                 put(V_MKN, a["mla_k_norm"][:, 0:P], 1)]
            for k in range(CONV_K):
                r.append((rows[36 * (k % 3):36 * (k % 3) + 36, 2 + k // 3, :],
                          a["ev_conv_w"][0, k, :].rearrange("(r n) -> r n", n=P)))
            for col, src in ((V_DAQ, a["da_q_norm"]), (V_DAK, a["da_k_norm"]),
                             (V_MQR, a["mla_q_norm"][:, P:P + 64]), (V_MKR, a["mla_k_norm"][:, P:P + 64])):
                for hf in range(2):
                    r.append((rows[col % P:col % P + 1, col // P, 64 * hf:64 * hf + 64], src))
            r.append((drow[V_SSDD % P:V_SSDD % P + 8, :], a["ssd_d"].rearrange("l (r two) -> (l r) two", two=2)))
            r.append((gbias[:, 0:16], a["dn_dt_bias"].rearrange("l d h -> l (d h)").broadcast_to([P, 16])))
            r.append((gbias[:, 16:48], a["ssd_dt_bias"].rearrange("l d h -> l (d h)").broadcast_to([P, 32])))
            r.append((alog[:, 0:16], a["dn_a_log"].rearrange("l d h -> l (d h)").broadcast_to([P, 16])))
            r.append((alog[:, 16:48], a["ssd_a_log"].rearrange("l d h -> l (d h)").broadcast_to([P, 32])))
            r.append((lrow[:, :, :].rearrange("p a n -> p (a n)"), a["da_lambda"].rearrange("l a n -> l (a n)").broadcast_to([P, 256])))
            return r

        def product(pe, pair, use, lhs, rhs, k, w, m=P, order=None, ready=None):
            pe.wait_ge(sig(f"gemm_evac{pair}"), use + 1)
            for s, c in enumerate(order or range(k)):
                if ready:
                    ready(s)
                for b, (t0, t1) in enumerate(((0, min(w, 512)), (512, w))):
                    if t1 <= t0:
                        continue
                    o = ps[0:m, 2 * pair + b, 0:t1 - t0]
                    nc.tensor.matmul(o, lhs(c)[0], rhs(c, t0, t1)[0], start=(s == 0), stop=False)
                    nc.tensor.matmul(o, lhs(c)[0], rhs(c, t0, t1)[1], start=False, stop=False)
                    last = nc.tensor.matmul(o, lhs(c)[1], rhs(c, t0, t1)[0], start=False, stop=(s == k - 1))
            return last.then_inc(sig("gemm_done"), 1)

        def slab_ready(pe, n, i):
            pe.wait_ge(sig("slab_lo"), 2 * i + n + 3)

        def pe_wide(pe, name, k, hh, hl, w, between=None, ready=None):
            n0, ns, u0, c0 = S[name]

            def body(i, last):
                for jj in range(2):
                    n = n0 + jj
                    slot = n % 2
                    slab_ready(pe, n, i)
                    for cc in range(2):
                        lw, ll = wide(Wh[slot], k), wide(Wl[slot], k)
                        ins = product(pe, cc, 2 * i + u0 + jj,
                                      lambda c: (lw[:, c, cc * P:(cc + 1) * P], ll[:, c, cc * P:(cc + 1) * P]),
                                      lambda c, t0, t1: (hh[:, c, t0:t1], hl[:, c, t0:t1]), k, w,
                                      ready=ready if jj == 0 and cc == 0 else None)
            if not between:
                return loop(pe, ns // 2, body)
            with pe.Fori(0, ADA_IN0) as i:
                body(i, False)
                between(i)
            with pe.Fori(ADA_IN0, ns // 2) as i:
                body(i, False)

        def pe_narrow(pe, name, k, hh, hl, w, order=None, ready=None):
            n0, ns, u0, c0 = S[name]

            def body(i, last):
                for jj in range(2):
                    n = n0 + jj
                    slot = n % 2
                    slab_ready(pe, n, i)
                    lw, ll = wide(Wh[slot], k, P), wide(Wl[slot], k, P)
                    product(pe, jj, i + u0, lambda c: (lw[:, c, :], ll[:, c, :]),
                            lambda c, t0, t1: (hh[:, c, t0:t1], hl[:, c, t0:t1]), k, w, order=order,
                            ready=ready if jj == 0 else None)
            loop(pe, ns // 2, body)

        def normed(pe, r):
            return lambda s: pe.wait_ge(sig("lo_done"), 8 * r + s + 1)

        def pe_rows(pe, name, k, hh, hl, between=None):
            n0, ns, u0, c0 = S[name]

            def body(i, last):
                for jj in range(2):
                    n = n0 + jj
                    slot = n % 2
                    slab_ready(pe, n, i)
                    lw, ll = wide(Wh[slot], k), wide(Wl[slot], k)
                    for cc in range(2):
                        pe.wait_ge(sig(f"gemm_evac{cc}"), 2 * i + u0 + jj + 1)
                        for r in range(3):
                            t = (3 * cc + r) * P
                            o = ps[:, 2 * cc + r // 2, (r % 2) * 256:(r % 2) * 256 + 256]
                            for c in range(k):
                                nc.tensor.matmul(o, hh[:, c, t:t + P], lw[:, c, :], start=(c == 0), stop=False)
                                nc.tensor.matmul(o, hh[:, c, t:t + P], ll[:, c, :], start=False, stop=False)
                                ins = nc.tensor.matmul(o, hl[:, c, t:t + P], lw[:, c, :], start=False, stop=(c == k - 1))
                        ins.then_inc(sig("gemm_done"), 1)
                if between:
                    between(i)
            loop(pe, ns // 2, body)

        def pe_ada_first(pe, q, it):
            pe.wait_ge(sig(f"ada_in{q}"), 16 * it + 16)
            for cc in range(2):
                for k in range(KD):
                    ins = nc.tensor.matmul(ps[:, 4, 4 * q + 2 * cc:4 * q + 2 * cc + 2], ada[q][:, k, cc * P:(cc + 1) * P],
                                           csil[:, k:16:8], start=(k == 0), stop=(k == KD - 1))
            ins.then_inc(sig("ada_sum"), 1)

        def pe_ada(pe, q, it, acc=aacc, used=None):
            pe.wait_ge(sig("ada_used"), 3 * it + q + 1 if used is None else used)
            for cc in range(2):
                for x in range(2):
                    c = 4 * q + 2 * cc + x
                    ins = nc.tensor.matmul(ps[:, 4, c:c + 1], acc[q][:, x, cc * P:(cc + 1) * P], ones[:, 0:1], start=True, stop=True)
            ins.then_inc(sig("ada_sum"), 1)

        def pe_norm(pe, r, w):
            for k in range(KD):
                pe.wait_ge(sig("sq_done"), 8 * r + k + 1)
                nc.tensor.matmul(ps[:, 6, 0:512], ones, sqb[k % 2][:, 0:512], start=(k == 0), stop=(k == KD - 1))\
                    .then_inc(sig("sq_used"), 1)
                if w > 512:
                    nc.tensor.matmul(ps[:, 7, 0:256], ones, sqb[k % 2][:, 512:768], start=(k == 0), stop=(k == KD - 1))\
                        .then_inc(sig("sq_used2"), 1)

        def pe_setup(pe):
            pe.wait_ge(sig("consts_in"), 16)
            pe.wait_ge(sig("rows_in"), 16 * len(rows_from()))
            pe.wait_ge(sig("rows_spread"), 1)
            for j in range(4):
                ins = nc.tensor.transpose(ps[:, 7, j * P:(j + 1) * P], rows[:, j, :], ident)
            ins.then_inc(sig("rows_turned"), 1)
            for t in range(NT):
                pe.wait_ge(sig("x_in"), 32)
                for hf in range(2):
                    u = 2 * t + hf
                    if u >= 6:
                        pe.wait_ge(sig("xt_evac"), u - 5)
                    for r in range(4):
                        k = 4 * hf + r
                        ins = nc.tensor.transpose(ps[:, u % 6, r * P:(r + 1) * P], X[:, t, k * P:(k + 1) * P], ident)
                    ins.then_inc(sig("xt_done"), 1)

        def pe_gate_products(pe):
            slab_ready(pe, 0, 0)
            lw, ll = wide(Wh[0], KD, 64), wide(Wl[0], KD, 64)
            for t in range(NT):
                o = ps[:, 5, t * 64:(t + 1) * 64]
                for c in range(KD):
                    if t == 0:
                        normed(pe, 0)(c)
                    tt = slice(t * P, (t + 1) * P)
                    nc.tensor.matmul(o, Hh[:, c, tt], lw[:, c, :], start=(c == 0), stop=False)
                    nc.tensor.matmul(o, Hh[:, c, tt], ll[:, c, :], start=False, stop=False)
                    ins = nc.tensor.matmul(o, Hl[:, c, tt], lw[:, c, :], start=False, stop=(c == KD - 1))
            ins.then_inc(sig("gemm_done"), 1)

        def sets(v, l, par):
            return v.rearrange("p (n two s) -> p n two s", two=2, s=1 << l)[:, :, par, :]

        def pe_deltanet(pe, g):
            flat = TTs[:, :, :, :, :].rearrange("p c d h n -> p (c d h n)")
            for x in range(4):
                pe.wait_ge(sig("dn_sq"), 4 * g + x + 1)
                if x >= 2:
                    pe.wait_ge(sig("dn_root"), 4 * g + x - 1)
                for b in range(3):
                    ins = nc.tensor.matmul(ps[:, 3 * (x % 2) + b, :], ones, flat[:, (3 * x + b) * 512:(3 * x + b + 1) * 512],
                                           start=True, stop=True)
                ins.then_inc(sig("dn_ss"), 1)
            pe.wait_ge(sig("dn_unit"), 4 * g + 4)
            pe.wait_ge(sig("dn_gg"), 6 * g + 6)
            pe.wait_ge(sig("ld_dv"), 16 * g + 16)
            for q, c in enumerate(INTRA):
                tc = slice(c * P, (c + 1) * P)
                for d in range(2):
                    if q:
                        pe.wait_ge(sig("dn_tt"), 72 * g + 12 * q - 1 + d)
                    nc.tensor.matmul(ps[:, 2 + d, :], tri[d], dgg[1][:, d, c, :].unsqueeze(2).broadcast_to([P, 4, P]),
                                     start=True, stop=False, skip_group_check=True)
                    for h in range(4):
                        ins = nc.tensor.matmul(ps[:, 2 + d, h * P:(h + 1) * P],
                                               dgg[0][:, d, c, h:h + 1].broadcast_to([P, P]), tri[d],
                                               start=False, stop=(h == 3), skip_group_check=True)
                    ins.then_inc(sig("dn_d"), 1)
                if q:
                    pe.wait_ge(sig("dn_at"), 12 * g + 2 * q)
                for b, mv_ in ((0, dk), (1, dq)):
                    for h in range(4):
                        ins = nc.tensor.matmul(ps[:, b, h * P:(h + 1) * P], dk[:, h, tc], mv_[:, h, tc], start=True, stop=True)
                ins.then_inc(sig("dn_kk"), 1)
                if q:
                    pe.wait_ge(sig("dn_xs"), 72 * g + 12 * q)
                for b, src in ((4, dk), (5, dv)):
                    for h in range(4):
                        ins = nc.tensor.transpose(ps[:, b, h * P:(h + 1) * P], src[:, h, tc], ident)
                ins.then_inc(sig("dn_tr"), 1)
                for d in range(2):
                    pe.wait_ge(sig("dn_as"), 84 * g + 14 * q + d + 1)
                    if d == 0:
                        pe.wait_ge(sig("dn_kv"), 12 * g + 2 * q + 2)
                    for h in range(4):
                        ins = nc.tensor.transpose(ps[:, 4 + d, h * P:(h + 1) * P], Am[d][0][:, h, :], ident)
                    ins.then_inc(sig("dn_x"), 1)
                for l in range(1, LEVELS):
                    for d in range(2):
                        pe.wait_ge(sig("dn_as"), 84 * g + 14 * q + 2 * l + d + 1)
                        pe.wait_ge(sig("dn_t"), 72 * g + 12 * q + 2 * (l - 1) + d + 1)
                        for h in range(4):
                            ins = nc.tensor.matmul(ps[:, 4 + d, h * P:(h + 1) * P], Am[d][l % 2][:, h, :], Tm[d][:, h, :],
                                                   start=True, stop=True)
                        ins.then_inc(sig("dn_x"), 1)
                    for d in range(2):
                        TT = TTs[:, c, d, :, :]
                        pe.wait_ge(sig("dn_xs"), 72 * g + 12 * q + 2 * (l - 1) + d + 1)
                        if l == 1:
                            pe.wait_ge(sig("dn_tt0"), 12 * g + 2 * q + d + 1)
                        else:
                            pe.wait_ge(sig("dn_tt"), 72 * g + 12 * q + 2 * (l - 2) + d + 1)
                        if l < LEVELS - 1:
                            for h in range(4):
                                ins = nc.tensor.matmul(ps[:, 6 + d, h * 64:(h + 1) * 64], TT[:, h, :],
                                                       sets(xs[d][:, h, :], l, d), start=True, stop=True)
                            ins.then_inc(sig("dn_tb"), 1)
                        for h in range(4):
                            ins = nc.tensor.matmul(ps[:, 2 + d, h * 64:(h + 1) * 64], xs[d][:, h, :],
                                                   sets(TT[:, h, :], l, 1 - d), start=True, stop=True)
                        ins.then_inc(sig("dn_ttb"), 1)
            pe.wait_ge(sig("dn_tt"), 72 * g + 72)
            pe.wait_ge(sig("dn_kv"), 12 * g + 12)
            pe.wait_ge(sig("dn_at"), 12 * g + 12)
            for k in range(NT):
                cs = [ORDER[d][k] for d in range(2)]
                if k:
                    for bank, src, name in ((0, dk, "rec_ks"), (2, dq, "rec_qs")):
                        for d in range(2):
                            tc = slice(cs[d] * P, (cs[d] + 1) * P)
                            pe.wait_ge(sig("rec_s"), 10 * g + 2 * (k - 1) + d + 1)
                            if k > 1 and bank == 2:
                                pe.wait_ge(sig("rec_t"), 10 * g + 2 * (k - 2) + d + 1)
                            for h in range(4):
                                ins = nc.tensor.matmul(ps[:, bank + d, h * P:(h + 1) * P], src[:, h, tc], Sst[d][:, h, :],
                                                       start=True, stop=True)
                            ins.then_inc(sig(name), 1)
                for d in range(2):
                    r = rr[d] if k else vtok[:, cs[d], :].rearrange("p (h n) -> p h n", h=4)
                    if k:
                        pe.wait_ge(sig("rec_r"), 10 * g + 2 * (k - 1) + d + 1)
                        pe.wait_ge(sig("rec_o"), 12 * g + 2 * (k - 1) + d + 1)
                    for h in range(4):
                        ins = nc.tensor.matmul(ps[:, 4 + d, h * P:(h + 1) * P], TTs[:, cs[d], d, h, :], r[:, h, :],
                                               start=True, stop=True)
                    ins.then_inc(sig("rec_v"), 1)
                for d in range(2):
                    if k < NT - 1:
                        pe.wait_ge(sig("rec_vs"), 10 * g + 2 * k + d + 1)
                        for h in range(4):
                            ins = nc.tensor.matmul(ps[:, 6 + d, h * P:(h + 1) * P], ktok[:, cs[d], h * P:(h + 1) * P],
                                                   vs[d][:, h, :], start=True, stop=True)
                        ins.then_inc(sig("rec_su"), 1)
                for d in range(2):
                    pe.wait_ge(sig("rec_vn"), 12 * g + 2 * k + d + 1)
                    for h in range(4):
                        ins = nc.tensor.matmul(ps[:, 4 + d, h * P:(h + 1) * P], ATs[:, cs[d], d, h, :], vn[d][:, h, :],
                                               start=True, stop=True)
                    ins.then_inc(sig("rec_ob"), 1)
            pe.wait_ge(sig("dn_on"), g + 1)
            oacc = dv[:, :, :].rearrange("p h t -> p (h t)").rearrange("p (c n) -> p c n", c=NT)
            for c in range(NT):
                if c >= 2:
                    pe.wait_ge(sig("dn_og"), 6 * g + c - 1)
                for h in range(4):
                    ins = nc.tensor.transpose(ps[:, 4 + c % 2, h * P:(h + 1) * P], oacc[:, c, h * P:(h + 1) * P], ident)
                ins.then_inc(sig("dn_ot"), 1)

        def pe_ssd(pe, g):
            pe.wait_ge(sig("sd_gg"), past("sd_gg") + 6 * g + 6)
            pe.wait_ge(sig("sd_in"), 48 * g + 48)
            def front(q, c):
                tc = slice(c * P, (c + 1) * P)
                if q:
                    pe.wait_ge(sig("sd_tok"), past("sd_tok") + 18 * g + 3 * q)
                for h in range(4):
                    nc.tensor.transpose(ps[:, 0, h * P:(h + 1) * P], sx[:, h, tc], ident)
                nc.tensor.transpose(ps[:, 1, 0:P], sB[:, tc], ident)
                nc.tensor.matmul(ps[:, 2, 0:P], sB[:, tc], sC[:, tc], start=True, stop=True).then_inc(sig("sd_tr"), 1)
                for d in range(2):
                    for f in range(2):
                        b = 3 + 2 * d + f
                        if q:
                            pe.wait_ge(sig("sd_arg"), past("sd_arg") + 24 * g + 4 * (q - 1) + 2 * d + f + 1)
                        nc.tensor.matmul(ps[:, b, :], tri[d], sgg[1][:, d, c, 4 * f:4 * f + 4].unsqueeze(2).broadcast_to([P, 4, P]),
                                         start=True, stop=False, skip_group_check=True)
                        for h in range(4):
                            ins = nc.tensor.matmul(ps[:, b, h * P:(h + 1) * P],
                                                   sgg[0][:, d, c, 4 * f + h:4 * f + h + 1].broadcast_to([P, P]), tri[d],
                                                   start=False, stop=(h == 3), skip_group_check=True)
                        ins.then_inc(sig("sd_d"), 1)
            front(0, INTRA[0])
            for q, c in enumerate(INTRA):
                if q < NT - 1:
                    front(q + 1, INTRA[q + 1])
                if q:
                    pe.wait_ge(sig("sd_y"), past("sd_y") + 6 * g + q)
                pe.wait_ge(sig("sd_m0"), past("sd_m0") + 12 * g + 2 * q + 2)
                pe.wait_ge(sig("sd_m1"), past("sd_m1") + 12 * g + 2 * q + 2)
                pe.wait_ge(sig("sd_xdt"), past("sd_xdt") + 12 * g + 2 * q + 2)
                for h in range(8):
                    for d in range(2):
                        ins = nc.tensor.matmul(ps[:, 7, h * 64:(h + 1) * 64], Es[d][h // 4][:, h % 4, :],
                                               xdt[:, d, c, h * 64:(h + 1) * 64], start=(d == 0), stop=(d == 1))
                ins.then_inc(sig("sd_yb"), 1)
            for k in range(NT):
                for d in range(2):
                    c = ORDER[d][k]
                    tc = slice(c * P, (c + 1) * P)
                    if k:
                        pe.wait_ge(sig("ss_s"), past("ss_s") + 10 * g + 2 * (k - 1) + d + 1)
                        if k > 1:
                            pe.wait_ge(sig("ss_t"), past("ss_t") + 10 * g + 2 * (k - 2) + d + 1)
                        nc.tensor.matmul(ps[:, d, :], sC[:, tc], hst[d][:, :], start=True, stop=True).then_inc(sig("ss_ch"), 1)
                    if k < NT - 1:
                        pe.wait_ge(sig("ss_x"), past("ss_x") + 10 * g + 2 * k + d + 1)
                        nc.tensor.matmul(ps[:, 2 + d, :], Btok[:, c, :], sxs[d][:, :], start=True, stop=True)\
                            .then_inc(sig("ss_su"), 1)
            pe.wait_ge(sig("ss_acc"), past("ss_acc") + 10 * g + 10)
            for c in range(NT):
                if c >= 2:
                    pe.wait_ge(sig("ss_yt"), past("ss_yt") + 6 * g + c - 1)
                for h in range(4):
                    ins = nc.tensor.transpose(ps[:, 4 + c % 2, h * P:(h + 1) * P], yacc[:, c, h * P:(h + 1) * P], ident)
                ins.then_inc(sig("ss_tt"), 1)
            for h in range(4):
                pe.wait_ge(sig("ss_sq"), past("ss_sq") + 4 * g + h + 1)
                nc.tensor.matmul(ps[:, 6, 0:512], ones, ssq[h % 2][:, 0:512], start=(h == 0), stop=(h == 3))
                nc.tensor.matmul(ps[:, 7, 0:256], ones, ssq[h % 2][:, 512:768], start=(h == 0), stop=(h == 3))\
                    .then_inc(sig("ss_ssum"), 1)

        UNITS = []
        for n, w, span, gain, r in ((8, LAT, 64, V_DAQ, 0), (8, T, 64, V_DAK, 1), (8, LAT, P, V_MQN, None),
                                    (4, LAT, 64, V_MQR, 2), (8, T, P, V_MKN, None), (1, T, 64, V_MKR, 3)):
            for _ in range(n):
                UNITS.append((w, span, gain, r, sum(x[3] is not None for x in UNITS)))
        ROTATING = (V_DAQ, V_DAK, V_MQR, V_MKR)

        def pe_units(pe):
            pe.wait_ge(sig("un_mat"), 4)
            for v, (w, span, gain, r, rv) in enumerate(UNITS):
                if r is not None:
                    pe.wait_ge(sig(f"un_in{v % 4}"), 16 * (v // 4) + 16)
                    if rv >= 4:
                        pe.wait_ge(sig("un_sin"), rv - 3)
                    nc.tensor.matmul(ps[:, 4 + rv % 4, :], rotg[:, r, :], qn[v % 4][:, 0:LAT], start=True, stop=True)\
                        .then_inc(sig("un_rot"), 1)
                pe.wait_ge(sig("un_sq"), v + 1)
                if v >= 2:
                    pe.wait_ge(sig("un_root"), v - 1)
                for b, (t0, t1) in enumerate(((0, 512), (512, w))):
                    if t1 > t0:
                        ins = nc.tensor.matmul(ps[:, 2 * (v % 2) + b, 0:t1 - t0], ones if span == P else blk,
                                               qsq[v % 2][:, t0:t1], start=True, stop=True)
                ins.then_inc(sig("un_ss"), 1)

        def attention_units():
            used, out = [0, 0], []
            for hu in range(4):
                da, hh = hu % 2 == 0, hu // 2
                for qt in range(4):
                    pairs = []
                    for p in ((0, 1) if da else (qt % 2,)):
                        pairs.append((p, used[p]))
                        used[p] += 1
                    out.append((4 * hu + qt, da, hh, qt, pairs))
            assert used == [12, 12]
            return out

        def pe_attention(pe):
            U = attention_units()
            with pe.Fori(0, 4) as i:
                def scores(u, da, hh, qt, pairs):
                    if qt == 0:
                        pe.wait_ge(sig(f"at_in{hh}{0 if da else 1}"), (48 if da else 64) * i + (48 if da else 64))
                    tq = slice(qt * P, (qt + 1) * P)
                    for p, use in pairs:
                        pe.wait_ge(sig(f"at_e{p}"), 12 * i + use + 1)
                        rows_ = slice(64 * p, 64 * p + 64) if da else slice(0, P)
                        q_, k_ = (aq[hh], ak[hh]) if da else (mq[hh], mk[hh])
                        for b, (t0, t1) in enumerate(((0, 512), (512, T))):
                            o = ps[:, 2 * p + b, 0:t1 - t0]
                            ins = nc.tensor.matmul(o, q_[rows_, tq], k_[rows_, t0:t1], start=True, stop=da)
                            if not da:
                                ins = nc.tensor.matmul(o, mr[hh][0:64, tq], mkr[0:64, t0:t1], start=False, stop=True)
                        ins.then_inc(sig(f"at_s{p}"), 1)
                def outputs(hu):
                    pe.wait_ge(sig("at_pt"), 16 * i + 4 * hu + 5)
                    pe.wait_ge(sig("at_o"), 4 * i + hu + 1)
                    v_ = (av if hu % 2 == 0 else mv)[hu // 2]
                    for kt in range(NT):
                        ins = nc.tensor.matmul(ps[:, 6 + hu % 2, :], v_[:, kt * P:(kt + 1) * P], pT[hu % 2][:, kt, :],
                                               start=(kt == 0), stop=(kt == NT - 1))
                    ins.then_inc(sig("at_pv"), 1)
                scores(*U[0])
                for u, da, hh, qt, _ in U:
                    if u < 15:
                        scores(*U[u + 1])
                    if u and qt == 0:
                        outputs(u // 4 - 1)
                    pe.wait_ge(sig("at_p"), past("at_p") + 16 * i + u + 1)
                    pe.wait_ge(sig("at_pt"), 16 * i + u + 1)
                    for kt in range(NT):
                        ins = nc.tensor.transpose(ps[:, 4 + kt // 4, (kt % 4) * P:(kt % 4 + 1) * P],
                                                  prb[2 * (u % 2)][:, kt * P:(kt + 1) * P], ident)
                    ins.then_inc(sig("at_tr"), 1)
                outputs(3)

        def pe_latents(pe):
            for k in range(6):
                pe.wait_ge(sig("la_sq"), k + 1)
                if k < 4:
                    ins = nc.tensor.matmul(ps[:, 6, :], ones, lato[k % 2][:, 0:512], start=(k == 0), stop=(k == 3))
                else:
                    nc.tensor.matmul(ps[:, 4, :], ones, lato[k % 2][:, 0:512], start=(k == 4), stop=(k == 5))
                    ins = nc.tensor.matmul(ps[:, 5, 0:256], ones, lato[k % 2][:, 512:T], start=(k == 4), stop=(k == 5))
                ins.then_inc(sig("la_ss"), 1)

        def pe_ffn(pe, layer, w):
            for grp, n in enumerate(GROUPS):
                pe_wide(pe, f"fi{layer}{grp}", KD, Hh, Hl, w, ready=None if grp else normed(pe, 2 * layer + 1))
                pe.wait_ge(sig("hid_lo"), 22 * layer + sum(GROUPS[:grp + 1]))
                pe.wait_ge(sig("hid_hi"), 22 * layer + sum(GROUPS[:grp + 1]))
                pe_wide(pe, f"fo{layer}{grp}", n, Gh, Gl, w)

        def pe_att_norm(pe):
            for k in range(8):
                pe.wait_ge(sig("an_sq"), past("an_sq") + k + 1)
                if k >= 2:
                    pe.wait_ge(sig("an_root"), past("an_root") + k - 1)
                nc.tensor.matmul(ps[:, 4 + k % 2, :], ones, asq[k % 2][:, :], start=True, stop=True).then_inc(sig("an_ss"), 1)

        def tensor_program(pe):
            pe_setup(pe)
            for it in range(3):
                if it == 0:
                    pe.wait_ge(sig("silu_c"), 1)
                    pe.wait_ge(sig("xt_evac"), 12)
                else:
                    pe.wait_ge(sig("mod_evac"), it)
                pe_ada_first(pe, 0, it)
                for q in (1, 2):
                    pe_ada(pe, q, it, used=2 * it + q + 3)
            phase_end(pe, "pe")
            phase_begin(pe, 1)
            pe_norm(pe, 0, T)
            phase_end(pe, "pe")
            pe_gate_products(pe)

            def ada_between(i):
                pe.wait_ge(sig("mod_evac"), i + 3)
                for q in range(3):
                    pe_ada(pe, q, i + 3)
            pe_wide(pe, "in0", KD, Hh, Hl, T, ada_between)
            phase_end(pe, "pe")
            phase_begin(pe, 3)
            flat = gcol[:, 0, :, :].rearrange("p c n -> p (c n)")
            for b, mat in enumerate((tri[0], tri[1], ones)):
                ins = nc.tensor.matmul(ps[:, b, 0:NT * 48], mat, flat, start=True, stop=True)
            ins.then_inc(sig("cum_sums"), 1)
            pe.wait_ge(sig("cum_ready"), 6)
            for base, part in ((3, pe_deltanet), (5, pe_ssd)):
                with pe.Fori(0, 2) as g:
                    phase_begin(pe, base + g)
                    part(pe, g)
                    phase_end(pe, "pe")
            phase_begin(pe, 7)
            pe_narrow(pe, "out0", 16, Mh, Ml, T, ready=lambda s: pe.wait_ge(sig("mix_lo"), s + 1))
            phase_end(pe, "pe")
            phase_begin(pe, 8)
            pe_norm(pe, 1, T)
            phase_end(pe, "pe")
            pe_ffn(pe, 0, T)
            phase_end(pe, "pe")
            phase_begin(pe, 10)
            pe_norm(pe, 2, T)
            phase_end(pe, "pe")
            pe_qkv1(pe)
            phase_end(pe, "pe")
            phase_begin(pe, 12)
            pe_latents(pe)
            pe.wait_ge(sig("la_lo"), 6)
            pe.wait_ge(sig("la_hi"), 6)
            pe_wide(pe, "uq1", 4, Hh, Hl, LAT)
            pe_wide(pe, "uk1", 2, Hh[:, 4:6, :], Hl[:, 4:6, :], T)
            pe_rows(pe, "uv1", 2, Hh[:, 4:6, :], Hl[:, 4:6, :])
            phase_end(pe, "pe")
            phase_begin(pe, 13)
            pe_units(pe)
            phase_end(pe, "pe")
            phase_begin(pe, 14)
            pe_attention(pe)
            phase_end(pe, "pe")
            phase_begin(pe, 15)
            pe_att_norm(pe)
            pe_narrow(pe, "out1", 16, Ah, Al, LAT, order=ATT_ORDER,
                      ready=lambda s: pe.wait_ge(sig("an_lo"), past("an_lo") + s + 1))
            phase_end(pe, "pe")
            phase_begin(pe, 16)
            pe_norm(pe, 3, LAT)
            phase_end(pe, "pe")
            pe_ffn(pe, 1, LAT)
            phase_end(pe, "pe")
            phase_begin(pe, 18)
            for t in range(4):
                for hf in range(2):
                    u = 2 * t + hf
                    for r in range(4):
                        ins = nc.tensor.transpose(ps[:, u, r * P:(r + 1) * P], xT[:, 4 * hf + r, t * P:(t + 1) * P], ident)
                    ins.then_inc(sig("yt_done"), 1)

        def pe_qkv1(pe):
            def modulation(it):
                pe.wait_ge(sig("mod_evac"), it)
                for q in range(3):
                    pe_ada(pe, q, it, aacc1)
            n0, ns, u0, c0 = S["qk1"]
            for part, w in ((0, LAT), (1, T)):
                def body(i, last):
                    for jj in range(2):
                        n = n0 + 4 * part + jj
                        slot = n % 2
                        slab_ready(pe, n, i)
                        for cc in range(2):
                            lw, ll = wide(Wh[slot]), wide(Wl[slot])
                            ins = product(pe, cc, 2 * i + u0 + 4 * part + jj,
                                          lambda c: (lw[:, c, cc * P:(cc + 1) * P], ll[:, c, cc * P:(cc + 1) * P]),
                                          lambda c, t0, t1: (Hh[:, c, t0:t1], Hl[:, c, t0:t1]), KD, w,
                                          ready=normed(pe, 2) if part + jj + cc == 0 else None)
                loop(pe, 2, body)
                modulation(ADA_IN0 + 3 + part)
            pe_rows(pe, "dv1", KD, Hh, Hl, between=lambda i: modulation(i + ADA_IN0 + 5))
            n0, ns, u0, c0 = S["lat1"]
            for jj in range(4):
                n = n0 + jj
                slot = n % 2
                slab_ready(pe, n, 0)
                w = LAT if jj < 2 else T
                lw, ll = (wide(Wh[slot]), wide(Wl[slot])) if jj < 3 else (wide(Wh[slot], KD, P), wide(Wl[slot], KD, P))
                for cc in range(2 if jj < 3 else 1):
                    ins = product(pe, cc, u0 + jj,
                                  lambda c: (lw[:, c, cc * P:(cc + 1) * P], ll[:, c, cc * P:(cc + 1) * P]),
                                  lambda c, t0, t1: (Hh[:, c, t0:t1], Hl[:, c, t0:t1]), KD, w)
            modulation(ADA_IN0 + 7)

        def pairbank(pair, w):
            return banks(2 * pair, 2, w)

        def act_norm(act, r, w, wides, between=None):
            for k in range(KD):
                if 8 * r + k >= 2:
                    act.wait_ge(sig("sq_used"), 8 * r + k - 1)
                if k >= 2 and w > 512:
                    act.wait_ge(sig("sq_used2"), 8 * wides + k - 1)
                nc.scalar.activation(sqb[k % 2][:, 0:w], xT[:, k, 0:w], ACT.Square).then_inc(sig("sq_done"), 1)
            if between:
                between()
            act.wait_ge(sig("sq_used"), 8 * r + 8)
            if w > 512:
                act.wait_ge(sig("sq_used2"), 8 * wides + 8)
            nc.scalar.activation(rstd[:, 0:w], banks(6, 2, w), ACT.Sqrt, scale=1.0 / D, bias=epsc[:, 0:1]).then_inc(sig("rstd_done"), 1)
            for k in range(KD):
                act.wait_ge(sig("mod_done"), 8 * r + k + 1)
                nc.scalar.activation(Hh[:, k, 0:w], mdl[k % 2][:, 0:w], ACT.Copy).then_inc(sig("hi_done"), 1)

        def act_stage(act, name, evac, prefetch=True):
            n0, ns, _, c0 = S[name]
            per = 1 if name.startswith("out") else 2

            def body(i, last):
                for jj in range(2):
                    if not (last and jj == 1 and not prefetch):
                        hi_slab(act, n0 + jj + 1, i, before=2 * per * i + c0 + per * jj)
                    if evac:
                        evac(i, jj, S[name][2])
            loop(act, ns // 2, body)

        def act_in0(act):
            n0, ns, u0, c0 = S["in0"]

            def copy_out(i, jj, cc):
                act.wait_ge(sig("gemm_done"), 4 * i + c0 + 2 * jj + cc + 1)
                act.wait_ge(sig("conv_step"), 16 * i + 4 * (2 * jj + cc) + 4)
                nc.scalar.activation(ubuf[cc][:, 2:514], ps[:, 2 * cc, :], ACT.Copy)
                nc.scalar.activation(ubuf[cc][:, 516:772], ps[:, 2 * cc + 1, 0:256], ACT.Copy)\
                    .then_inc(sig(f"gemm_evac{cc}"), 1)
                m = 4 * i + 2 * jj + cc
                act.wait_ge(sig(f"gemm_evac{cc}"), 2 * i + jj + 2)
                act.wait_ge(sig("silu_done"), m + 1)
                nc.scalar.activation(ybuf[cc][:, 0:770], ubuf[cc][:, 0:770], ACT.Copy, scale=vec[:, ds(V_TAP + m, 1)])\
                    .then_inc(sig("tap0"), 1)

            def silu_out(i, jj, cc):
                m = 4 * i + 2 * jj + cc
                act.wait_ge(sig("conv_step"), 16 * i + 4 * (2 * jj + cc) + 12)
                act.wait_ge(sig(f"store{cc}"), 64 * i + 32 * jj + 32)
                nc.scalar.activation(obuf[cc][:, 0:770], ybuf[cc][:, 0:770], ACT.Silu,
                                     bias=vec[:, ds(V_CONVB + m, 1)]).then_inc(sig("silu_done"), 1)
                act.wait_ge(sig("silu_done"), 4 * i + 2 * jj + cc + 3)
                act.dma_start(scr_p[:, ds(m, 1), 0:512], obuf[cc][:, 0:512].unsqueeze(1)).then_inc(sig(f"store{cc}"), 16)
                act.dma_start(scr_p[:, ds(m, 1), 512:T], obuf[cc][:, 514:770].unsqueeze(1)).then_inc(sig(f"store{cc}"), 16)

            def conv_body(i):
                hi_slab(act, n0 + 1, i, before=4 * i + c0)
                copy_out(i, 0, 0)
                copy_out(i, 0, 1)
                silu_out(i, 0, 0)
                hi_slab(act, n0 + 2, i, before=4 * i + c0 + 2)
                copy_out(i, 1, 0)
                silu_out(i, 0, 1)
                copy_out(i, 1, 1)
                silu_out(i, 1, 0)
                silu_out(i, 1, 1)
            act.wait_ge(sig("edges"), 6)
            with act.Fori(0, 9) as i:
                conv_body(i)

            def gate_body(i, last):
                for jj in range(2):
                    if not (last and jj == 1):
                        hi_slab(act, n0 + 18 + jj + 1, i, before=4 * i + c0 + 36 + 2 * jj)
                    for cc in range(2):
                        act.wait_ge(sig("gemm_done"), 4 * i + c0 + 36 + 2 * jj + cc + 1)
                        act.wait_ge(sig(f"store{cc}"), 64 * i + 32 * jj + 64 * 9 + 32)
                        nc.scalar.activation(obuf[cc][:, 0:T], pairbank(cc, T), ACT.Silu)\
                            .then_inc(sig(f"gemm_evac{cc}"), 1)
                        act.wait_ge(sig(f"gemm_evac{cc}"), 2 * i + 18 + jj + 2)
                        m = 4 * i + 2 * jj + cc + 36
                        act.dma_start(scr_p[:, ds(m, 1), 0:512], obuf[cc][:, 0:512].unsqueeze(1)).then_inc(sig(f"store{cc}"), 16)
                        act.dma_start(scr_p[:, ds(m, 1), 512:T], obuf[cc][:, 512:T].unsqueeze(1)).then_inc(sig(f"store{cc}"), 16)
            loop(act, 4, gate_body)

        def act_deltanet(act, g):
            def square(x):
                src = (dq, dk)[x // 2][:, 2 * (x % 2):2 * (x % 2) + 2, :].rearrange("p h t -> p (h t)")
                if x % 2 == 0:
                    act.wait_ge(sig(("ld_dq", "ld_dk")[x // 2]), 16 * g + 16)
                nc.scalar.activation(TTs[:, :, :, :, :].rearrange("p c d h n -> p (c d h n)")[:, x * 1536:(x + 1) * 1536],
                                     src, ACT.Square).then_inc(sig("dn_sq"), 1)

            def root(x):
                act.wait_ge(sig("dn_ss"), 4 * g + x + 1)
                nc.scalar.activation(ATs[:, :, :, :, :].rearrange("p c d h n -> p (c d h n)")[:, x * 1536:(x + 1) * 1536],
                                     banks(3 * (x % 2), 3, 1536), ACT.Ln, scale=(float(P) if x < 2 else 1.0),
                                     bias=epsc[:, 1:2] if x < 2 else epsc[:, 0:1]).then_inc(sig("dn_root"), 1)

            def inverse(x):
                act.wait_ge(sig("dn_root"), 4 * g + x + 1)
                flat = ATs[:, :, :, :, :].rearrange("p c d h n -> p (c d h n)")[:, x * 1536:(x + 1) * 1536]
                nc.scalar.activation(flat, flat, ACT.Exp, scale=-0.5).then_inc(sig("dn_rec"), 1)
            square(0)
            for x in range(4):
                if x < 3:
                    square(x + 1)
                root(x)
                inverse(x)
            for q, c in enumerate(INTRA):
                for d in range(2):
                    act.wait_ge(sig("dn_arg"), 12 * g + 2 * q + d + 1)
                    nc.scalar.activation(Ed[d][:, :, :], Ed[d][:, :, :], ACT.Exp).then_inc(sig("dn_e"), 1)
                act.wait_ge(sig("dn_tr"), 6 * g + q + 1)
                nc.scalar.activation(ktok[:, c, :], ps[:, 4, :], ACT.Copy).then_inc(sig("dn_kv"), 1)
                nc.scalar.activation(vtok[:, c, :], ps[:, 5, :], ACT.Copy).then_inc(sig("dn_kv"), 1)
                for l in range(1, LEVELS):
                    for d in range(2):
                        act.wait_ge(sig("dn_x"), 84 * g + 14 * q + 2 * l + d + 1)
                        if l > 1 or q:
                            act.wait_ge(sig("dn_ttb"), 72 * g + 12 * q + 2 * (l - 2) + d + 1)
                        nc.scalar.activation(xs[d][:, :, :].rearrange("p h n -> p (h n)"), ps[:, 4 + d, :], ACT.Copy)\
                            .then_inc(sig("dn_xs"), 1)
            act.wait_ge(sig("dn_orec"), 2 * g + 2)
            nc.scalar.activation(drs[:, :, :], drs[:, :, :], ACT.Sqrt).then_inc(sig("dn_oroot"), 1)

        def act_ssd(act, g):
            for q, c in enumerate(INTRA):
                act.wait_ge(sig("sd_tr"), past("sd_tr") + 6 * g + q + 1)
                nc.scalar.activation(xtok[:, c, :], ps[:, 0, :], ACT.Copy).then_inc(sig("sd_tok"), 1)
                nc.scalar.activation(Btok[:, c, :], ps[:, 1, 0:P], ACT.Copy).then_inc(sig("sd_tok"), 1)
                if q:
                    act.wait_ge(sig("sd_m0"), past("sd_m0") + 12 * g + 2 * q)
                    act.wait_ge(sig("sd_m1"), past("sd_m1") + 12 * g + 2 * q)
                nc.scalar.activation(bcs[:, :], ps[:, 2, 0:P], ACT.Copy).then_inc(sig("sd_tok"), 1)
                for d in range(2):
                    for f in range(2):
                        act.wait_ge(sig("sd_arg"), past("sd_arg") + 24 * g + 4 * q + 2 * d + f + 1)
                        nc.scalar.activation(Es[d][f][:, :, :], Es[d][f][:, :, :], ACT.Exp).then_inc(sig("sd_e"), 1)
                act.wait_ge(sig("sd_yb"), past("sd_yb") + 6 * g + q + 1)
                nc.scalar.activation(yacc[:, c, :], ps[:, 7, :], ACT.Copy).then_inc(sig("sd_y"), 1)
            for h in range(4):
                act.wait_ge(sig("ss_gated"), 4 * g + h + 1)
                if h >= 2:
                    act.wait_ge(sig("ss_ssum"), past("ss_ssum") + 4 * g + h - 1)
                nc.scalar.activation(ssq[h % 2][:, :], sx[:, h, :], ACT.Square).then_inc(sig("ss_sq"), 1)
            act.wait_ge(sig("ss_rec"), past("ss_rec") + 2 * g + 2)
            nc.scalar.activation(srs[:, :], srs[:, :], ACT.Sqrt).then_inc(sig("ss_root"), 1)

        def act_ffn(act, layer, w):
            for grp, n in enumerate(GROUPS):
                name = f"fi{layer}{grp}"

                def hidden(i, jj, u0):
                    act.wait_ge(sig("gemm_done"), 4 * i + S[name][3] + 2 * jj + 1)
                    act.wait_ge(sig("gemm_evac1"), 2 * i + u0 + jj)
                    nc.scalar.activation(sgb[jj][:, 0:w], pairbank(0, w), ACT.Silu).then_inc(sig("gemm_evac0"), 1)
                    act.wait_ge(sig("gemm_evac1"), 2 * i + u0 + jj + 2)
                    nc.scalar.activation(Gh[:, ds(2 * i + jj, 1), 0:w], hdb[jj][:, 0:w].unsqueeze(1), ACT.Copy)\
                        .then_inc(sig("hid_hi"), 1)
                act_stage(act, name, hidden)
                act_stage(act, f"fo{layer}{grp}", None, prefetch=not (layer and grp == 2))

        def act_units(act):
            for v, (w, span, _, _, _) in enumerate(UNITS):
                act.wait_ge(sig("un_ss"), v + 1)
                if v >= 2:
                    act.wait_ge(sig("un_done"), v - 1)
                rs = qrs[v % 2][:, 0:w]
                nc.scalar.activation(rs, banks(2 * (v % 2), 2, w), ACT.Ln, scale=1.0 / span, bias=epsc[:, 0:1])\
                    .then_inc(sig("un_root"), 1)
                act.wait_ge(sig("un_root"), v + 1)
                nc.scalar.activation(rs, rs, ACT.Exp, scale=-0.5).then_inc(sig("un_rec"), 1)

        def act_attention(act):
            U = attention_units()
            with act.Fori(0, 4) as i:
                def exps(u, da, hh, qt, pairs):
                    for x, (p, use) in enumerate(pairs):
                        act.wait_ge(sig(f"at_m{p}"), past(f"at_m{p}") + 12 * i + use + 1)
                        act.wait_ge(sig("at_tr"), 16 * i + u + 1)
                        st = stat[u % 2]
                        nc.scalar.activation(prb[2 * (u % 2) + x][:, :], pairbank(p, T), ACT.Exp,
                                             bias=st[:, x:x + 1], scale=(64 if da else 192) ** -0.5,
                                             accum_out=st[:, 2 + x:3 + x]).then_inc(sig(f"at_e{p}"), 1)

                def turned(u, da, hh, qt, pairs):
                    hu = u // 4
                    act.wait_ge(sig("at_tr"), 16 * i + u + 3)
                    if qt == 0:
                        act.wait_ge(sig("at_pv"), 4 * i + hu + 2)
                    nc.scalar.activation(pT[hu % 2][:, :, qt * P:(qt + 1) * P],
                                         banks(4, 2, T).rearrange("p (k n) -> p k n", k=NT), ACT.Copy)\
                        .then_inc(sig("at_pt"), 1)

                def take(hu):
                    act.wait_ge(sig("at_pv"), 4 * i + hu + 4)
                    nc.scalar.activation(att[:, ds(2 * i + (8 if hu % 2 else 0) + hu // 2, 1), :], ps[:, 6 + hu % 2:7 + hu % 2, :], ACT.Copy)\
                        .then_inc(sig("at_o"), 1)
                exps(*U[0])
                for x in U:
                    u = x[0]
                    if u < 15:
                        exps(*U[u + 1])
                    turned(*x)
                    if u % 4 == 0 and u:
                        take(u // 4 - 1)
                take(3)

        def scalar_program(act):
            act.sem_inc(sig("at_pt"), 1)
            act.sem_inc(sig("at_o"), 2)
            for e in (0, 1):
                act.sem_inc(sig(f"at_e{e}"), 1)
            act.wait_ge(sig("rows_clear"), 1)
            for dst, src in rows_from()[::2]:
                act.dma_start(dst, src).then_inc(sig("rows_in"), 16)
            act.wait_ge(sig("vec_ready"), 1)
            nc.scalar.activation(csil[:, :], vec[:, V_C:V_C + 16], ACT.Silu).then_inc(sig("silu_c"), 1)
            for u in range(1, 12, 2):
                act.wait_ge(sig("xt_done"), u + 1)
                act.wait_ge(sig("xt_evac"), u)
                t, hf = u // 2, u % 2
                nc.scalar.activation(xT[:, 4 * hf:4 * hf + 4, t * P:(t + 1) * P],
                                     ps[:, u % 6, :].rearrange("p (k n) -> p k n", k=4), ACT.Copy).then_inc(sig("xt_evac"), 1)
            phase_end(act, "act")
            phase_begin(act, 1)
            act_norm(act, 0, T, 0, between=lambda: hi_slab(act, 0, 0))
            hi_slab(act, 1, 0)
            phase_end(act, "act")
            phase_begin(act, 2)
            act.wait_ge(sig("gate_step"), 3)
            nc.scalar.activation(bet[:, :, :], gts[:, :, 0:16], ACT.Exp, scale=-1.0).then_inc(sig("gate_exp"), 1)
            nc.scalar.activation(spw[1][:, :, :], spw[1][:, :, :], ACT.Exp).then_inc(sig("gate_exp"), 1)
            nc.scalar.activation(alog[:, :], alog[:, :], ACT.Exp).then_inc(sig("gate_exp"), 1)
            nc.scalar.activation(lam[:, 2:4], lam[:, 0:2], ACT.Exp).then_inc(sig("gate_exp"), 1)
            act_in0(act)
            phase_end(act, "act")
            phase_begin(act, 3)
            act.wait_ge(sig("cum_ready"), 6)
            for j in (2, 3, 4):
                nc.scalar.activation(gcol[:, j, :, :], gcol[:, j, :, :], ACT.Exp).then_inc(sig("cum_exp"), 1)
            for base, part in ((3, act_deltanet), (5, act_ssd)):
                with act.Fori(0, 2) as g:
                    phase_begin(act, base + g)
                    part(act, g)
                    phase_end(act, "act")
            phase_begin(act, 7)
            act.wait_ge(sig("mix_out"), 80)
            hi_slab(act, S["out0"][0], 0)
            with act.Fori(0, 4) as i:
                for j in range(4):
                    act.wait_ge(sig(f"mix_in{j}"), 16 * i + 16)
                    nc.scalar.activation(Mh[:, ds(4 * i + j, 1), :], mst[j][:, :].unsqueeze(1), ACT.Copy).then_inc(sig("mix_hi"), 1)
            act_stage(act, "out0", None)
            phase_end(act, "act")
            phase_begin(act, 8)
            act_norm(act, 1, T, 1)
            phase_end(act, "act")
            phase_begin(act, 9)
            act_ffn(act, 0, T)
            phase_end(act, "act")
            phase_begin(act, 10)
            act_norm(act, 2, T, 2)
            phase_end(act, "act")
            phase_begin(act, 11)
            act_qkv1(act)
            phase_end(act, "act")
            phase_begin(act, 12)
            for e in (0, 1):
                act.wait_ge(sig(f"lstore{e}"), 16 * 13)
            for k in range(6):
                w = LAT if k < 4 else T
                if k >= 2:
                    act.wait_ge(sig("la_ss"), k - 1)
                nc.scalar.activation(lato[k % 2][:, 0:w], latr[:, k, 0:w], ACT.Square).then_inc(sig("la_sq"), 1)
            act.wait_ge(sig("la_ss"), 6)
            nc.scalar.activation(latn[:, 0, 0:LAT], ps[:, 6, :], ACT.Sqrt, scale=1.0 / 512, bias=epsc[:, 0:1]).then_inc(sig("la_root"), 1)
            nc.scalar.activation(latn[:, 1, :], banks(4, 2, T), ACT.Sqrt, scale=1.0 / 256, bias=epsc[:, 0:1]).then_inc(sig("la_root"), 1)
            for k in range(6):
                w = LAT if k < 4 else T
                act.wait_ge(sig("la_n"), k + 1)
                nc.scalar.activation(Hh[:, k, 0:w], latr[:, k, 0:w], ACT.Copy).then_inc(sig("la_hi"), 1)
            act_copy_stage(act, "uq1", LAT, 24, lambda i, jj, cc: scr_chunk(4 * i + 16 + 2 * jj + cc, LAT))
            act_copy_stage(act, "uk1", T, 36, lambda i, jj, cc: scr_chunk(4 * i + 28 + 2 * jj + cc, T))
            act_copy_stage(act, "uv1", T, 44, lambda i, jj, cc: v_block(1, i, jj, cc), prefetch=False)
            phase_end(act, "act")
            phase_begin(act, 13)
            act_units(act)
            phase_end(act, "act")
            phase_begin(act, 14)
            act_attention(act)
            phase_end(act, "act")
            phase_begin(act, 15)
            hi_slab(act, S["out1"][0], 0)
            for s in range(10):
                if s < 8:
                    if s >= 2:
                        act.wait_ge(sig("an_ss"), past("an_ss") + s - 1)
                    nc.scalar.activation(asq[s % 2][:, :], att[:, s, :], ACT.Square).then_inc(sig("an_sq"), 1)
                    nc.scalar.activation(Ah[:, 8 + s, :], att[:, 8 + s, :], ACT.Copy).then_inc(sig("an_hi"), 1)
                if 0 < s < 9:
                    act.wait_ge(sig("an_ss"), past("an_ss") + s)
                    if s >= 3:
                        act.wait_ge(sig("an_n"), past("an_n") + s - 2)
                    nc.scalar.activation(ars[(s - 1) % 2][:, :], ps[:, 4 + (s - 1) % 2, :], ACT.Sqrt, scale=1.0 / P,
                                         bias=epsc[:, 0:1]).then_inc(sig("an_root"), 1)
                if s >= 2:
                    act.wait_ge(sig("an_n"), past("an_n") + s - 1)
                    nc.scalar.activation(Ah[:, s - 2, :], att[:, s - 2, :], ACT.Copy).then_inc(sig("an_hi"), 1)
            act_stage(act, "out1", None)
            phase_end(act, "act")
            phase_begin(act, 16)
            act_norm(act, 3, LAT, 3)
            phase_end(act, "act")
            phase_begin(act, 17)
            act_ffn(act, 1, LAT)
            phase_end(act, "act")
            phase_begin(act, 18)
            for u in range(1, 8, 2):
                act.wait_ge(sig("yt_done"), u + 1)
                nc.scalar.activation(Y[:, u // 2, 512:1024], ps[:, u, :], ACT.Copy).then_inc(sig("y_odd"), 1)

        def copy_and_store(act, i, use, chunk, count, cc, w, dst):
            act.wait_ge(sig("gemm_done"), 4 * i + chunk + cc + 1)
            act.wait_ge(sig(f"lstore{cc}"), 32 * i + 16 * count + 16)
            nc.scalar.activation(lato[cc][:, 0:w], pairbank(cc, w), ACT.Copy)\
                .then_inc(sig(f"gemm_evac{cc}"), 1)
            act.wait_ge(sig(f"gemm_evac{cc}"), 2 * i + use + 2)
            src = lato[cc][:, 0:T].rearrange("p (t n) -> p t n", t=3) if dst.shape[1] == 3 else lato[cc][:, 0:w].unsqueeze(1)
            act.dma_start(dst, src).then_inc(sig(f"lstore{cc}"), 16)

        def act_copy_stage(act, name, w, count0, dst, prefetch=True):
            def evac(i, jj, u0):
                for cc in range(2):
                    copy_and_store(act, i, u0 + jj, S[name][3] + 2 * jj, count0 // 2 + jj, cc, w, dst(i, jj, cc))
            act_stage(act, name, evac, prefetch)

        def scr_chunk(chunk, w):
            return scr_p[:, ds(chunk, 1), 0:w]

        def v_block(x, i, jj, cc):
            return vscr[x].rearrange("(t p) n -> p t n", p=P)[:, 3 * cc:3 * cc + 3, ds(512 * i + 256 * jj, 256)]

        def act_qkv1(act):
            n0, ns, u0, c0 = S["qk1"]
            for part, w in ((0, LAT), (1, T)):
                def body(i, last):
                    for jj in range(2):
                        hi_slab(act, n0 + 4 * part + jj + 1, i, before=4 * i + c0 + 8 * part + 2 * jj)
                        for cc in range(2):
                            copy_and_store(act, i, u0 + 4 * part + jj, c0 + 8 * part + 2 * jj, 4 * part + jj, cc, w,
                                           scr_chunk(4 * i + 8 * part + 2 * jj + cc, w))
                loop(act, 2, body)
            act_copy_stage(act, "dv1", T, 16, lambda i, jj, cc: v_block(0, i, jj, cc))
            n0, ns, u0, c0 = S["lat1"]
            for jj in range(4):
                hi_slab(act, n0 + jj + 1, 0, before=c0 + 2 * jj)
                w = LAT if jj < 2 else T
                for cc in range(2 if jj < 3 else 1):
                    act.wait_ge(sig("gemm_done"), c0 + 2 * jj + cc + 1)
                    ins = nc.scalar.activation(latr[:, 2 * jj + cc, 0:w], pairbank(cc, w), ACT.Copy)
                    ins.then_inc(sig(f"gemm_evac{cc}"), 1)
            act.sem_inc(sig("gemm_evac1"), 1)
            act.wait_ge(sig("gemm_evac0"), u0 + 5)
            act.dma_start(scr_chunk(36, T), latr[:, 6:7, :]).then_inc(sig("kr_stored"), 16)

        def pool_stage(pool, name, prefetch=True):
            n0, ns, _, c0 = S[name]

            def body(i, last):
                for jj in range(2):
                    if not (last and jj == 1 and not prefetch):
                        lo_slab(pool, n0 + jj + 1, i)
            loop(pool, ns // 2, body)

        def pool_norm(pool, r, w):
            pool.wait_ge(sig("rec_done"), r + 1)
            for k in range(KD):
                if 8 * r + k >= 2:
                    pool.wait_ge(sig("mod_done"), 8 * r + k - 1)
                nc.gpsimd.tensor_tensor(nrm[k % 2][:, 0:w], xT[:, k, 0:w], rstd[:, 0:w], ALU.mult).then_inc(sig("nrm_done"), 1)

        def pool_deltanet(pool, g):
            pool.wait_ge(sig("cum_exp"), 3)
            for j in range(6):
                src = bet[:, :, :] if j == 5 else gcol[:, j, :, 0:16]
                nc.gpsimd.tensor_copy(dgg[j][:, :, :, :],
                                      src.rearrange("p c (d x) -> p d c x", d=2)[:, :, :, ds(4 * g, 4)]).then_inc(sig("dn_gg"), 1)
            pool.wait_ge(sig("dn_gg"), 6 * g + 6)
            for q, c in enumerate(INTRA):
                for d in range(2):
                    pool.wait_ge(sig("dn_e"), 12 * g + 2 * q + d + 1)
                    nc.gpsimd.tensor_tensor(EB[d][:, :, :], Ed[d][:, :, :],
                                            dgg[5][:, d, c, :].unsqueeze(2).broadcast_to([P, 4, P]), ALU.mult)\
                        .then_inc(sig("dn_eb"), 1)
                for l in range(LEVELS):
                    for d in range(2):
                        if l == 0:
                            pool.wait_ge(sig("dn_at"), 12 * g + 2 * q + d + 1)
                        if l >= 2 or q:
                            back = 84 * g + 14 * q + 2 * (l - 2) + d + 1
                            pool.wait_ge(sig("dn_x"), back)
                        if l == 2:
                            pool.wait_ge(sig("dn_tt0"), 12 * g + 2 * q + d + 1)
                        nc.gpsimd.tensor_tensor(Am[d][l % 2][:, :, :], AT[d][:, :, :],
                                                level(d, l).unsqueeze(1).broadcast_to([P, 4, P]), ALU.mult)\
                            .then_inc(sig("dn_as"), 1)
                    if l == 0:
                        for d in range(2):
                            pool.wait_ge(sig("dn_as"), 84 * g + 14 * q + d + 1)
                            nc.gpsimd.tensor_tensor(TTs[:, c, d, :, :], ident.unsqueeze(1).broadcast_to([P, 4, P]),
                                                    Am[d][0][:, :, :], ALU.subtract).then_inc(sig("dn_tt0"), 1)
            for k in range(NT):
                for d in range(2):
                    c = ORDER[d][k]
                    if 0 < k < NT - 1:
                        pool.wait_ge(sig("rec_ks"), 10 * g + 2 * (k - 1) + d + 1)
                        pool.wait_ge(sig("rec_qs"), 10 * g + 2 * (k - 1) + d + 1)
                        pool.wait_ge(sig("rec_s"), 10 * g + 2 * (k - 1) + d + 1)
                        nc.gpsimd.tensor_tensor(Sst[d][:, :, :], Sst[d][:, :, :],
                                                dgg[4][:, d, c, :].unsqueeze(2).broadcast_to([P, 4, P]), ALU.mult)\
                            .then_inc(sig("rec_sd"), 1)
                for d in range(2):
                    c = ORDER[d][k]
                    if k < NT - 1:
                        pool.wait_ge(sig("rec_vn"), 12 * g + 2 * k + d + 1)
                        if k:
                            pool.wait_ge(sig("rec_su"), 10 * g + 2 * (k - 1) + d + 1)
                        nc.gpsimd.tensor_tensor(vs[d][:, :, :], vn[d][:, :, :],
                                                dgg[3][:, d, c, :].unsqueeze(2).broadcast_to([P, 4, P]), ALU.mult)\
                            .then_inc(sig("rec_vs"), 1)
            pool.wait_ge(sig("rec_o"), 12 * g + 12)
            pool.wait_ge(sig("rec_acc"), 6 * g + 6)
            flat = dk[:, :, :].rearrange("p h t -> p (h t)")
            of = dv[:, :, :].rearrange("p h t -> p (h t)")
            nc.gpsimd.tensor_tensor(flat, of, of, ALU.mult).then_inc(sig("dn_osq"), 1)

        def pool_ssd(pool, g):
            pool.wait_ge(sig("cum_exp"), 3)
            for j in range(6):
                src = dts[:, :, :] if j == 5 else gcol[:, j, :, 16:48]
                nc.gpsimd.tensor_copy(sgg[j][:, :, :, :],
                                      src.rearrange("p c (d x) -> p d c x", d=2)[:, :, :, ds(8 * g, 8)]).then_inc(sig("sd_gg"), 1)
            pool.wait_ge(sig("sd_gg"), past("sd_gg") + 6 * g + 6)
            for q, c in enumerate(INTRA):
                pool.wait_ge(sig("sd_tok"), past("sd_tok") + 18 * g + 3 * q + 3)
                for d in range(2):
                    nc.gpsimd.tensor_tensor(xdt[:, d, c, :].rearrange("p (h n) -> p h n", h=8),
                                            xtok[:, c, :].rearrange("p (h n) -> p h n", h=8),
                                            sgg[5][:, d, c, :].unsqueeze(2).broadcast_to([P, 8, 64]), ALU.mult)\
                        .then_inc(sig("sd_xdt"), 1)
                for f in range(2):
                    pool.wait_ge(sig("sd_e"), past("sd_e") + 24 * g + 4 * q + 2 + f + 1)
                    nc.gpsimd.tensor_tensor(Es[1][f][:, :, :], Es[1][f][:, :, :],
                                            bcs[:, :].unsqueeze(1).broadcast_to([P, 4, P]), ALU.mult).then_inc(sig("sd_m1"), 1)
            for k in range(NT - 1):
                for d in range(2):
                    c = ORDER[d][k]
                    if k:
                        pool.wait_ge(sig("ss_su"), past("ss_su") + 10 * g + 2 * (k - 1) + d + 1)
                    nc.gpsimd.tensor_tensor(sxs[d][:, :].rearrange("p (h n) -> p h n", h=8),
                                            xdt[:, d, c, :].rearrange("p (h n) -> p h n", h=8),
                                            sgg[3][:, d, c, :].unsqueeze(2).broadcast_to([P, 8, 64]), ALU.mult)\
                        .then_inc(sig("ss_x"), 1)

        def pool_units(pool):
            for r, gain in enumerate(ROTATING):
                nc.gpsimd.tensor_scalar(gcos[:, r, :], cos, vec[:, gain:gain + 1], None, ALU.mult).then_inc(sig("un_tab"), 1)
            pool.wait_ge(sig("un_tab"), 4)
            for n in range(len(UNITS) + 1):
                if n < len(UNITS):
                    w = UNITS[n][0]
                    pool.wait_ge(sig(f"un_in{n % 4}"), 16 * (n // 4) + 16)
                    if n >= 2:
                        pool.wait_ge(sig("un_ss"), n - 1)
                    nc.gpsimd.tensor_tensor(qsq[n % 2][:, 0:w], qn[n % 4][:, 0:w], qn[n % 4][:, 0:w], ALU.mult).then_inc(sig("un_sq"), 1)
                v = n - 1
                if n == 0 or UNITS[v][3] is None:
                    continue
                _, _, _, r, rv = UNITS[v]
                if rv >= 2:
                    pool.wait_ge(sig("un_add"), rv - 1)
                nc.gpsimd.tensor_tensor(qcos[rv % 2][:, :], qn[v % 4][:, 0:LAT], gcos[:, r, :], ALU.mult).then_inc(sig("un_cos"), 1)

        def gpsimd_program(pool):
            pool.sem_inc(sig("slab_lo"), 2)
            pool.sem_inc(sig("ada_used"), 3)
            nc.gpsimd.memset(epsc[:, 0:1], EPS)
            nc.gpsimd.memset(epsc[:, 1:2], P * EPS)
            nc.gpsimd.memset(rows[:, :, :], 0.0).then_inc(sig("rows_clear"), 1)
            pool.wait_ge(sig("rows_in"), 16 * len(rows_from()))
            r0 = V_SSDD % P
            nc.gpsimd.tensor_copy(rows[r0:r0 + 8, V_SSDD // P, :].rearrange("r (two n) -> r two n", two=2),
                                  drow[r0:r0 + 8, :].unsqueeze(2).broadcast_to([8, 2, 64])).then_inc(sig("rows_spread"), 1)
            phase_end(pool, "pool")
            phase_begin(pool, 1)
            lo_slab(pool, 0, 0)
            pool_norm(pool, 0, T)
            lo_slab(pool, 1, 0)
            phase_end(pool, "pool")
            phase_begin(pool, 2)
            for j in range(2):
                for e in (0, 514, 772):
                    nc.gpsimd.memset(ubuf[j][:, e:e + 2], 0.0).then_inc(sig("edges"), 1)
            pool_stage(pool, "in0", prefetch=False)
            phase_end(pool, "pool")
            for base, part in ((3, pool_deltanet), (5, pool_ssd)):
                with pool.Fori(0, 2) as g:
                    phase_begin(pool, base + g)
                    part(pool, g)
                    phase_end(pool, "pool")
            phase_begin(pool, 7)
            lo_slab(pool, S["out0"][0], 0)
            with pool.Fori(0, 4) as i:
                for j in range(4):
                    pool.wait_ge(sig("mix_hi"), 4 * i + j + 1)
                    nc.gpsimd.tensor_tensor(Ml[:, ds(4 * i + j, 1), :], mst[j][:, :].unsqueeze(1),
                                            Mh[:, ds(4 * i + j, 1), :].bitcast(f32), ALU.subtract).then_inc(sig("mix_lo"), 1)
            pool_stage(pool, "out0")
            phase_end(pool, "pool")
            phase_begin(pool, 8)
            pool_norm(pool, 1, T)
            phase_end(pool, "pool")
            phase_begin(pool, 9)
            for grp in range(3):
                pool_stage(pool, f"fi0{grp}")
                pool_stage(pool, f"fo0{grp}")
            phase_end(pool, "pool")
            phase_begin(pool, 10)
            pool_norm(pool, 2, T)
            phase_end(pool, "pool")
            phase_begin(pool, 11)
            for name in ("qk1", "dv1", "lat1"):
                pool_stage(pool, name)
            phase_end(pool, "pool")
            phase_begin(pool, 12)
            pool_stage(pool, "uq1")
            pool_stage(pool, "uk1")
            pool_stage(pool, "uv1", prefetch=False)
            phase_end(pool, "pool")
            phase_begin(pool, 13)
            pool_units(pool)
            phase_end(pool, "pool")
            phase_begin(pool, 14)
            phase_end(pool, "pool")
            phase_begin(pool, 15)
            lo_slab(pool, S["out1"][0], 0)
            for s, k in enumerate(ATT_ORDER):
                pool.wait_ge(sig("an_hi"), past("an_hi") + s + 1)
                nc.gpsimd.tensor_tensor(Al[:, k, :], att[:, k, :], Ah[:, k, :].bitcast(f32), ALU.subtract).then_inc(sig("an_lo"), 1)
            pool_stage(pool, "out1")
            phase_end(pool, "pool")
            phase_begin(pool, 16)
            pool_norm(pool, 3, LAT)
            phase_end(pool, "pool")
            phase_begin(pool, 17)
            for grp in range(3):
                pool_stage(pool, f"fi1{grp}")
                pool_stage(pool, f"fo1{grp}", prefetch=(grp < 2))
            phase_end(pool, "pool")

        def dve_norm(dve, r, w, layer, part, gain):
            for x, mod in enumerate((modl, modc)):
                nc.vector.scalar_tensor_tensor(amod[:, x, :], mod[:, 48 * layer + 8 * (part + 1):48 * layer + 8 * (part + 2)],
                                               1.0, vec[:, gain:gain + 8], ALU.add, ALU.mult).then_inc(sig("amod_done"), 1)
            dve.wait_ge(sig("rstd_done"), r + 1)
            nc.vector.reciprocal(rstd[:, 0:w], rstd[:, 0:w]).then_inc(sig("rec_done"), 1)
            dve.wait_ge(sig("amod_done"), 2 * r + 2)

            def low(k):
                dve.wait_ge(sig("hi_done"), 8 * r + k + 1)
                nc.vector.tensor_tensor(Hl[:, k, 0:w], mdl[k % 2][:, 0:w], Hh[:, k, 0:w].bitcast(f32), ALU.subtract)\
                    .then_inc(sig("lo_done"), 1)
            for k in range(KD):
                if k >= 2:
                    low(k - 2)
                    dve.wait_ge(sig("lo_done"), 8 * r + k - 1)
                dve.wait_ge(sig("nrm_done"), 8 * r + k + 1)
                for x, (t0, t1, mod) in enumerate(((0, LAT, modl), (LAT, w, modc))):
                    if t1 > t0:
                        c = 48 * layer + 8 * part + k
                        ins = nc.vector.tensor_scalar(mdl[k % 2][:, t0:t1], nrm[k % 2][:, t0:t1], amod[:, x, k:k + 1],
                                                      mod[:, c:c + 1], ALU.mult, ALU.add)
                ins.then_inc(sig("mod_done"), 1)
            low(6)
            low(7)

        def dve_ada(dve, q, it, wts=ada, acc=aacc, base=None):
            dve.wait_ge(sig(f"ada_in{q}"), 16 * it + 16)
            if type(it) is not int or it:
                dve.wait_ge(sig("ada_sum"), 3 * it + q - 2)
            base = 48 * it + 16 * q - 48 if base is None else base
            for k in range(KD):
                for x in range(2):
                    o, w, c = acc[q][:, x, :], wts[q][:, k, :], csil[:, 8 * x + k:8 * x + k + 1]
                    if k == 0:
                        ins = nc.vector.tensor_scalar(o, w, c, None, ALU.mult)
                    else:
                        dve.wait_ge(sig("ada_step"), base + 2 * k + x - 1)
                        ins = nc.vector.scalar_tensor_tensor(o, w, c, o, ALU.mult, ALU.add)
                    ins.then_inc(sig("ada_step"), 1)
            dve.wait_ge(sig("ada_step"), base + 16)
            dve.sem_inc(sig("ada_used"), 1)

        def dve_mod(dve, it):
            dve.wait_ge(sig("ada_sum"), 3 * it + 3)
            src = ps[:, 4, 0:12].rearrange("p (c s) -> p c s", s=2)
            nc.vector.tensor_tensor(modl[:, ds(6 * it, 6)], src[:, :, 0], vec[:, ds(6 * it, 6)], ALU.add)
            nc.vector.tensor_tensor(modc[:, ds(6 * it, 6)], src[:, :, 1], vec[:, ds(6 * it, 6)], ALU.add)\
                .then_inc(sig("mod_evac"), 1)

        def dve_gates(dve):
            link = Link(dve, "gate_step")
            dve.wait_ge(sig("gemm_done"), 1)
            link(nc.vector.tensor_copy(gts[:, :, :], ps[:, 5, 0:NT * 64].rearrange("p (c n) -> p c n", n=64)))
            x, ax = spw[0], spw[1]
            link(nc.vector.tensor_tensor(x[:, :, :], gts[:, :, 16:64], gbias[:, :].unsqueeze(1).broadcast_to([P, NT, 48]), ALU.add))
            link(nc.vector.scalar_tensor_tensor(ax[:, :, :].rearrange("p c n -> p (c n)"), x[:, :, :].rearrange("p c n -> p (c n)"),
                                                -1.0, x[:, :, :].rearrange("p c n -> p (c n)"), ALU.mult, ALU.min))
            dve.wait_ge(sig("gate_exp"), 4)
            f = [t[:, :, :].rearrange("p c n -> p (c n)") for t in spw]
            link(nc.vector.tensor_scalar(f[2], f[1], 2.0, None, ALU.add))
            link(nc.vector.reciprocal(f[3], f[2]))
            link(nc.vector.tensor_tensor(f[2], f[1], f[3], ALU.mult))
            link(nc.vector.tensor_tensor(f[3], f[2], f[2], ALU.mult))
            link(nc.vector.tensor_scalar(f[4], f[3], 1.0 / 17, None, ALU.mult))
            for m in (15, 13, 11, 9, 7, 5, 3):
                link(nc.vector.scalar_tensor_tensor(f[4], f[4], 1.0 / m, f[3], ALU.add, ALU.mult))
            link(nc.vector.scalar_tensor_tensor(f[4], f[4], 1.0, f[2], ALU.add, ALU.mult))
            link(nc.vector.tensor_scalar(f[5], f[0], 0.0, None, ALU.max))
            link(nc.vector.scalar_tensor_tensor(f[5], f[4], 2.0, f[5], ALU.mult, ALU.add))
            link(nc.vector.tensor_copy(dts[:, :, :], spw[5][:, :, 16:48]))
            link(nc.vector.tensor_tensor(gcol[:, 1, :, :], spw[5][:, :, :], alog[:, :].unsqueeze(1).broadcast_to([P, NT, 48]), ALU.mult))
            link(nc.vector.tensor_scalar(gcol[:, 0, :, :], gcol[:, 1, :, :], -1.0, None, ALU.mult))
            link(nc.vector.tensor_scalar(bet[:, :, :], bet[:, :, :], 1.0, None, ALU.add))
            link(nc.vector.reciprocal(bet[:, :, :], bet[:, :, :]))
            link(nc.vector.tensor_tensor(lam[:, 4:5], lam[:, 2:3], lam[:, 3:4], ALU.subtract))
            link(nc.vector.tensor_scalar(lam[:, 5:6], lam[:, 4:5], LAMBDA_INIT, -1.0, ALU.add, ALU.mult))
            link(nc.vector.tensor_scalar(lam[:, 6:7], vec[:, V_DASUB:V_DASUB + 1], 1.0 - LAMBDA_INIT, None, ALU.mult))

        def dve_conv(dve, i, modulate=True):
            for r in range(4):
                if r < 3 and modulate:
                    dve_ada(dve, r, i + 3)
                m, cc = 4 * i + r, r % 2
                dve.wait_ge(sig("tap0"), 4 * i + r + 1)
                for k in range(1, CONV_K):
                    col = 256 + P * (k // 3) + 36 * (k % 3)
                    w = vec[:, ds(col + m, 1)]
                    if k > 1:
                        dve.wait_ge(sig("conv_step"), 16 * i + 4 * r + k + 7)
                    nc.vector.scalar_tensor_tensor(ybuf[cc][:, 0:770], ubuf[cc][:, k:k + 770], w, ybuf[cc][:, 0:770],
                                                   ALU.mult, ALU.add).then_inc(sig("conv_step"), 1)

        def dve_deltanet(dve, g):
            for x in range(4):
                flat = ATs[:, :, :, :, :].rearrange("p c d h n -> p (c d h n)")[:, x * 1536:(x + 1) * 1536]
                dve.wait_ge(sig("dn_rec"), 4 * g + x + 1)
                sf = (dq, dk)[x // 2][:, 2 * (x % 2):2 * (x % 2) + 2, :].rearrange("p h t -> p (h t)")
                nc.vector.tensor_tensor(sf, sf, flat, ALU.mult).then_inc(sig("dn_unit"), 1)
            dve.wait_ge(sig("dn_gg"), 6 * g + 6)
            dve.wait_ge(sig("dn_unit"), 4 * g + 4)
            for q, c in enumerate(INTRA):
                for d in range(2):
                    dve.wait_ge(sig("dn_d"), 12 * g + 2 * q + d + 1)
                    nc.vector.scalar_tensor_tensor(Ed[d][:, :, :], ps[:, 2 + d, :].rearrange("p (h n) -> p h n", h=4), 0.0,
                                                   neg[d].unsqueeze(1).broadcast_to([P, 4, P]), ALU.min, ALU.add)\
                        .then_inc(sig("dn_arg"), 1)
                dve.wait_ge(sig("dn_kk"), 6 * g + q + 1)
                for d in range(2):
                    dve.wait_ge(sig("dn_e"), 12 * g + 2 * q + d + 1)
                    nc.vector.tensor_tensor(ATs[:, c, d, :, :], ps[:, 1, :].rearrange("p (h n) -> p h n", h=4), Ed[d][:, :, :], ALU.mult)
                    dve.wait_ge(sig("dn_eb"), 12 * g + 2 * q + d + 1)
                    if q:
                        dve.wait_ge(sig("dn_as"), 84 * g + 14 * q - 1 + d)
                    nc.vector.tensor_tensor(AT[d][:, :, :], ps[:, 0, :].rearrange("p (h n) -> p h n", h=4), EB[d][:, :, :], ALU.mult)\
                        .then_inc(sig("dn_at"), 1)
                for d in range(2):
                    dve.wait_ge(sig("dn_x"), 84 * g + 14 * q + d + 1)
                    nc.vector.tensor_tensor(Tm[d][:, :, :], ident.unsqueeze(1).broadcast_to([P, 4, P]),
                                            ps[:, 4 + d, :].rearrange("p (h n) -> p h n", h=4), ALU.subtract).then_inc(sig("dn_t"), 1)
                for l in range(1, LEVELS):
                    s = 1 << l
                    for d in range(2):
                        if l < LEVELS - 1:
                            dve.wait_ge(sig("dn_tb"), 60 * g + 10 * q + 2 * (l - 1) + d + 1)
                            dve.wait_ge(sig("dn_t"), 72 * g + 12 * q + 2 * (l - 1) + d + 1)
                            v = sets(Tm[d][:, :, :].rearrange("p h n -> p (h n)"), l, d)
                            nc.vector.tensor_tensor(v, v, ps[:, 6 + d, 0:256].rearrange("p (n s) -> p n s", s=s), ALU.subtract)\
                                .then_inc(sig("dn_t"), 1)
                        dve.wait_ge(sig("dn_ttb"), 72 * g + 12 * q + 2 * (l - 1) + d + 1)
                        if l > 1:
                            dve.wait_ge(sig("dn_tt"), 72 * g + 12 * q + 2 * (l - 2) + d + 1)
                        v = sets(TTs[:, c, d, :, :].rearrange("p h n -> p (h n)"), l, 1 - d)
                        nc.vector.tensor_tensor(v, v, ps[:, 2 + d, 0:256].rearrange("p (n s) -> p n s", s=s), ALU.subtract)\
                            .then_inc(sig("dn_tt"), 1)
            oacc = dv[:, :, :].rearrange("p h t -> p (h t)").rearrange("p (c h n) -> p c h n", c=NT, h=4)

            def bc(j, d, c):
                return dgg[j][:, d, c, :].unsqueeze(2).broadcast_to([P, 4, P])

            def bank(b):
                return ps[:, b, :].rearrange("p (h n) -> p h n", h=4)
            seen = set()
            dve.wait_ge(sig("dn_kv"), 12 * g + 12)
            for k in range(NT):
                cs = [ORDER[d][k] for d in range(2)]
                for d in range(2):
                    c = cs[d]
                    if k:
                        dve.wait_ge(sig("rec_ks"), 10 * g + 2 * (k - 1) + d + 1)
                        nc.vector.tensor_tensor(rr[d][:, :, :], bank(d), bc(2, d, c), ALU.mult).then_inc(sig("rec_m"), 1)
                        dve.wait_ge(sig("rec_m"), 10 * g + 2 * (k - 1) + d + 1)
                        nc.vector.tensor_tensor(rr[d][:, :, :], vtok[:, c, :].rearrange("p (h n) -> p h n", h=4), rr[d][:, :, :],
                                                ALU.subtract).then_inc(sig("rec_r"), 1)
                for d in range(2):
                    dve.wait_ge(sig("rec_v"), 12 * g + 2 * k + d + 1)
                    nc.vector.tensor_tensor(vn[d][:, :, :], bank(4 + d), bc(5, d, cs[d]), ALU.mult).then_inc(sig("rec_vn"), 1)
                for d in range(2):
                    if k:
                        dve.wait_ge(sig("rec_qs"), 10 * g + 2 * (k - 1) + d + 1)
                        nc.vector.tensor_tensor(to[d][:, :, :], bank(2 + d), bc(2, d, cs[d]), ALU.mult).then_inc(sig("rec_t"), 1)
                for d in range(2):
                    if k < NT - 1:
                        dve.wait_ge(sig("rec_su"), 10 * g + 2 * k + d + 1)
                        if k:
                            dve.wait_ge(sig("rec_sd"), 8 * g + 2 * (k - 1) + d + 1)
                            nc.vector.tensor_tensor(Sst[d][:, :, :], Sst[d][:, :, :], bank(6 + d), ALU.add).then_inc(sig("rec_s"), 1)
                        else:
                            nc.vector.tensor_copy(Sst[d][:, :, :], bank(6 + d)).then_inc(sig("rec_s"), 1)
                for d in range(2):
                    c = cs[d]
                    dve.wait_ge(sig("rec_ob"), 12 * g + 2 * k + d + 1)
                    if k:
                        dve.wait_ge(sig("rec_t"), 10 * g + 2 * (k - 1) + d + 1)
                        if c in seen:
                            nc.vector.tensor_tensor(to[d][:, :, :], to[d][:, :, :], bank(4 + d), ALU.add).then_inc(sig("rec_o"), 1)
                            dve.wait_ge(sig("rec_o"), 12 * g + 2 * k + d + 1)
                            nc.vector.tensor_tensor(oacc[:, c, :, :], oacc[:, c, :, :], to[d][:, :, :], ALU.add).then_inc(sig("rec_acc"), 1)
                        else:
                            nc.vector.tensor_tensor(oacc[:, c, :, :], to[d][:, :, :], bank(4 + d), ALU.add).then_inc(sig("rec_o"), 1)
                    else:
                        nc.vector.tensor_copy(oacc[:, c, :, :], bank(4 + d)).then_inc(sig("rec_o"), 1)
                    seen.add(c)
            dve.wait_ge(sig("dn_osq"), g + 1)
            nc.vector.tensor_reduce(drs[:, :, :], dk[:, :, :].rearrange("p h t -> p (h t)").rearrange("p (c h n) -> p c h n", c=NT, h=4),
                                    AX.X, ALU.add).then_inc(sig("dn_ored"), 1)
            dve.wait_ge(sig("dn_ored"), g + 1)
            nc.vector.tensor_scalar(drs[:, :, :], drs[:, :, :], 1.0 / P, EPS, ALU.mult, ALU.add).then_inc(sig("dn_orec"), 1)
            dve.wait_ge(sig("dn_orec"), 2 * g + 1)
            nc.vector.reciprocal(drs[:, :, :], drs[:, :, :]).then_inc(sig("dn_orec"), 1)
            dve.wait_ge(sig("dn_oroot"), g + 1)
            nc.vector.tensor_tensor(oacc, oacc, drs[:, :, :].unsqueeze(3).broadcast_to([P, NT, 4, P]), ALU.mult).then_inc(sig("dn_on"), 1)
            dve.wait_ge(sig("ld_dz"), 16 * g + 16)
            for c in range(NT):
                dve.wait_ge(sig("dn_ot"), 6 * g + c + 1)
                nc.vector.scalar_tensor_tensor(dq[:, :, c * P:(c + 1) * P], bank(4 + c % 2), vec[:, V_DNN:V_DNN + 1],
                                               dq[:, :, c * P:(c + 1) * P], ALU.mult, ALU.mult).then_inc(sig("dn_og"), 1)

        def dve_ssd(dve, g):
            dve.wait_ge(sig("sd_gg"), past("sd_gg") + 6 * g + 6)
            dve.wait_ge(sig("sd_in"), 48 * g + 48)
            for q, c in enumerate(INTRA):
                for d in range(2):
                    for f in range(2):
                        dve.wait_ge(sig("sd_d"), past("sd_d") + 24 * g + 4 * q + 2 * d + f + 1)
                        if q:
                            dve.wait_ge(sig("sd_yb"), past("sd_yb") + 6 * g + q)
                        nc.vector.scalar_tensor_tensor(Es[d][f][:, :, :], ps[:, 3 + 2 * d + f, :].rearrange("p (h n) -> p h n", h=4), 0.0,
                                                       neg[d].unsqueeze(1).broadcast_to([P, 4, P]), ALU.min, ALU.add)\
                            .then_inc(sig("sd_arg"), 1)
                dve.wait_ge(sig("sd_tok"), past("sd_tok") + 18 * g + 3 * q + 3)
                for f in range(2):
                    dve.wait_ge(sig("sd_e"), past("sd_e") + 24 * g + 4 * q + f + 1)
                    nc.vector.tensor_tensor(Es[0][f][:, :, :], Es[0][f][:, :, :], bcs[:, :].unsqueeze(1).broadcast_to([P, 4, P]),
                                            ALU.mult).then_inc(sig("sd_m0"), 1)
            dve.wait_ge(sig("sd_y"), past("sd_y") + 6 * g + 6)
            acc = 0
            for k in range(NT):
                for d in range(2):
                    c = ORDER[d][k]

                    def e(v):
                        return v.rearrange("p (h n) -> p h n", h=8)

                    def bc(j):
                        return sgg[j][:, d, c, :].unsqueeze(2).broadcast_to([P, 8, 64])
                    if k:
                        dve.wait_ge(sig("ss_ch"), past("ss_ch") + 10 * g + 2 * (k - 1) + d + 1)
                        nc.vector.tensor_tensor(e(sty[d][:, :]), e(ps[:, d, :]), bc(2), ALU.mult).then_inc(sig("ss_t"), 1)
                    if k < NT - 1:
                        if k:
                            nc.vector.tensor_tensor(e(hst[d][:, :]), e(hst[d][:, :]), bc(4), ALU.mult).then_inc(sig("ss_sd"), 1)
                            dve.wait_ge(sig("ss_sd"), past("ss_sd") + 8 * g + 2 * (k - 1) + d + 1)
                        dve.wait_ge(sig("ss_su"), past("ss_su") + 10 * g + 2 * k + d + 1)
                        if k:
                            nc.vector.tensor_tensor(hst[d][:, :], hst[d][:, :], ps[:, 2 + d, :], ALU.add).then_inc(sig("ss_s"), 1)
                        else:
                            nc.vector.tensor_copy(hst[d][:, :], ps[:, 2 + d, :]).then_inc(sig("ss_s"), 1)
                    if k:
                        dve.wait_ge(sig("ss_t"), past("ss_t") + 10 * g + 2 * (k - 1) + d + 1)
                        if acc:
                            dve.wait_ge(sig("ss_acc"), past("ss_acc") + 10 * g + acc)
                        nc.vector.tensor_tensor(yacc[:, c, :], yacc[:, c, :], sty[d][:, :], ALU.add).then_inc(sig("ss_acc"), 1)
                        acc += 1
            for h in range(4):
                nc.vector.tensor_scalar(sx[:, h, :], sx[:, h, :], vec[:, ds(V_SSDD + 4 * g + h, 1)], None, ALU.mult).then_inc(sig("ss_dx"), 1)
            dve.wait_ge(sig("ss_dx"), 4 * g + 4)
            for c in range(NT):
                dve.wait_ge(sig("ss_tt"), past("ss_tt") + 6 * g + c + 1)
                v = sx[:, :, c * P:(c + 1) * P]
                nc.vector.tensor_tensor(v, v, ps[:, 4 + c % 2, :].rearrange("p (h n) -> p h n", h=4), ALU.add).then_inc(sig("ss_yt"), 1)
            dve.wait_ge(sig("ss_yt"), past("ss_yt") + 6 * g + 6)
            dve.wait_ge(sig("sd_z"), 16 * g + 16)
            for h in range(4):
                nc.vector.tensor_tensor(sx[:, h, :], sx[:, h, :], sz[:, h, :], ALU.mult).then_inc(sig("ss_gated"), 1)
            dve.wait_ge(sig("ss_ssum"), past("ss_ssum") + 4 * g + 4)
            nc.vector.tensor_scalar(srs[:, :], banks(6, 2, T), 1.0 / 512, EPS, ALU.mult, ALU.add).then_inc(sig("ss_rec"), 1)
            dve.wait_ge(sig("ss_rec"), past("ss_rec") + 2 * g + 1)
            nc.vector.reciprocal(srs[:, :], srs[:, :]).then_inc(sig("ss_rec"), 1)
            dve.wait_ge(sig("ss_root"), past("ss_root") + g + 1)
            dve.wait_ge(sig("ss_gated"), 4 * g + 4)
            for h in range(4):
                nc.vector.scalar_tensor_tensor(sx[:, h, :], sx[:, h, :], vec[:, ds(V_SSDN + 4 * g + h, 1)], srs[:, :],
                                               ALU.mult, ALU.mult).then_inc(sig("ss_out"), 1)

        def residual(dve, use, pair, layer, part, k, w):
            dve.wait_ge(sig("gemm_done"), use)
            c = 48 * layer + 8 * part
            for t0, t1, mod in ((0, LAT, modl), (LAT, w, modc)):
                if t1 > t0:
                    x = xT[:, ds(k, 1), t0:t1].rearrange("p a t -> p (a t)")
                    ins = nc.vector.scalar_tensor_tensor(x, pairbank(pair, w)[:, t0:t1], mod[:, ds(k + c, 1)], x, ALU.mult, ALU.add)
            ins.then_inc(sig(f"gemm_evac{pair}"), 1)

        def dve_out(dve, name, layer, w):
            n0, ns, u0, c0 = S[name]
            with dve.Fori(0, 4) as i:
                for jj in range(2):
                    residual(dve, 2 * i + c0 + jj + 1, jj, layer, 2, 2 * i + jj, w)

        def dve_ffn(dve, layer, w):
            for grp, n in enumerate(GROUPS):
                first = 22 * layer + sum(GROUPS[:grp])
                n0, ns, u0, c0 = S[f"fi{layer}{grp}"]
                with dve.Fori(0, n // 2) as i:
                    for jj in range(2):
                        dve.wait_ge(sig("gemm_done"), 4 * i + c0 + 2 * jj + 2)
                        dve.wait_ge(sig("gemm_evac0"), 2 * i + u0 + jj + 2)
                        nc.vector.tensor_tensor(hdb[jj][:, 0:w], sgb[jj][:, 0:w], pairbank(1, w), ALU.mult)\
                            .then_inc(sig("gemm_evac1"), 1)
                        dve.wait_ge(sig("hid_hi"), 2 * i + first + jj + 1)
                        nc.vector.tensor_tensor(Gl[:, ds(2 * i + jj, 1), 0:w], hdb[jj][:, 0:w].unsqueeze(1),
                                                Gh[:, ds(2 * i + jj, 1), 0:w].bitcast(f32), ALU.subtract).then_inc(sig("hid_lo"), 1)
                n0, ns, u0, c0 = S[f"fo{layer}{grp}"]
                with dve.Fori(0, 2) as i:
                    for jj in range(2):
                        for cc in range(2):
                            residual(dve, 4 * i + c0 + 2 * jj + cc + 1, cc, layer, 5, 4 * i + 2 * jj + cc, w)

        def dve_units(dve):
            for r, gain in enumerate(ROTATING):
                nc.vector.tensor_scalar(rotg[:, r, :], rot, vec[:, gain:gain + 1], None, ALU.mult).then_inc(sig("un_mat"), 1)
            for v, (w, span, gain, r, rv) in enumerate(UNITS):
                x, rs, q = qn[v % 4], qrs[v % 2], qsin[rv % 2]
                if r is not None:
                    dve.wait_ge(sig("un_rot"), rv + 1)
                    if rv >= 2:
                        dve.wait_ge(sig("un_done"), v - 1)
                    nc.vector.tensor_tensor(q[:, :], ps[:, 4 + rv % 4, :], sin, ALU.mult).then_inc(sig("un_sin"), 1)
                if r is not None:
                    dve.wait_ge(sig("un_sin"), rv + 1)
                    dve.wait_ge(sig("un_cos"), rv + 1)
                    nc.vector.tensor_tensor(q[:, :], q[:, :], qcos[rv % 2][:, :], ALU.add).then_inc(sig("un_add"), 1)
                dve.wait_ge(sig("un_rec"), v + 1)
                t0 = 0
                if r is not None:
                    t0 = LAT
                    dve.wait_ge(sig("un_add"), rv + 1)
                    ins = nc.vector.tensor_tensor(x[:, 0:LAT], q[:, :], rs[:, 0:LAT], ALU.mult)
                if w > t0:
                    ins = nc.vector.scalar_tensor_tensor(x[:, t0:w], x[:, t0:w], vec[:, gain:gain + 1], rs[:, t0:w],
                                                         ALU.mult, ALU.mult)
                ins.then_inc(sig("un_done"), 1)

        def dve_attention(dve):
            U = attention_units()
            with dve.Fori(0, 4) as i:
                def maxima(xs, u, da, hh, qt, pairs):
                    st = stat[u % 2]
                    for x, (p, use) in [(x, pairs[x]) for x in xs if x < len(pairs)]:
                        dve.wait_ge(sig(f"at_s{p}"), past(f"at_s{p}") + 12 * i + use + 1)
                        nc.vector.tensor_reduce(st[:, x:x + 1], pairbank(p, T), AX.X, ALU.max).then_inc(sig(f"at_x{p}"), 1)
                    for x, (p, use) in [(x, pairs[x]) for x in xs if x < len(pairs)]:
                        dve.wait_ge(sig(f"at_x{p}"), past(f"at_x{p}") + 12 * i + use + 1)
                        nc.vector.tensor_scalar(st[:, x:x + 1], st[:, x:x + 1], -(64 if da else 192) ** -0.5, None, ALU.mult)\
                            .then_inc(sig(f"at_m{p}"), 1)

                def weights(between, u, da, hh, qt, pairs):
                    st, n = stat[u % 2], len(pairs)
                    for p, use in pairs:
                        dve.wait_ge(sig(f"at_e{p}"), 12 * i + use + 2)
                    nc.vector.reciprocal(st[:, 4:4 + n], st[:, 2:2 + n]).then_inc(sig("at_r"), 1)
                    dve.wait_ge(sig("at_r"), past("at_r") + 16 * i + u + 1)
                    p0, p1 = prb[2 * (u % 2)], prb[2 * (u % 2) + 1]
                    ins = nc.vector.tensor_scalar(p0[:, :], p0[:, :], st[:, 4:5], None, ALU.mult)
                    if not da:
                        ins.then_inc(sig("at_p"), 1)
                        between()
                        return
                    ins.then_inc(sig("at_w"), 1)
                    nc.vector.tensor_scalar(st[:, 5:6], st[:, 5:6], lam[:, 5:6], None, ALU.mult).then_inc(sig("at_w"), 1)
                    between()
                    dve.wait_ge(sig("at_w"), past("at_w") + 16 * i + 2 * (4 * hh + qt) + 2)
                    nc.vector.scalar_tensor_tensor(p0[:, :], p1[:, :], st[:, 5:6], p0[:, :], ALU.mult, ALU.add).then_inc(sig("at_p"), 1)
                maxima((0, 1), *U[0])
                for x in U[:-1]:
                    weights(lambda: maxima((0,), *U[x[0] + 1]), *x)
                    maxima((1,), *U[x[0] + 1])
                weights(lambda: None, *U[-1])

        def vector_program(dve):
            dve.sem_inc(sig("gemm_evac0"), 1)
            dve.sem_inc(sig("gemm_evac1"), 1)
            dve.sem_inc(sig("conv_step"), 8)
            dve.wait_ge(sig("rows_turned"), 1)
            nc.vector.tensor_copy(vec[:, :], ps[:, 7, :]).then_inc(sig("vec_ready"), 1)
            for u in range(0, 12, 2):
                dve.wait_ge(sig("xt_done"), u + 1)
                if u:
                    dve.wait_ge(sig("xt_evac"), u)
                t, hf = u // 2, u % 2
                nc.vector.tensor_copy(xT[:, 0:4, t * P:(t + 1) * P], ps[:, u % 6, :].rearrange("p (k n) -> p k n", k=4))\
                    .then_inc(sig("xt_evac"), 1)
            dve.wait_ge(sig("rows_in"), 16 * len(rows_from()))
            pair = lrow[:, :, :].rearrange("p (x two) n -> p x two n", two=2)
            nc.vector.tensor_tensor(pair[:, :, 0, :], pair[:, :, 0, :], pair[:, :, 1, :], ALU.mult).then_inc(sig("lam_step"), 1)
            dve.wait_ge(sig("lam_step"), 1)
            nc.vector.tensor_reduce(lam[:, 0:2], pair[:, :, 0, :], AX.X, ALU.add).then_inc(sig("lam_step"), 1)
            dve.wait_ge(sig("silu_c"), 1)
            for it in range(3):
                for q in (1, 2):
                    dve_ada(dve, q, it, base=32 * it + 16 * (q - 1))
                dve_mod(dve, it)
            phase_end(dve, "dve")
            phase_begin(dve, 1)
            dve_norm(dve, 0, T, 0, 0, V_NMIX)
            phase_end(dve, "dve")
            phase_begin(dve, 2)
            dve_gates(dve)
            dve.wait_ge(sig("edges"), 6)
            with dve.Fori(0, ADA_IN0) as i:
                dve_conv(dve, i)
                dve_mod(dve, i + 3)
            with dve.Fori(ADA_IN0, 9) as i:
                dve_conv(dve, i, modulate=False)
            phase_end(dve, "dve")
            phase_begin(dve, 3)
            dve.wait_ge(sig("cum_sums"), 1)
            link = Link(dve, "cum_ready")

            def sums(b):
                return ps[:, b, 0:NT * 48].rearrange("p (c n) -> p c n", n=48)
            for b, c0, c1 in ((0, 0, 8), (0, 16, 32), (1, 8, 16), (1, 32, 48)):
                link(nc.vector.tensor_copy(gcol[:, 2, :, c0:c1], sums(b)[:, :, c0:c1]))
            link(nc.vector.tensor_tensor(gcol[:, 3, :, :], sums(2), gcol[:, 2, :, :], ALU.subtract))
            link(nc.vector.tensor_copy(gcol[:, 4, :, :], sums(2)))
            for base, part in ((3, dve_deltanet), (5, dve_ssd)):
                with dve.Fori(0, 2) as g:
                    phase_begin(dve, base + g)
                    part(dve, g)
                    phase_end(dve, "dve")
            phase_begin(dve, 7)
            dve_out(dve, "out0", 0, T)
            phase_end(dve, "dve")
            phase_begin(dve, 8)
            dve_norm(dve, 1, T, 0, 3, V_NFFN)
            phase_end(dve, "dve")
            phase_begin(dve, 9)
            dve_ffn(dve, 0, T)
            phase_end(dve, "dve")
            phase_begin(dve, 10)
            dve_norm(dve, 2, T, 1, 0, V_NMIX + 8)
            phase_end(dve, "dve")
            phase_begin(dve, 11)
            for it in range(ADA_IN0 + 3, 16):
                for q in range(3):
                    dve_ada(dve, q, it, ada1, aacc1)
                dve_mod(dve, it)
            phase_end(dve, "dve")
            phase_begin(dve, 12)
            dve.wait_ge(sig("la_root"), 2)
            nc.vector.reciprocal(latn[:, 0, 0:LAT], latn[:, 0, 0:LAT]).then_inc(sig("la_rec"), 1)
            nc.vector.reciprocal(latn[:, 1, :], latn[:, 1, :]).then_inc(sig("la_rec"), 1)
            dve.wait_ge(sig("la_rec"), 2)
            for k in range(6):
                w, x = (LAT, 0) if k < 4 else (T, 1)
                nc.vector.scalar_tensor_tensor(latr[:, k, 0:w], latr[:, k, 0:w], vec[:, V_QA + k:V_QA + k + 1], latn[:, x, 0:w],
                                               ALU.mult, ALU.mult).then_inc(sig("la_n"), 1)
            for k in range(6):
                w = LAT if k < 4 else T
                dve.wait_ge(sig("la_hi"), k + 1)
                nc.vector.tensor_tensor(Hl[:, k, 0:w], latr[:, k, 0:w], Hh[:, k, 0:w].bitcast(f32), ALU.subtract).then_inc(sig("la_lo"), 1)
            phase_end(dve, "dve")
            phase_begin(dve, 13)
            dve_units(dve)
            phase_end(dve, "dve")
            phase_begin(dve, 14)
            dve_attention(dve)
            phase_end(dve, "dve")
            phase_begin(dve, 15)
            for k in range(8):
                dve.wait_ge(sig("an_root"), past("an_root") + k + 1)
                nc.vector.reciprocal(ars[k % 2][:, :], ars[k % 2][:, :]).then_inc(sig("an_rec"), 1)
                dve.wait_ge(sig("an_rec"), past("an_rec") + k + 1)
                nc.vector.scalar_tensor_tensor(att[:, k, :], att[:, k, :], lam[:, 6:7], ars[k % 2][:, :], ALU.mult, ALU.mult)\
                    .then_inc(sig("an_n"), 1)
            dve_out(dve, "out1", 1, LAT)
            phase_end(dve, "dve")
            phase_begin(dve, 16)
            dve_norm(dve, 3, LAT, 1, 3, V_NFFN + 8)
            phase_end(dve, "dve")
            phase_begin(dve, 17)
            dve_ffn(dve, 1, LAT)
            phase_end(dve, "dve")
            phase_begin(dve, 18)
            for u in range(0, 8, 2):
                dve.wait_ge(sig("yt_done"), u + 1)
                nc.vector.tensor_copy(Y[:, u // 2, 0:512], ps[:, u, :]).then_inc(sig("y_even"), 1)

        def sp_stage(sp, name, src, k=KD, w=256, view=None):
            n0, ns, _, c0 = S[name]
            with sp.Fori(0, ns // 2) as i:
                for jj in range(2):
                    load_slab(sp, n0 + jj, i, src(i, jj), k, w, view)

        def rows_of(w, k):
            return w.rearrange("(k p) n -> p k n", p=P)

        def sp_ffn(sp, layer):
            w1 = a["ffn_w_in"][layer].rearrange("(k p) (u n) -> p k u n", p=P, u=2)
            w2 = a["ffn_w_out"][layer].rearrange("(k p) n -> p k n", p=P)
            for grp, n in enumerate(GROUPS):
                c0 = sum(GROUPS[:grp])
                sp_stage(sp, f"fi{layer}{grp}", lambda i, jj: w1[:, :, :, ds(256 * i + P * (c0 + jj), P)],
                         view=lambda t: t[:, 0:2048].rearrange("p (k u n) -> p k u n", k=KD, u=2))
                sp_stage(sp, f"fo{layer}{grp}", lambda i, jj: w2[:, c0:c0 + n, ds(512 * i + 256 * jj, 256)], k=n)

        def sync_program(sp):
            for e in (0, 1):
                sp.sem_inc(sig(f"store{e}"), 32)
                sp.sem_inc(sig(f"lstore{e}"), 16)
            sp.sem_inc(sig("silu_done"), 2)
            sp.sem_inc(sig("at_tr"), 2)
            sp.sem_inc(sig("at_pv"), 3)
            sp.sem_inc(sig("mix_out"), 16)
            sp.dma_start(cst[:, :], a["consts"]).then_inc(sig("consts_in"), 16)
            sp.wait_ge(sig("rows_clear"), 1)
            for dst, src in rows_from()[1::2]:
                sp.dma_start(dst, src).then_inc(sig("rows_in"), 16)
            sp.dma_start(X[:, 0:4, :], a["x"][0].rearrange("(t p) n -> p t n", p=P)).then_inc(sig("x_in"), 16)
            sp.dma_start(X[:, 4:6, :], a["ctx"][0].rearrange("(t p) n -> p t n", p=P)).then_inc(sig("x_in"), 16)
            adaw = [rows_of(a["ada_w"][layer], KD) for layer in range(2)]
            w0 = rows_of(a["ev_w_in"][0], KD)
            for it in range(3):
                for q in range(3):
                    if it:
                        sp.wait_ge(sig("ada_sum"), 3 * it + q - 2)
                    n = 3 * it + q
                    sp.dma_start(ada[q][:, :, :], adaw[0][:, :, n * 256:(n + 1) * 256]).then_inc(sig(f"ada_in{q}"), 16)
            load_slab(sp, 0, 0, w0[:, :, EV_MAIN:EV_IN], KD, 64)
            load_slab(sp, 1, 0, w0[:, :, 0:256])
            sp.wait_ge(sig("ada_sum"), 9)
            n0 = S["in0"][0]
            for q in range(3):
                sp.dma_start(ada[q][:, :, :], adaw[0][:, :, (9 + q) * 256:(10 + q) * 256]).then_inc(sig(f"ada_in{q}"), 16)
            load_slab(sp, 2, 0, w0[:, :, 256:512])
            for lo, n_it, layer in ((1, 5, 0), (5, ADA_IN0, 1), (ADA_IN0, 13, None)):
                with sp.Fori(lo, n_it) as i:
                    for jj in range(2):
                        load_slab(sp, n0 + jj, i, w0[:, :, ds(512 * i + 256 * jj, 256)])
                        for q in ((0, 1), (2,))[jj] if layer is not None else ():
                            sp.wait_ge(sig("ada_used"), 3 * i + 9 + q - 2)
                            sp.dma_start(ada[q][:, :, :], adaw[layer][:, :, ds(768 * i + (2304 if layer == 0 else 2304 - 6144) + 256 * q, 256)])\
                                .then_inc(sig(f"ada_in{q}"), 16)
            wo0 = rows_of(a["ev_w_out"][0], 16)
            for jj in range(2):
                load_slab(sp, S["out0"][0] + jj, 0, wo0[:, :, jj * P:(jj + 1) * P], 16, P)
            with sp.Fori(0, 2) as g:
                phase_begin(sp, 3 + g)
                for e in (0, 1):
                    sp.wait_ge(sig(f"store{e}"), 32 * 27)
                sp.wait_ge(sig("mix_out"), 16 * g + 16)
                for t, off, name in ((dq, 0, "ld_dq"), (dk, 8, "ld_dk"), (dv, 16, "ld_dv")):
                    sp.dma_start(t[:, :, :], scr_p[:, ds(4 * g + off, 4), :]).then_inc(sig(name), 16)
                sp.wait_ge(sig("rec_qs"), 10 * g + 10)
                sp.dma_start(dq[:, :, :], scr_p[:, ds(4 * g + 36, 4), :]).then_inc(sig("ld_dz"), 16)
                sp.wait_ge(sig("dn_og"), 6 * g + 6)
                sp.dma_start(mix_p[:, ds(4 * g, 4), :], dq[:, :, :]).then_inc(sig("mix_out"), 16)
            phase_begin(sp, 5)
            sp.wait_ge(sig("mix_out"), 48)
            for j in range(4):
                sp.dma_start(mst[j][:, :], mix_p[:, j, :]).then_inc(sig(f"mix_in{j}"), 16)
            with sp.Fori(0, 2) as g:
                phase_begin(sp, 5 + g)
                sp.wait_ge(sig("mix_out"), 16 * g + 48)
                sp.dma_start(sx[:, :, :], scr_p[:, ds(4 * g + 24, 4), :]).then_inc(sig("sd_in"), 16)
                sp.dma_start(sB[:, :], scr_p[:, ds(g + 32, 1), :].rearrange("p a t -> p (a t)")).then_inc(sig("sd_in"), 16)
                sp.dma_start(sC[:, :], scr_p[:, ds(g + 34, 1), :].rearrange("p a t -> p (a t)")).then_inc(sig("sd_in"), 16)
                sp.dma_start(sz[:, :, :], scr_p[:, ds(4 * g + 44, 4), :]).then_inc(sig("sd_z"), 16)
                sp.wait_ge(sig("ss_out"), 4 * g + 4)
                sp.dma_start(mix_p[:, ds(4 * g + 8, 4), :], sx[:, :, :]).then_inc(sig("mix_out"), 16)
            phase_begin(sp, 7)
            sp.wait_ge(sig("mix_out"), 80)
            for i in range(1, 4):
                for j in range(4):
                    sp.wait_ge(sig("mix_lo"), 4 * (i - 1) + j + 1)
                    sp.dma_start(mst[j][:, :], mix_p[:, 4 * i + j, :]).then_inc(sig(f"mix_in{j}"), 16)
            with sp.Fori(1, 4) as i:
                for jj in range(2):
                    load_slab(sp, S["out0"][0] + jj, i, wo0[:, :, ds(256 * i + P * jj, P)], 16, P)
            sp_ffn(sp, 0)
            w1 = rows_of(a["od_w_in"][0], KD)

            def modulation(it):
                for q in range(3):
                    if it > ADA_IN0 + 3:
                        sp.wait_ge(sig("ada_used"), 3 * it + q - 2)
                    c = 256 * (3 * it + q) - 6144
                    sp.dma_start(ada1[q][:, :, :], adaw[1][:, :, c:c + 256]).then_inc(sig(f"ada_in{q}"), 16)
            for s in range(15):
                load_slab(sp, S["qk1"][0] + s, 0, w1[:, :, 256 * s:256 * s + 256])
                if s == 2:
                    phase_begin(sp, 11)
                if s in (3, 5, 7, 9, 13):
                    modulation(ADA_IN0 + 3 + (3, 5, 7, 9, 13).index(s))
            n0 = S["lat1"][0]
            load_slab(sp, n0 + 3, 0, w1[:, :, 3840:3904].unsqueeze(2).broadcast_to([P, KD, 2, 64]),
                      view=lambda t: t[:, 0:1024].rearrange("p (k two n) -> p k two n", k=KD, two=2))
            wq = a["mla_w_uq"][0].rearrange("(k p) (h n) -> p k h n", p=P, h=8)
            n0 = S["uq1"][0]
            for s_ in range(4):
                load_slab(sp, n0 + s_, 0, wq[:, :, 2 * s_:2 * s_ + 2, 0:P],
                          view=lambda t: t[:, 0:1024].rearrange("p (k h n) -> p k h n", k=4, h=2), k=4)
            for s_ in range(2):
                load_slab(sp, n0 + 4 + s_, 0, wq[:, :, 4 * s_:4 * s_ + 4, P:192],
                          view=lambda t: t[:, 0:1024].rearrange("p (k h n) -> p k h n", k=4, h=4), k=4)
            wkv = a["mla_w_ukv"][0].rearrange("(k p) (h n) -> p k h n", p=P, h=8)
            for name, c0 in (("uk1", 0), ("uv1", P)):
                for s_ in range(4):
                    load_slab(sp, S[name][0] + s_, 0, wkv[:, :, 2 * s_:2 * s_ + 2, c0:c0 + P],
                              view=lambda t: t[:, 0:512].rearrange("p (k h n) -> p k h n", k=2, h=2), k=2)
            wo1 = rows_of(a["od_w_out"][0], 16)
            for jj in range(2):
                load_slab(sp, S["out1"][0] + jj, 0, wo1[:, :, jj * P:(jj + 1) * P], 16, P)
            phase_begin(sp, 13)
            for e in (0, 1):
                sp.wait_ge(sig(f"lstore{e}"), 16 * 27)
            sp.wait_ge(sig("kr_stored"), 16)
            sp_units(sp)
            phase_begin(sp, 14)
            for j in range(4):
                sp.wait_ge(sig(f"ustore{j}"), 16 * len(UNITS[j::4]))
            sp.dma_start(mkr[0:64, :], scr["chunks"][36, 0:64, :]).then_inc(sig("mkr_in"), 16)
            rows64 = scr["chunks"].rearrange("m p t -> (m p) t")
            with sp.Fori(0, 4) as i:
                for hh in range(2):
                    for da in (True, False):
                        hu = 2 * hh + (0 if da else 1)
                        sp.wait_ge(sig("at_pv"), 4 * i + max(hu - 1, 0) + 1)
                        name = f"at_in{hh}{0 if da else 1}"
                        if da:
                            parts = ((aq, 0, LAT), (ak, 8, T))
                            vx, vt = 0, av
                        else:
                            parts = ((mq, 16, LAT), (mk, 28, T))
                            vx, vt = 1, mv
                        for t_, off, w in parts:
                            sp.dma_start(t_[hh][:, 0:w], scr_p[:, ds(2 * i + hh + off, 1), 0:w].rearrange("p a t -> p (a t)"))\
                                .then_inc(sig(name), 16)
                        if not da:
                            sp.dma_start(mr[hh][0:64, :], rows64[ds(24 * P + 128 * i + 64 * hh, 64), 0:LAT]).then_inc(sig(name), 16)
                        sp.dma_start(vt[hh][:, :].rearrange("p (t n) -> p t n", n=P),
                                     vscr[vx].rearrange("(t p) n -> p t n", p=P)[:, :, ds(256 * i + P * hh, P)]).then_inc(sig(name), 16)
            with sp.Fori(1, 4) as i:
                for jj in range(2):
                    load_slab(sp, S["out1"][0] + jj, i, wo1[:, :, ds(256 * i + P * jj, P)], 16, P)
            sp_ffn(sp, 1)
            sp.wait_ge(sig("y_even"), 4)
            sp.wait_ge(sig("y_odd"), 4)
            sp.dma_start(out[0].rearrange("(t p) n -> p t n", p=P), Y[:, :, :]).then_inc(sig("out_done"), 16)
            sp.wait_ge(sig("out_done"), 16)

        def sp_units(sp):
            for v in range(len(UNITS) + 2):
                if v < len(UNITS):
                    w = UNITS[v][0]
                    if v >= 4:
                        sp.wait_ge(sig(f"ustore{v % 4}"), 16 * (v // 4))
                    sp.dma_start(qn[v % 4][:, 0:w], scr["chunks"][v, :, 0:w]).then_inc(sig(f"un_in{v % 4}"), 16)
                if v >= 2:
                    u = v - 2
                    w = UNITS[u][0]
                    sp.wait_ge(sig("un_done"), u + 1)
                    sp.dma_start(scr["chunks"][u, :, 0:w], qn[u % 4][:, 0:w]).then_inc(sig(f"ustore{u % 4}"), 16)

        block = whole.enter_context(nc.Block())

        @block.sync
        def _(sp):
            sync_program(sp)

        @block.scalar
        def _(act):
            scalar_program(act)

        @block.gpsimd
        def _(pool):
            gpsimd_program(pool)

        @block.vector
        def _(dve):
            vector_program(dve)

        @block.tensor
        def _(pe):
            tensor_program(pe)


INPUTS = ["x", "c", "ctx", "c_ctx", "ada_w", "ada_b", "norm_mix", "norm_ffn", "ffn_w_in", "ffn_w_out",
          "ev_w_in", "ev_conv_w", "ev_conv_b", "dn_a_log", "dn_dt_bias", "dn_norm", "ssd_a_log", "ssd_dt_bias",
          "ssd_d", "ssd_norm", "ev_w_out", "od_w_in", "da_q_norm", "da_k_norm", "da_lambda", "da_sub_norm",
          "mla_q_a_norm", "mla_w_uq", "mla_kv_a_norm", "mla_w_ukv", "mla_q_norm", "mla_k_norm", "od_w_out"]


def kernel(**inputs):
    import concourse.bacc as bacc
    from concourse.bass_utils import run_bass_kernel_spmd

    f32 = mybir.dt.float32
    nc = bacc.Bacc("TRN2", target_bir_lowering=False, num_devices=1)
    arrays, a = {}, {}
    for name in INPUTS:
        arr = np.ascontiguousarray(inputs[name])
        arrays["in_" + name] = arr
        a[name] = nc.dram_tensor("in_" + name, arr.shape, f32, kind="ExternalInput").ap()
    arrays["consts"] = constants()
    a["consts"] = nc.dram_tensor("consts", (P, C_ALL), f32, kind="ExternalInput").ap()
    out = nc.dram_tensor("out", (1, LAT, D), f32, kind="ExternalOutput").ap()
    kw = {}
    scr = {"chunks": nc.dram_tensor("chunks", (52, P, T), f32, **kw).ap(),
           "values": nc.dram_tensor("values", (2, T, D), f32, **kw).ap(),
           "mix": nc.dram_tensor("mix", (16, P, T), f32, **kw).ap()}
    build(nc, a, out, scr)
    r = run_bass_kernel_spmd(nc, [arrays], core_ids=[0])
    return r.results[0]["out"]
```
